# Optimizing a Trainium2 kernel written in Bass

```python
import math
import jax, jax.numpy as jnp
from jax import lax
import numpy as np

D_MODEL = 1024
BATCH = 1
SEQ = 256
DEPTH = 2

GRID_W = 64
CTX_LEN = 256
HEAD_DIM = 64
A_HEADS = 6
A_KV_HEADS = 2
A_GROUP = A_HEADS // A_KV_HEADS
WINDOW = 128
B_HEADS = 4
B_NOPE = 64
B_ROPE = 32
B_V = 64
B_Q_LORA = 256
B_KV_LORA = 128
C_HEADS = 6
C_KV_HEADS = 2
C_GROUP = C_HEADS // C_KV_HEADS
Q_BLOCK = 128
N_EXPERTS = 16
EXPERT_FF = 1024
CAPACITY_FACTOR = 2
N_BRANCHES = 3
ROPE_THETA = 10000.0
LN_EPS = 1e-5
RMS_EPS = 1e-6
ALPHA = (2 * DEPTH) ** 0.25
BETA = (8 * DEPTH) ** -0.25
A_SCALE = HEAD_DIM ** -0.5
B_SCALE = (B_NOPE + B_ROPE) ** -0.5
C_SCALE = HEAD_DIM ** -0.5
A_Q_W = A_HEADS * HEAD_DIM
A_KV_W = A_KV_HEADS * HEAD_DIM
C_Q_W = C_HEADS * HEAD_DIM
C_KV_W = C_KV_HEADS * HEAD_DIM
B_O_W = B_HEADS * B_V
IN_SIZES = (A_Q_W, A_KV_W, A_KV_W, B_Q_LORA, B_KV_LORA, B_ROPE, C_Q_W, C_KV_W, C_KV_W, N_BRANCHES * D_MODEL)
IN_W = sum(IN_SIZES)
BRANCH_W = A_Q_W + B_O_W + C_Q_W

kernel_name = "hybrid_diffusion_prefix_trunk"

def layer_norm(x, g, b):
    xf = x.astype(jnp.float32)
    mu = xf.mean(-1, keepdims=True)
    var = jnp.square(xf - mu).mean(-1, keepdims=True)
    return ((xf - mu) * lax.rsqrt(var + LN_EPS) * g + b).astype(x.dtype)

def rms_norm(x, g):
    xf = x.astype(jnp.float32)
    return (xf * lax.rsqrt(jnp.mean(xf * xf, -1, keepdims=True) + RMS_EPS) * g).astype(x.dtype)

def rope_1d(x, pos):
    half = x.shape[-1] // 2
    freqs = ROPE_THETA ** (-jnp.arange(half, dtype=jnp.float32) / half)
    ang = pos.astype(jnp.float32)[:, None] * freqs
    cos = jnp.cos(ang)[:, None, :]
    sin = jnp.sin(ang)[:, None, :]
    x1, x2 = x[..., :half], x[..., half:]
    return jnp.concatenate([x1 * cos - x2 * sin, x1 * sin + x2 * cos], -1).astype(x.dtype)

def axial_rope(x, row, col):
    a = x.shape[-1] // 2
    return jnp.concatenate([rope_1d(x[..., :a], row), rope_1d(x[..., a:], col)], -1)

def sink_softmax(scores, sink):
    m = jnp.maximum(scores.max(-1, keepdims=True), sink)
    e = jnp.exp(scores - m)
    return e / (e.sum(-1, keepdims=True) + jnp.exp(sink - m))

def windowed_sink_attention(q, k, v, ck, cv, sink):
    b, s, g, r, d = q.shape
    nblk = s // Q_BLOCK
    span = Q_BLOCK + 2 * WINDOW
    kp = jnp.pad(k, ((0, 0), (WINDOW, WINDOW), (0, 0), (0, 0)))
    vp = jnp.pad(v, ((0, 0), (WINDOW, WINDOW), (0, 0), (0, 0)))
    qb = jnp.moveaxis(q.reshape(b, nblk, Q_BLOCK, g, r, d), 1, 0)
    sink_b = sink.astype(jnp.float32).reshape(1, g, r, 1, 1)

    def block(args):
        i, qi = args
        start = i * Q_BLOCK
        ki = lax.dynamic_slice_in_dim(kp, start, span, axis=1)
        vi = lax.dynamic_slice_in_dim(vp, start, span, axis=1)
        qpos = start + jnp.arange(Q_BLOCK)
        kpos = start - WINDOW + jnp.arange(span)
        valid = (kpos[None, :] >= 0) & (kpos[None, :] < s) & (jnp.abs(qpos[:, None] - kpos[None, :]) <= WINDOW)
        s_loc = jnp.einsum('bqgrd,bkgd->bgrqk', qi, ki).astype(jnp.float32) * A_SCALE
        s_loc = jnp.where(valid, s_loc, -jnp.inf)
        s_ctx = jnp.einsum('bqgrd,bkgd->bgrqk', qi, ck).astype(jnp.float32) * A_SCALE
        p = sink_softmax(jnp.concatenate([s_loc, s_ctx], -1), sink_b).astype(v.dtype)
        return (jnp.einsum('bgrqk,bkgd->bqgrd', p[..., :span], vi)
                + jnp.einsum('bgrqk,bkgd->bqgrd', p[..., span:], cv))

    out = lax.map(block, (jnp.arange(nblk), qb))
    return jnp.moveaxis(out, 0, 1).reshape(b, s, g * r * d)

def sink_dense_attention(q, k, v, sink):
    b, n, g, r, d = q.shape
    sc = jnp.einsum('bqgrd,bkgd->bgrqk', q, k).astype(jnp.float32) * A_SCALE
    p = sink_softmax(sc, sink.astype(jnp.float32).reshape(1, g, r, 1, 1)).astype(v.dtype)
    return jnp.einsum('bgrqk,bkgd->bqgrd', p, v).reshape(b, n, g * r * d)

def dense_attention(q, k, v, scale):
    b, n, g, r, dk = q.shape
    nblk = n // Q_BLOCK
    qb = jnp.moveaxis(q.reshape(b, nblk, Q_BLOCK, g, r, dk), 1, 0)

    def block(qi):
        sc = jnp.einsum('bqgrd,bkgd->bgrqk', qi, k).astype(jnp.float32) * scale
        p = jax.nn.softmax(sc, axis=-1).astype(v.dtype)
        return jnp.einsum('bgrqk,bkgd->bqgrd', p, v)

    out = lax.map(block, qb)
    return jnp.moveaxis(out, 0, 1).reshape(b, n, g * r * v.shape[-1])

def project_heads(h, w_in, b_q_norm, b_kv_norm, b_w_uq, b_w_ukv, c_q_norm, c_k_norm, row, col):
    offs = [int(o) for o in np.cumsum(IN_SIZES)[:-1]]
    a_q, a_k, a_v, b_cq, b_ckv, b_kr, c_q, c_k, c_v, gate_logits = jnp.split(h @ w_in, offs, axis=-1)
    bsz, n, _ = h.shape
    heads = lambda t, nh: t.reshape(bsz, n, nh, HEAD_DIM)
    rot = (lambda t: axial_rope(t, row, col)) if row is not None else (lambda t: t)
    qa = rot(heads(a_q, A_HEADS)).reshape(bsz, n, A_KV_HEADS, A_GROUP, HEAD_DIM)
    ka = rot(heads(a_k, A_KV_HEADS))
    va = heads(a_v, A_KV_HEADS)
    qb = (rms_norm(b_cq, b_q_norm) @ b_w_uq).reshape(bsz, n, B_HEADS, B_NOPE + B_ROPE)
    qb = jnp.concatenate([qb[..., :B_NOPE], rot(qb[..., B_NOPE:])], -1)[:, :, :, None, :]
    kvb = (rms_norm(b_ckv, b_kv_norm) @ b_w_ukv).reshape(bsz, n, B_HEADS, B_NOPE + B_V)
    kr = jnp.broadcast_to(rot(b_kr[:, :, None, :]), (bsz, n, B_HEADS, B_ROPE))
    kb = jnp.concatenate([kvb[..., :B_NOPE], kr], -1)
    vb = kvb[..., B_NOPE:]
    qc = rot(rms_norm(heads(c_q, C_HEADS), c_q_norm)).reshape(bsz, n, C_KV_HEADS, C_GROUP, HEAD_DIM)
    kc = rot(rms_norm(heads(c_k, C_KV_HEADS), c_k_norm))
    vc = heads(c_v, C_KV_HEADS)
    return (qa, ka, va, qb, kb, vb, qc, kc, vc, gate_logits)

def merge_branches(o_a, o_b, o_c, gate_logits, w_branch, w_out):
    g_a, g_b, g_c = jnp.split(jax.nn.sigmoid(gate_logits), N_BRANCHES, axis=-1)
    p_a = o_a @ w_branch[:A_Q_W]
    p_b = o_b @ w_branch[A_Q_W:A_Q_W + B_O_W]
    p_c = o_c @ w_branch[A_Q_W + B_O_W:]
    return (g_a * p_a + g_b * p_b + g_c * p_c) @ w_out

def mix_latent(lat, cts, a_sink, w_branch, w_out):
    qa, ka, va, qb, kb, vb, qc, kc, vc, gl = lat
    _, cka, cva, _, ckb, cvb, _, ckc, cvc, _ = cts
    o_a = windowed_sink_attention(qa, ka, va, cka, cva, a_sink)
    o_b = dense_attention(qb, jnp.concatenate([ckb, kb], 1), jnp.concatenate([cvb, vb], 1), B_SCALE)
    o_c = dense_attention(qc, jnp.concatenate([ckc, kc], 1), jnp.concatenate([cvc, vc], 1), C_SCALE)
    return merge_branches(o_a, o_b, o_c, gl, w_branch, w_out)

def mix_context(cts, a_sink, w_branch, w_out):
    qa, ka, va, qb, kb, vb, qc, kc, vc, gl = cts
    o_a = sink_dense_attention(qa, ka, va, a_sink)
    o_b = dense_attention(qb, kb, vb, B_SCALE)
    o_c = dense_attention(qc, kc, vc, C_SCALE)
    return merge_branches(o_a, o_b, o_c, gl, w_branch, w_out)

def expert_choice_ffn(h, w_router, w_gate, w_up, w_down):
    b, n, d = h.shape
    cap = CAPACITY_FACTOR * n // N_EXPERTS
    aff = jax.nn.softmax((h @ w_router).astype(jnp.float32), axis=-1)
    top_aff, top_idx = lax.top_k(jnp.swapaxes(aff, 1, 2), cap)
    flat = top_idx.reshape(b, N_EXPERTS * cap)
    bidx = jnp.arange(b)[:, None]
    xs = h[bidx, flat].reshape(b, N_EXPERTS, cap, d)
    hid = jax.nn.silu(jnp.einsum('becd,edf->becf', xs, w_gate)) * jnp.einsum('becd,edf->becf', xs, w_up)
    ys = jnp.einsum('becf,efd->becd', hid, w_down) * top_aff[..., None].astype(h.dtype)
    return jnp.zeros_like(h).at[bidx, flat].add(ys.reshape(b, N_EXPERTS * cap, d))

def setup_inputs(seed: int = 0) -> dict:
    key = jax.random.key(seed)
    ks = jax.random.split(key, 24)
    nrm = lambda k, shape, scale: jax.random.normal(k, shape, jnp.float32) * scale
    gain = lambda k, shape: 1.0 + 0.02 * jax.random.normal(k, shape, jnp.float32)
    L = DEPTH
    return {
        "x": nrm(ks[0], (BATCH, SEQ, D_MODEL), 1.0),
        "c": nrm(ks[1], (BATCH, D_MODEL), 1.0),
        "ctx": nrm(ks[2], (BATCH, CTX_LEN, D_MODEL), 1.0),
        "c_ctx": nrm(ks[3], (D_MODEL,), 1.0),
        "w_ada": nrm(ks[4], (L, D_MODEL, 6 * D_MODEL), 0.5 * D_MODEL ** -0.5),
        "b_ada": nrm(ks[5], (L, 6 * D_MODEL), 0.01),
        "w_in": nrm(ks[6], (L, D_MODEL, IN_W), D_MODEL ** -0.5),
        "a_sink": nrm(ks[7], (L, A_HEADS), 0.5),
        "b_q_norm": gain(ks[8], (L, B_Q_LORA)),
        "b_kv_norm": gain(ks[9], (L, B_KV_LORA)),
        "b_w_uq": nrm(ks[10], (L, B_Q_LORA, B_HEADS * (B_NOPE + B_ROPE)), B_Q_LORA ** -0.5),
        "b_w_ukv": nrm(ks[11], (L, B_KV_LORA, B_HEADS * (B_NOPE + B_V)), B_KV_LORA ** -0.5),
        "c_q_norm": gain(ks[12], (L, HEAD_DIM)),
        "c_k_norm": gain(ks[13], (L, HEAD_DIM)),
        "w_branch": nrm(ks[14], (L, BRANCH_W, D_MODEL), A_Q_W ** -0.5),
        "w_out": nrm(ks[15], (L, D_MODEL, D_MODEL), BETA * D_MODEL ** -0.5),
        "ln1_g": gain(ks[16], (L, D_MODEL)),
        "ln1_b": nrm(ks[17], (L, D_MODEL), 0.01),
        "w_router": nrm(ks[18], (L, D_MODEL, N_EXPERTS), D_MODEL ** -0.5),
        "w_gate": nrm(ks[19], (L, N_EXPERTS, D_MODEL, EXPERT_FF), D_MODEL ** -0.5),
        "w_up": nrm(ks[20], (L, N_EXPERTS, D_MODEL, EXPERT_FF), D_MODEL ** -0.5),
        "w_down": nrm(ks[21], (L, N_EXPERTS, EXPERT_FF, D_MODEL), BETA * EXPERT_FF ** -0.5),
        "ln2_g": gain(ks[22], (L, D_MODEL)),
        "ln2_b": nrm(ks[23], (L, D_MODEL), 0.01),
    }

def reference(x, c, ctx, c_ctx, w_ada, b_ada, w_in, a_sink, b_q_norm, b_kv_norm, b_w_uq, b_w_ukv,
              c_q_norm, c_k_norm, w_branch, w_out, ln1_g, ln1_b, w_router, w_gate, w_up, w_down,
              ln2_g, ln2_b):
    n = x.shape[1]
    rows = n // GRID_W
    row = jnp.repeat(jnp.arange(rows), GRID_W)
    col = jnp.tile(jnp.arange(GRID_W), rows)
    cx = ctx
    for l in range(DEPTH):
        last = l == DEPTH - 1
        mod = (jax.nn.silu(c) @ w_ada[l] + b_ada[l])[:, None, :]
        mod_c = (jax.nn.silu(c_ctx) @ w_ada[l] + b_ada[l])[None, None, :]
        sh1, sc1, g1, sh2, sc2, g2 = jnp.split(mod, 6, axis=-1)
        sh1c, sc1c, g1c, sh2c, sc2c, g2c = jnp.split(mod_c, 6, axis=-1)
        h = x * (1.0 + sc1) + sh1
        hc = cx * (1.0 + sc1c) + sh1c
        lat = project_heads(h, w_in[l], b_q_norm[l], b_kv_norm[l], b_w_uq[l], b_w_ukv[l],
                            c_q_norm[l], c_k_norm[l], row, col)
        cts = project_heads(hc, w_in[l], b_q_norm[l], b_kv_norm[l], b_w_uq[l], b_w_ukv[l],
                            c_q_norm[l], c_k_norm[l], None, None)
        y = mix_latent(lat, cts, a_sink[l], w_branch[l], w_out[l])
        x = layer_norm(ALPHA * x + g1 * y, ln1_g[l], ln1_b[l])
        if not last:
            yc = mix_context(cts, a_sink[l], w_branch[l], w_out[l])
            cx = layer_norm(ALPHA * cx + g1c * yc, ln1_g[l], ln1_b[l])
        h = x * (1.0 + sc2) + sh2
        y = expert_choice_ffn(h, w_router[l], w_gate[l], w_up[l], w_down[l])
        x = layer_norm(ALPHA * x + g2 * y, ln2_g[l], ln2_b[l])
        if not last:
            hc = cx * (1.0 + sc2c) + sh2c
            yc = expert_choice_ffn(hc, w_router[l], w_gate[l], w_up[l], w_down[l])
            cx = layer_norm(ALPHA * cx + g2c * yc, ln2_g[l], ln2_b[l])
    return x


_drawn_inputs = setup_inputs


def setup_inputs(seed=0):
    import zlib

    import numpy as np

    out = dict(_drawn_inputs(seed))
    spreads = {}
    factors = {'ctx': 6.727,
     'c_ctx': 2.87,
     'b_ada': 8.0,
     'a_sink': 64.0,
     'b_q_norm': 8.0,
     'b_kv_norm': 8.0,
     'b_w_uq': 8.0,
     'b_w_ukv': 3.611,
     'c_q_norm': 8.0,
     'c_k_norm': 8.0,
     'ln1_b': 3.912,
     'ln2_b': 4.062}
    for name, (base, spread) in spreads.items():
        noise = np.random.default_rng([zlib.crc32(name.encode()), seed]).standard_normal(out[name].shape)
        drawn = base * np.exp(spread * noise) if base else spread * noise
        out[name] = __import__('jax').numpy.asarray(drawn.astype(out[name].dtype))
    for name, factor in factors.items():
        out[name] = (out[name] * factor).astype(out[name].dtype)
    return out
```

```python
import concourse.bass as bass
from concourse import mybir
from contextlib import ExitStack

F32 = mybir.dt.float32
ALU = mybir.AluOpType
ACT = mybir.ActivationFunctionType
AX = mybir.AxisListType.X

P = 128
D = 1024
KT = D // P
DEPTH = 2
HD = 64
HEADS_A, HEADS_B = 6, 4
QK_B, ROPE_B = 96, 32
EXPERTS, CAP = 16, 32
ALPHA = (2 * DEPTH) ** 0.25
SCALE_AC, SCALE_B = HD ** -0.5, QK_B ** -0.5
LN_EPS, RMS_EPS = 1e-5, 1e-6
RING, SLOT = 8, 2048
ADA_BANK, TURN_BANK = 7, 6
GATE_COL = 1696
CHUNKS = {0: [(0, 512)], 1: [(512, 512)], 2: [(1056, 512)], 3: [(1024, 32), (1568, 128)]}
BRANCH_TILES = [(0, 3), (3, 5), (5, 8)]
SH1, SC1, G1, SH2, SC2, G2 = range(6)
C_ID, C_MASK, C_ROPE, C_IOTA, C_ALL = 0, 128, 640, 1024, 1056

QKV_STEPS = [("P", 1, 0), ("P", 1, 1), ("N", 0), ("P", 1, 2), ("N", 1), ("P", 1, 3), ("N", 2), ("P", 3, 0), ("N", 3),
             ("P", 3, 1), ("U", 0), ("P", 3, 2), ("U", 1), ("TB", 0), ("P", 3, 3), ("U", 2), ("TB", 1), ("P", 0, 0),
             ("U", 3), ("TB", 2), ("P", 0, 1), ("TB", 3), ("TA", 0), ("P", 0, 2), ("TA", 1), ("P", 0, 3), ("TA", 2),
             ("P", 2, 0), ("TA", 3), ("P", 2, 1), ("TC", 0), ("P", 2, 2), ("TC", 1), ("P", 2, 3), ("TC", 2),
             ("TC", 3)]
PAIRS = [("A", 0), ("A", 2), ("A", 4), ("B", 0), ("B", 2), ("C", 0), ("C", 2), ("C", 4)]


def trunk(nc, x, c, ctx_in, c_ctx, w_ada, b_ada, w_in, a_sink, b_q_norm, b_kv_norm, b_w_uq, b_w_ukv, c_q_norm,
          c_k_norm, w_branch, w_out, ln1_g, ln1_b, w_router, w_gate, w_up, w_down, ln2_g, ln2_b, consts, out):
    es = ExitStack()
    with es:
        def sb(name, shape):
            return es.enter_context(nc.sbuf_tensor(name, shape, F32))

        def sem(name):
            return es.enter_context(nc.semaphore(name))

        ring = sb("ring", [P, RING, SLOT])
        X = sb("X", [P, 4, D])
        hT = sb("hT", [P, KT, 512])
        A = sb("A", [P, 13312])
        B = sb("B", [P, 4096])
        PR = sb("PR", [P, 4096])
        W = sb("W", [P, 4096])
        cst = sb("cst", [P, C_ALL])
        cs = sb("cs", [P, KT, 32])
        cin = sb("cin", [2 * KT, P])
        modrow = sb("modrow", [P, 512])
        modsb = sb("modsb", [32, P])
        modb = sb("modb", [32, P])
        modcol = sb("modcol", [P, DEPTH, 2, 48])
        wr = sb("wr", [P, KT, EXPERTS])
        sink = sb("sink", [P, HEADS_A])
        nsink = sb("nsink", [P, HEADS_A])
        eps = sb("eps", [P, 2])
        krr = sb("krr", [P, 4, ROPE_B])
        small = sb("small", [P, 64])
        stats = sb("stats", [P, 2, 6])
        affn = sb("affn", [P, 2, 32])
        posn = sb("posn", [P, 2, 32])
        max8 = sb("max8", [32, 8])
        psum = es.enter_context(nc.psum_tensor("psum", [P, 8, 512], F32))
        mod_raw = nc.dram_tensor("mod_raw", (DEPTH, 2, 48, P), F32).ap()
        mod_all = nc.dram_tensor("mod_all", (DEPTH, 2, 48, P), F32).ap()

        def part(t, at, *shape):
            n = 1
            for s in shape:
                n *= s
            v = t[:, at:at + n]
            if len(shape) == 2:
                v = v.rearrange("p (a b) -> p a b", b=shape[1])
            if len(shape) == 3:
                v = v.rearrange("p (a b c) -> p a b c", b=shape[1], c=shape[2])
            return v

        ident = cst[:, C_ID:C_ID + P]
        iota1 = cst[:, C_IOTA:C_IOTA + CAP]
        qT = {"A": part(A, 0, 6, 512), "C": part(A, 3072, 6, 512), "B": part(A, 6144, 4, 512)}
        kT = {"A": part(A, 8192, 512), "C": part(A, 8704, 512), "B": part(A, 9216, 4, 512)}
        V = {"A": part(A, 11264, 4, P), "C": part(A, 11776, 4, P), "B": part(A, 12288, 4, 256)}
        merged = part(A, 0, 4, D)
        mT = part(A, 4096, KT, 512)
        xsT = part(A, 0, KT, 1024)
        sil = part(A, 8192, 2, 512)
        hid = part(A, 9216, 2, 512)
        hidT = part(A, 10240, 2, 512)
        ysb = part(A, 11264, 2, 512)
        onehot = part(A, 9216, 4, 512)
        qpad = part(B, 0, 2, 768)
        knat = part(B, 1536, 2, P)
        cqn = part(B, 1792, 2, 384)
        qbn = part(B, 2560, 2, 384)
        kbn = part(B, 3328, 2, 384)
        oT = part(B, 0, KT, 512)
        YG = part(B, 0, 4, D)
        uq = part(PR, 0, 2, 384)
        ukv = part(PR, 768, 512)
        gain_cq = part(PR, 1280, 384)
        gain_q = part(PR, 1664, HD)
        gain_k = part(PR, 1728, HD)
        norm_g, norm_b = part(PR, 0, D), part(PR, D, D)
        gate_of = {0: part(PR, 2048, D), 1: part(PR, 3072, D)}
        m1, m2, sq, xg = (part(W, 512 * i, 512) for i in range(4))
        cqT = part(W, 2048, 3, 512)
        prob = part(W, 0, 2, 512)
        pT = part(W, 1024, 3, 1024)
        sg = part(W, 0, 2, 512)
        gtmp = part(W, 1024, 512)
        ln_t = part(W, 0, 2, D)
        yg_t = part(W, 2048, 512)
        ones = part(W, 2560, 256)
        topT = part(W, 3072, 4, 256)
        ohw = part(hT[:, :, :].rearrange("p a b -> p (a b)"), 0, 4, 512)
        ohT = part(hT[:, :, :].rearrange("p a b -> p (a b)"), 2048, 8, 256)

        bank_filled = [sem(f"bank_filled{b}") for b in range(8)]
        bank_drained = [sem(f"bank_drained{b}") for b in range(8)]
        slot_filled = [sem(f"slot_filled{s}") for s in range(RING)]
        slot_free = [sem(f"slot_free{s}") for s in range(RING)]
        consts_in = sem("consts_in")
        c_in = sem("c_in")
        zeros_set = sem("zeros_set")
        x_in = sem("x_in")
        proj_par_in = sem("proj_par_in")
        norm_par_in = sem("norm_par_in")
        router_in = sem("router_in")
        sink_in = sem("sink_in")
        modrow_stored = sem("modrow_stored")
        mod_loaded = sem("mod_loaded")
        mod_biased = sem("mod_biased")
        mod_stored = sem("mod_stored")
        mod_cols = sem("mod_cols")
        part_in = sem("part_in")
        parts = [0]
        root_ready = sem("root_ready")
        sumsq_ready = sem("sumsq_ready")
        rms_taken = sem("rms_taken")
        cqn_ready = sem("cqn_ready")
        qkb_ready = sem("qkb_ready")
        qk_ready = sem("qk_ready")
        pads_zero = sem("pads_zero")
        max_ready = sem("max_ready")
        prob_ready = sem("prob_ready")
        gate_used = sem("gate_used")
        merged_ready = sem("merged_ready")
        var_ready = sem("var_ready")
        std_ready = sem("std_ready")
        x_ready = sem("x_ready")
        aff_max = sem("aff_max")
        aff_exp = sem("aff_exp")
        aff_ready = sem("aff_ready")
        pos_ready = sem("pos_ready")
        onehot_ready = sem("onehot_ready")
        hid_ready = sem("hid_ready")
        y_ready = sem("y_ready")
        y_moved = [sem(f"y_moved{i}") for i in (0, 1)]
        y_used = sem("y_used")
        out_stored = sem("out_stored")
        dve_step = sem("dve_step")
        act_step = sem("act_step")
        pool_step = sem("pool_step")
        block = es.enter_context(nc.Block())

        groups = {}
        fills, drains = [0] * 8, [0] * 8
        turn = [0]
        pieces, freed = [], []
        frees = [0] * RING

        def filled(eng, key):
            b, n, _ = groups[key]
            eng.wait_ge(bank_filled[b], n)
            return b

        def drained(eng, key):
            b, _, n = groups[key]
            eng.wait_ge(bank_drained[b], n)

        def second(eng, key):
            b, _, n = groups[key]
            eng.wait_ge(bank_drained[b], n - 1)
            return b

        def streams(l):
            return [0, 1] if l < DEPTH - 1 else [1]

        def tiles(l):
            return [t for s in streams(l) for t in (2 * s, 2 * s + 1)]

        def first_tile(l):
            return sum(len(tiles(i)) for i in range(l))

        def units(l, s):
            return [(4 * j + 2 * h + q, j, h, q) for j in range(8) for h in (0, 1) for q in (0, 1)]

        def unit_base(l, s):
            return 32 * (2 * l + s) if l == 0 else 64

        ADA_LATER = [(0, 1), (0, 2), (1, 0), (1, 1), (1, 2)]

        def ada_events(step):
            due = {}
            if step < 8 * len(ADA_LATER):
                due["products"] = ADA_LATER[step // 8] + (step % 8,)
            for name, lag in (("move", 0), ("bias", 5), ("turn", 7), ("columns", 7)):
                n = step - lag
                if n >= 0 and n % 8 == 7 and n // 8 < len(ADA_LATER):
                    due[name] = ADA_LATER[n // 8]
            return due

        @block.tensor
        def _(pe):
            def begin(key, takers=1, bank=None):
                b = turn[0] % 6 if bank is None else bank
                if bank is None:
                    turn[0] += 1
                if drains[b]:
                    pe.wait_ge(bank_drained[b], drains[b])
                fills[b] += 1
                drains[b] += takers
                groups[key] = (b, fills[b], drains[b])
                return b

            def end(ins, b):
                ins.then_inc(bank_filled[b], 1)
                return (bank_filled[b], fills[b])

            def piece(src, *shape):
                n = len(pieces)
                dst = part(ring[:, n % RING, :], 0, *shape)
                pieces.append((dst, src))
                freed.append(None)
                pe.wait_ge(slot_filled[n % RING], 16 * (n // RING + 1))
                return n, dst

            def free(n, ins=None, event=None):
                if event is None:
                    frees[n % RING] += 1
                    ins.then_inc(slot_free[n % RING], 1)
                    event = (slot_free[n % RING], frees[n % RING])
                freed[n] = event

            def mm(o, a, b, start=True, stop=True):
                return nc.tensor.matmul(o, a, b, start=start, stop=stop, skip_group_check=True)

            def ada_products(l, third, k):
                if k == 0:
                    begin(("ada", l, third), bank=ADA_BANK)
                n, w = piece(w_ada[l, k * P:(k + 1) * P, third * 2048:(third + 1) * 2048], 2048)
                for g in range(4):
                    ins = mm(psum[32 * g:32 * g + 32, ADA_BANK, :], cs[:, k, :], w[:, 512 * g:512 * g + 512],
                             k == 0, k == KT - 1)
                if k == KT - 1:
                    free(n, event=end(ins, ADA_BANK))
                else:
                    free(n, ins)

            def ada_turn(l, third):
                b = begin(("adaT", l, third), bank=TURN_BANK)
                pe.wait_ge(mod_biased, 3 * l + third + 1)
                end(nc.tensor.transpose(psum[:, b, 0:32], modsb[:, :], ident[0:32, 0:32]), b)

            def transposes(key, sources, rows=P, takers=1):
                b = begin(key, takers)
                for i, s in enumerate(sources):
                    ins = nc.tensor.transpose(psum[0:rows, b, i * P:(i + 1) * P], s, ident)
                end(ins, b)

            def x_transposes(name, l, t):
                for j in (0, 1):
                    transposes((name, l, t, j), [X[:, t, k * P:(k + 1) * P] for k in range(4 * j, 4 * j + 4)])

            def qkv(l):
                held = {}
                for step in QKV_STEPS:
                    kind, t = step[0], step[-1]
                    cut = l == DEPTH - 1 and t < 2
                    if kind == "P":
                        ch = step[1]
                        width = sum(w for _, w in CHUNKS[ch])
                        if t == 0:
                            held = [piece([w_in[l, 512 * h:512 * h + 512, a:a + w] for a, w in CHUNKS[ch]], 4, width)
                                    for h in (0, 1)]
                        b = begin(("P", l, ch, t), takers=2 if ch != 0 else 1)
                        lo = 384 if cut and ch in (0, 2) else 0
                        if ch == 1:
                            drained(pe, ("hT", l, t, 0))
                            drained(pe, ("hT", l, t, 1))
                        for k in range(KT):
                            ins = mm(psum[:, b, lo:width], hT[:, k, t * P:(t + 1) * P], held[k // 4][1][:, k % 4, lo:],
                                     k == 0, k == KT - 1)
                        event = end(ins, b)
                        if t == 3:
                            for n, _ in held:
                                free(n, event=event)
                    if kind == "N":
                        pe.wait_ge(cqn_ready, 4 * l + t + 1)
                        transposes(("N", l, t), [cqn[:, t % 2, j * P:(j + 1) * P] for j in range(3)])
                    if kind == "U":
                        drained(pe, ("N", l, t))
                        if t == 0:
                            pe.wait_ge(proj_par_in, 96 * (l + 1))
                        if not cut:
                            b = begin(("UQ", l, t))
                            for j in (0, 1):
                                ins = mm(psum[:, b, 0:384], cqT[:, j, t * P:(t + 1) * P], uq[:, j, :], j == 0, j == 1)
                            end(ins, b)
                        b = begin(("UKV", l, t), takers=2)
                        end(mm(psum[:, b, :], cqT[:, 2, t * P:(t + 1) * P], ukv), b)
                    if kind == "TB":
                        pe.wait_ge(qkb_ready, 4 * l + t + 1)
                        kb = kbn[:, t % 2, :].rearrange("p (h d) -> p h d", h=4)
                        qb = qbn[:, t % 2, :].rearrange("p (h d) -> p h d", h=4)
                        if not cut:
                            transposes(("TBq", l, t), [qb[:, h, :] for h in range(4)], rows=QK_B)
                        transposes(("TBk", l, t), [kb[:, h, :] for h in range(4)], rows=QK_B)
                    if kind in ("TA", "TC"):
                        pe.wait_ge(qk_ready, 8 * l + t + 1 + 4 * (kind == "TC"))
                        q = qpad[:, t % 2, :].rearrange("p (h d) -> p h d", h=6)
                        if not cut:
                            transposes((kind + "q", l, t), [q[:, h, :] for h in range(4)])
                            transposes((kind + "r", l, t), [q[:, h, :] for h in (4, 5)] + [knat[:, t % 2, :]])
                        else:
                            transposes((kind + "r", l, t), [knat[:, t % 2, :]])

            def attention(l, s, step):
                nk = 2 if s == 0 else 4
                us = units(l, s)
                for i in range(len(us) + 4):
                    if i < len(us):
                        u, j, h, q = us[i]
                        br, head = PAIRS[j][0], PAIRS[j][1] + h
                        t = 2 * s + q
                        b = begin(("S", l, s, u))
                        if br == "B":
                            mm_in = qT["B"][0:QK_B, head, t * P:(t + 1) * P], kT["B"][0:QK_B, head, 0:nk * P]
                        else:
                            mm_in = qT[br][:, head, t * P:(t + 1) * P], kT[br][:, 0:nk * P]
                        if i == 0:
                            for tt in range(4):
                                drained(pe, ("TBk", l, tt))
                                drained(pe, ("TAr", l, tt))
                                drained(pe, ("TCr", l, tt))
                                if not (l == DEPTH - 1 and tt < 2):
                                    for name in ("TBq", "TAq", "TCq"):
                                        drained(pe, (name, l, tt))
                        end(mm(psum[:, b, 0:nk * P], *mm_in), b)
                    if l == 0:
                        due = ada_events(step)
                        if "turn" in due:
                            ada_turn(*due["turn"])
                        if "products" in due:
                            ada_products(*due["products"])
                    step += 1
                    if 2 <= i < len(us) + 2:
                        u = us[i - 2][0]
                        pe.wait_ge(prob_ready, unit_base(l, s) + u + 1)
                        transposes(("T", l, s, u), [prob[:, u % 2, k * P:(k + 1) * P] for k in range(nk)])
                    if i >= 4 and us[i - 4][0] % 4 == 3:
                        u, j, _, _ = us[i - 4]
                        for v in range(u - 3, u + 1):
                            drained(pe, ("T", l, s, v))
                        b = begin(("O", l, s, j))
                        br, h0 = PAIRS[j]
                        for k in range(nk):
                            for h in (0, 1):
                                col = HD * (h0 + h if br == "B" else (h0 + h) // 3)
                                p = pT[:, (2 * j + h) % 3, :].rearrange("p (k q) -> p k q", q=256)
                                ins = mm(psum[HD * h:HD * h + HD, b, 0:256], V[br][:, k, col:col + HD], p[:, k, :],
                                         k == 0, k == nk - 1)
                        end(ins, b)
                return step

            def gates(l):
                for n in (0, 1):
                    for br, (lo, hi) in enumerate(BRANCH_TILES):
                        at = GATE_COL + br * D + n * 512
                        wg = [piece([w_in[l, 512 * h:512 * h + 512, at:at + 512]], 4, 512) for h in (0, 1)]
                        wb = piece([w_branch[l, lo * P:hi * P, n * 512:n * 512 + 512]], hi - lo, 512)
                        for t in tiles(l):
                            b = begin(("G", l, n, br, t))
                            for k in range(KT):
                                ins = mm(psum[:, b, :], hT[:, k, t * P:(t + 1) * P], wg[k // 4][1][:, k % 4, :], k == 0,
                                         k == KT - 1)
                            end(ins, b)
                            if n == 0 and br == 0 and t == tiles(l)[0]:
                                for s in streams(l):
                                    for j in range(8):
                                        drained(pe, ("O", l, s, j))
                            b = begin(("BR", l, n, br, t))
                            for k in range(lo, hi):
                                ins = mm(psum[:, b, :], oT[:, k, t * P:(t + 1) * P], wb[1][:, k - lo, :], k == lo,
                                         k == hi - 1)
                            event = end(ins, b)
                        for m, _ in wg + [wb]:
                            free(m, event=event)

            def project(l):
                ts = tiles(l)
                wo = None
                for i in range(len(ts) + 1):
                    if i < len(ts):
                        t = ts[i]
                        pe.wait_ge(merged_ready, first_tile(l) + i + 1)
                        for j in (0, 1):
                            transposes(("M", l, t, j),
                                       [merged[:, t, k * P:(k + 1) * P] for k in range(4 * j, 4 * j + 4)])
                    if i >= 1:
                        t = ts[i - 1]
                        if wo is None:
                            wo = [piece([w_out[l, 512 * h:512 * h + 512, 512 * n:512 * n + 512]], 4, 512)
                                  for n in (0, 1) for h in (0, 1)]
                        drained(pe, ("M", l, t, 0))
                        drained(pe, ("M", l, t, 1))
                        for n in (0, 1):
                            b = begin(("Y", l, t, n))
                            for k in range(KT):
                                ins = mm(psum[:, b, :], mT[:, k, t * P:(t + 1) * P], wo[2 * n + k // 4][1][:, k % 4, :],
                                         k == 0, k == KT - 1)
                            event = end(ins, b)
                for m, _ in wo:
                    free(m, event=event)

            def route(l):
                R = EXPERTS * len(streams(l))
                for i, t in enumerate(tiles(l)):
                    pe.wait_ge(x_ready, 2 * first_tile(l) + i + 1)
                    x_transposes("h2T", l, t)
                for t in tiles(l):
                    drained(pe, ("h2T", l, t, 0))
                    drained(pe, ("h2T", l, t, 1))
                    if t == tiles(l)[0]:
                        pe.wait_ge(router_in, 16 * (l + 1))
                    b = begin(("R", l, t))
                    for k in range(KT):
                        ins = mm(psum[:, b, 0:EXPERTS], hT[:, k, t * P:(t + 1) * P], wr[:, k, :], k == 0, k == KT - 1)
                    end(ins, b)
                pe.wait_ge(aff_ready, l + 1)
                transposes(("AT", l), [affn[:, i, 0:R] for i in (0, 1)], rows=R)
                b = begin(("PT", l))
                pe.wait_ge(pos_ready, l + 1)
                for i in (0, 1):
                    ins = nc.tensor.transpose(psum[:, b, R * i:R * i + R], topT[0:R, 3, i * P:(i + 1) * P],
                                              ident[0:R, 0:R])
                end(ins, b)
                pe.wait_ge(onehot_ready, 2 * first_tile(l) + 2 * len(tiles(l)))
                for k in range(KT):
                    for s in streams(l):
                        b = begin(("XS", l, k, s))
                        for i in (0, 1):
                            ins = mm(psum[:, b, :], X[:, 2 * s + i, k * P:(k + 1) * P], onehot[:, 2 * s + i, :],
                                     i == 0, i == 1)
                        end(ins, b)
                for t in tiles(l):
                    transposes(("OT", l, t), [ohw[:, t, g * P:(g + 1) * P] for g in range(4)])

            def experts(l):
                M = CAP * len(streams(l))
                G = P // M
                Wd = D // G

                def into(e):
                    bg = begin(("HG", l, e))
                    bu = begin(("HU", l, e))
                    if e == 0:
                        for k in range(KT):
                            for s in streams(l):
                                drained(pe, ("XS", l, k, s))
                    for kp in range(4):
                        for b, w in ((bg, w_gate), (bu, w_up)):
                            n, v = piece([w[l, e, kp * 256:kp * 256 + 256, :]], 2, D)
                            for k in (2 * kp, 2 * kp + 1):
                                for g in range(G):
                                    ins = mm(psum[g * M:(g + 1) * M, b, 0:Wd], xsT[:, k, e * M:(e + 1) * M],
                                             v[:, k % 2, g * Wd:(g + 1) * Wd], k == 0, k == KT - 1)
                            if kp == 3:
                                free(n, event=end(ins, b))
                            else:
                                free(n, ins)

                def turn_hidden(e):
                    pe.wait_ge(hid_ready, EXPERTS * l + e + 1)
                    transposes(("HT", l, e), [hid[:, e % 2, j * P:(j + 1) * P] for j in range(Wd // P)])

                def down(e):
                    drained(pe, ("HT", l, e))
                    b = begin(("YE", l, e))
                    for kp in range(4):
                        n, v = piece([w_down[l, e, kp * 256:kp * 256 + 256, :]], 2, D)
                        for k in (2 * kp, 2 * kp + 1):
                            q, j = k // (Wd // P), k % (Wd // P)
                            for g in range(G):
                                ins = mm(psum[g * M:(g + 1) * M, b, 0:Wd],
                                         hidT[:, e % 2, j * P + q * M:j * P + (q + 1) * M],
                                         v[:, k % 2, g * Wd:(g + 1) * Wd], k == 0, k == KT - 1)
                        if kp == 3:
                            free(n, event=end(ins, b))
                        else:
                            free(n, ins)

                def scatter(g):
                    if g == 0:
                        for t in tiles(l):
                            drained(pe, ("OT", l, t))
                    for half in y_moved:
                        pe.wait_ge(half, 64 * 2 * (4 * l + g + 1))
                    for t in tiles(l):
                        s, i = t // 2, t % 2
                        for n in (0, 1):
                            b = begin(("SC", l, g, t, n))
                            end(mm(psum[:, b, :], ohT[:, 4 * s + g, i * P:(i + 1) * P],
                                   YG[:, 2 * (g % 2) + s, 512 * n:512 * n + 512]), b)

                for e in range(EXPERTS + 1):
                    if e < EXPERTS:
                        into(e)
                    if e >= 5 and e % 4 == 1:
                        scatter(e // 4 - 1)
                    if e >= 1:
                        down(e - 1)
                    if e < EXPERTS:
                        turn_hidden(e)
                scatter(3)

            pe.wait_ge(consts_in, 16)
            pe.wait_ge(c_in, 32)
            b = begin("c", bank=ADA_BANK)
            end(nc.tensor.transpose(psum[:, b, 0:2 * KT], cin[:, :], ident[0:2 * KT, 0:2 * KT]), b)
            for k in range(KT):
                ada_products(0, 0, k)
            ada_turn(0, 0)
            step = 0
            for l in range(DEPTH):
                for t in range(4):
                    if l == 0:
                        if t == 0:
                            pe.wait_ge(x_in, 32)
                    else:
                        pe.wait_ge(x_ready, 2 * first_tile(l - 1) + len(tiles(l - 1)) + t + 1)
                    x_transposes("hT", l, t)
                qkv(l)
                for s in streams(l):
                    step = attention(l, s, step)
                gates(l)
                project(l)
                route(l)
                experts(l)

        @block.sync
        def _(sp):
            for n, (dst, src) in enumerate(pieces):
                if n >= RING:
                    sp.wait_ge(*freed[n - RING])
                if not isinstance(src, list):
                    sp.dma_start(dst, src).then_inc(slot_filled[n % RING], 16)
                    continue
                if len(src) == 1:
                    sp.dma_start(dst, src[0].rearrange("(k p) n -> p k n", p=P)).then_inc(slot_filled[n % RING], 16)
                    continue
                at = 0
                for i, s in enumerate(src):
                    w = s.shape[1]
                    ins = sp.dma_start(dst[:, :, at:at + w], s.rearrange("(k p) n -> p k n", p=P))
                    if i == 0:
                        ins.then_inc(part_in, 16)
                        parts[0] += 16
                        sp.wait_ge(part_in, parts[0])
                    else:
                        ins.then_inc(slot_filled[n % RING], 16)
                    at += w
            sp.wait_ge(x_ready, 2 * first_tile(DEPTH))
            sp.dma_start(out.rearrange("b (t p) d -> p (b t) d", p=P), X[:, 2:4, :]).then_inc(out_stored, 16)
            sp.wait_ge(out_stored, 16)

        @block.gpsimd
        def _(pool):
            nc.gpsimd.memset(cs[:, :, :], 0.0).then_inc(zeros_set, 1)
            nc.gpsimd.memset(eps[:, 0:1], LN_EPS).then_inc(zeros_set, 1)
            nc.gpsimd.memset(eps[:, 1:2], RMS_EPS).then_inc(zeros_set, 1)
            pool.dma_start(X[:, 0:2, :], ctx_in.rearrange("b (t p) d -> p (b t) d", p=P)).then_inc(x_in, 16)
            pool.dma_start(X[:, 2:4, :], x.rearrange("b (t p) d -> p (b t) d", p=P)).then_inc(x_in, 16)

            def mod_trip(l, third):
                drained(pool, ("ada", l, third))
                n = 3 * l + third
                for g in range(4):
                    pool.dma_start(mod_raw[l, :, 16 * third + 4 * g:16 * third + 4 * g + 4, :]
                                   .rearrange("s c p -> s (c p)"), modrow[32 * g:32 * g + 2, :]) \
                        .then_inc(modrow_stored, 16)
                pool.wait_ge(modrow_stored, 64 * (n + 1))
                if n:
                    filled(pool, ("adaT", *divmod(n - 1, 3)))
                    pool.wait_ge(mod_stored, 32 * n)
                for s in (0, 1):
                    pool.dma_start(modsb[16 * s:16 * s + 16, :], mod_raw[l, s, 16 * third:16 * third + 16, :]) \
                        .then_inc(mod_loaded, 16)
                    pool.dma_start(modb[16 * s:16 * s + 16, :],
                                   b_ada[l, 2048 * third:2048 * third + 2048].rearrange("(c p) -> c p", p=P)) \
                        .then_inc(mod_loaded, 16)
                pool.wait_ge(mod_biased, n + 1)
                for s in (0, 1):
                    pool.dma_start(mod_all[l, s, 16 * third:16 * third + 16, :], modsb[16 * s:16 * s + 16, :]) \
                        .then_inc(mod_stored, 16)

            def row(ap):
                return ap.rearrange("(a n) -> a n", a=1).partition_broadcast(P)

            def norm_par(l, second):
                g, b = ((ln2_g, ln2_b) if second else (ln1_g, ln1_b))
                pool.dma_start(norm_g, row(g[l, :])).then_inc(norm_par_in, 16)
                pool.dma_start(norm_b, row(b[l, :])).then_inc(norm_par_in, 16)
                ch = G2 if second else G1
                for s in (0, 1):
                    pool.dma_start(gate_of[s], row(mod_all[l, s, 8 * ch:8 * ch + 8, :].rearrange("c p -> (c p)"))) \
                        .then_inc(norm_par_in, 16)

            mod_trip(0, 0)
            for l in range(DEPTH):
                if l:
                    pool.wait_ge(x_ready, 2 * first_tile(l))
                    for t in tiles(l - 1):
                        for n in (0, 1):
                            filled(pool, ("SC", l - 1, 3, t, n))
                pool.dma_start(uq, b_w_uq[l].rearrange("(j p) n -> p j n", p=P)).then_inc(proj_par_in, 16)
                pool.dma_start(ukv, b_w_ukv[l]).then_inc(proj_par_in, 16)
                pool.dma_start(gain_cq[:, 0:256], row(b_q_norm[l, :])).then_inc(proj_par_in, 16)
                pool.dma_start(gain_cq[:, 256:384], row(b_kv_norm[l, :])).then_inc(proj_par_in, 16)
                pool.dma_start(part(PR, 1664, HD), row(c_q_norm[l, :])).then_inc(proj_par_in, 16)
                pool.dma_start(part(PR, 1728, HD), row(c_k_norm[l, :])).then_inc(proj_par_in, 16)
                pool.dma_start(sink[:, :], row(a_sink[l, :])).then_inc(sink_in, 16)
                pool.dma_start(wr[:, :, :], w_router[l].rearrange("(k p) e -> p k e", p=P)).then_inc(router_in, 16)
                nc.gpsimd.memset(qpad[:, :, :], 0.0).then_inc(pads_zero, 1)
                if l == 0:
                    for item in ADA_LATER[:2]:
                        mod_trip(*item)
                pool.wait_ge(qk_ready, 8 * l + 8)
                filled(pool, ("UKV", l, 3))
                pool.wait_ge(mod_stored, 32 * 3)
                if l:
                    pool.wait_ge(mod_stored, 32 * 6)
                norm_par(l, False)
                if l == 0:
                    for item in ADA_LATER[2:]:
                        mod_trip(*item)
                pool.wait_ge(x_ready, 2 * first_tile(l) + len(tiles(l)))
                norm_par(l, True)
                M = CAP * len(streams(l))
                Wd = D * M // P
                for e in range(EXPERTS):
                    g = e // 4
                    if e % 4 == 0 and g >= 2:
                        for t in tiles(l):
                            for n in (0, 1):
                                filled(pool, ("SC", l, g - 2, t, n))
                    pool.wait_ge(y_ready, EXPERTS * l + e + 1)
                    for n in range(P // M):
                        for i, s in enumerate(streams(l)):
                            at = n * M + i * CAP
                            pool.dma_start(YG[CAP * (e % 4):CAP * (e % 4) + CAP, 2 * (g % 2) + s,
                                              n * Wd:(n + 1) * Wd], ysb[at:at + CAP, e % 2, 0:Wd]) \
                                .then_inc(y_moved[e % 2], 16)

        @block.scalar
        def _(act):
            act.dma_start(cin[0:KT, :], c_ctx.rearrange("(k p) -> k p", p=P)).then_inc(c_in, 16)
            act.dma_start(cin[KT:2 * KT, :], c[0, :].rearrange("(k p) -> k p", p=P)).then_inc(c_in, 16)
            act.dma_start(cst[:, :], consts).then_inc(consts_in, 16)
            steps = [0]

            def run(ins):
                steps[0] += 1
                ins.then_inc(act_step, 1)

            def settle():
                act.wait_ge(act_step, steps[0])

            act.wait_ge(zeros_set, 3)
            b = filled(act, "c")
            nc.scalar.activation(cs[:, :, 0:2], psum[:, b, 0:2 * KT].rearrange("p (s k) -> p k s", s=2), ACT.Silu) \
                .then_inc(bank_drained[b], 1)

            def ada_move(l, third):
                b = filled(act, ("ada", l, third))
                if (l, third) != (0, 0):
                    act.wait_ge(modrow_stored, 64 * (3 * l + third))
                nc.scalar.copy(modrow[:, :], psum[:, b, :]).then_inc(bank_drained[b], 1)

            def modulated(name, l, t, scale, shift):
                s = t // 2
                for j in (0, 1):
                    b = filled(act, (name, l, t, j))
                    for i in range(4):
                        k = 4 * j + i
                        ins = nc.scalar.activation(hT[:, k, t * P:(t + 1) * P], psum[:, b, i * P:(i + 1) * P],
                                                   ACT.Identity, scale=modcol[:, l, s, 8 * scale + k:8 * scale + k + 1],
                                                   bias=modcol[:, l, s, 8 * shift + k:8 * shift + k + 1])
                    ins.then_inc(bank_drained[b], 1)

            def qkv(l):
                for step in QKV_STEPS:
                    kind, t = step[0], step[-1]
                    cut = l == DEPTH - 1 and t < 2
                    cols = slice(t * P, (t + 1) * P)
                    n = 8 * l + t
                    if kind == "P" and step[1] == 1:
                        b = filled(act, ("P", l, 1, t))
                        nc.scalar.copy(V["A"][:, t, :], psum[:, b, 0:P])
                        if n:
                            act.wait_ge(rms_taken, n if t else 8 * l)
                        run(nc.scalar.activation(sq[:, 0:256], psum[:, b, 128:384], ACT.Square,
                                                 accum_out=small[:, 0:1]))
                        settle()
                        nc.scalar.activation(sq[:, 0:128], psum[:, b, 384:512], ACT.Square,
                                             accum_out=small[:, 1:2]).then_inc(bank_drained[b], 1)
                        run(nc.scalar.activation(small[:, 2:3], small[:, 0:1], ACT.Sqrt, bias=eps[:, 1:2],
                                                 scale=1.0 / 256))
                        settle()
                        nc.scalar.activation(small[:, 3:4], small[:, 1:2], ACT.Sqrt, bias=eps[:, 1:2],
                                             scale=1.0 / 128).then_inc(root_ready, 1)
                    if kind == "P" and step[1] == 3:
                        b = filled(act, ("P", l, 3, t))
                        nc.scalar.copy(V["C"][:, t, :], psum[:, b, 32:160]).then_inc(bank_drained[b], 1)
                    if kind == "P" and step[1] == 2:
                        b = filled(act, ("P", l, 2, t))
                        lo = 384 if cut else 0
                        act.wait_ge(rms_taken, 8 * l + 4 + t)
                        nc.scalar.activation(sq[:, lo:512], psum[:, b, lo:512], ACT.Square) \
                            .then_inc(bank_drained[b], 1)
                        act.wait_ge(sumsq_ready, 4 * l + t + 1)
                        nc.scalar.activation(small[:, 12 + lo // 64:20], small[:, 4 + lo // 64:12], ACT.Sqrt,
                                             bias=eps[:, 1:2], scale=1.0 / HD).then_inc(root_ready, 1)
                    if kind == "N":
                        b = filled(act, ("N", l, t))
                        nc.scalar.copy(cqT[:, :, cols], psum[:, b, 0:384].rearrange("p (j q) -> p j q", j=3)) \
                            .then_inc(bank_drained[b], 1)
                    if kind == "U":
                        b = filled(act, ("UKV", l, t))
                        nc.scalar.copy(V["B"][:, t, :].rearrange("p (h d) -> p h d", h=4),
                                       psum[:, b, :].rearrange("p (h d) -> p h d", h=4)[:, :, HD:]) \
                            .then_inc(bank_drained[b], 1)
                    if kind == "TB":
                        for name, dst in ((("TBq", qT["B"]),) if not cut else ()) + (("TBk", kT["B"]),):
                            b = filled(act, (name, l, t))
                            nc.scalar.copy(dst[0:QK_B, :, cols], psum[0:QK_B, b, :].rearrange("p (h q) -> p h q", h=4)) \
                                .then_inc(bank_drained[b], 1)
                    if kind in ("TA", "TC"):
                        if not cut:
                            b = filled(act, (kind + "q", l, t))
                            nc.scalar.copy(qT[kind[1]][:, 0:4, cols], psum[:, b, :].rearrange("p (h q) -> p h q", h=4)) \
                                .then_inc(bank_drained[b], 1)
                            b = filled(act, (kind + "r", l, t))
                            nc.scalar.copy(qT[kind[1]][:, 4:6, cols],
                                           psum[:, b, 0:256].rearrange("p (h q) -> p h q", h=2))
                            nc.scalar.copy(kT[kind[1]][:, cols], psum[:, b, 256:384]).then_inc(bank_drained[b], 1)
                        else:
                            b = filled(act, (kind + "r", l, t))
                            nc.scalar.copy(kT[kind[1]][:, cols], psum[:, b, 0:P]).then_inc(bank_drained[b], 1)

            def attention(l, s, step):
                nk = 2 if s == 0 else 4
                us = units(l, s)
                for i in range(len(us) + 4):
                    if i < len(us):
                        u, j, h, q = us[i]
                        br, head = PAIRS[j][0], PAIRS[j][1] + h
                        b = filled(act, ("S", l, s, u))
                        act.wait_ge(max_ready, unit_base(l, s) + u + 1)
                        if u >= 2:
                            filled(act, ("T", l, s, u - 2))
                        c4 = 24 + 4 * (u % 2)
                        if br == "A":
                            nc.scalar.activation(small[:, c4 + 1:c4 + 2], sink[:, head:head + 1], ACT.Exp,
                                                 bias=small[:, c4:c4 + 1])
                        nc.scalar.activation(prob[:, u % 2, 0:nk * P], psum[:, b, 0:nk * P], ACT.Exp,
                                             bias=small[:, c4:c4 + 1], scale=SCALE_B if br == "B" else SCALE_AC,
                                             accum_out=small[:, c4 + 2:c4 + 3]).then_inc(bank_drained[b], 1)
                    if l == 0 and "move" in ada_events(step):
                        ada_move(*ada_events(step)["move"])
                    step += 1
                    if 2 <= i < len(us) + 2:
                        u, j, h, q = us[i - 2]
                        b = filled(act, ("T", l, s, u))
                        hd = 2 * j + h
                        if hd >= 3:
                            filled(act, ("O", l, s, (hd - 3) // 2))
                        p = pT[:, hd % 3, :].rearrange("p (k q) -> p k q", q=256)
                        nc.scalar.copy(p[:, 0:nk, q * P:(q + 1) * P],
                                       psum[:, b, 0:nk * P].rearrange("p (k q) -> p k q", k=nk)) \
                            .then_inc(bank_drained[b], 1)
                    if i >= 4 and us[i - 4][0] % 4 == 3:
                        j = us[i - 4][1]
                        b = filled(act, ("O", l, s, j))
                        nc.scalar.copy(oT[:, j, 256 * s:256 * s + 256], psum[:, b, 0:256]) \
                            .then_inc(bank_drained[b], 1)
                return step

            def norm_roots(l, second):
                for i, t in enumerate(tiles(l)):
                    n = 2 * first_tile(l) + second * len(tiles(l)) + i + 1
                    act.wait_ge(var_ready, n)
                    nc.scalar.activation(small[:, 43:44], small[:, 42:43], ACT.Sqrt, bias=eps[:, 0:1]) \
                        .then_inc(std_ready, 1)

            step = 0
            ada_move(0, 0)
            for l in range(DEPTH):
                n_gates = 6 * first_tile(l)
                for t in range(4):
                    if t == 0:
                        act.wait_ge(mod_cols, 1 if l == 0 else 6)
                    modulated("hT", l, t, SC1, SH1)
                qkv(l)
                for s in streams(l):
                    step = attention(l, s, step)
                for n in (0, 1):
                    for br in range(3):
                        for t in tiles(l):
                            b = filled(act, ("G", l, n, br, t))
                            i = n_gates
                            n_gates += 1
                            if i >= 2:
                                act.wait_ge(gate_used, i - 1)
                            nc.scalar.activation(sg[:, i % 2, :], psum[:, b, :], ACT.Sigmoid) \
                                .then_inc(bank_drained[b], 1)
                ts = tiles(l)
                for i in range(len(ts) + 1):
                    if i < len(ts):
                        for j in (0, 1):
                            b = filled(act, ("M", l, ts[i], j))
                            nc.scalar.copy(mT[:, 4 * j:4 * j + 4, ts[i] * P:(ts[i] + 1) * P],
                                           psum[:, b, :].rearrange("p (k q) -> p k q", k=4)) \
                                .then_inc(bank_drained[b], 1)
                norm_roots(l, 0)
                act.wait_ge(mod_cols, 3 if l == 0 else 6)
                for t in tiles(l):
                    modulated("h2T", l, t, SC2, SH2)
                for i, t in enumerate(tiles(l)):
                    b = filled(act, ("R", l, t))
                    act.wait_ge(aff_max, first_tile(l) + i + 1)
                    nc.scalar.activation(affn[:, t % 2, 16 * (t // 2 - streams(l)[0]):16 * (t // 2 - streams(l)[0]) + 16],
                                         psum[:, b, 0:EXPERTS], ACT.Exp, bias=small[:, 44:45],
                                         accum_out=small[:, 45:46]).then_inc(bank_drained[b], 1)
                M = CAP * len(streams(l))
                for k in range(KT):
                    for i, s in enumerate(streams(l)):
                        b = filled(act, ("XS", l, k, s))
                        dst = xsT[:, k, 0:EXPERTS * M].rearrange("p (e m) -> p e m", m=M)[:, :, CAP * i:CAP * i + CAP]
                        nc.scalar.activation(dst, psum[:, b, :].rearrange("p (e m) -> p e m", m=CAP), ACT.Identity,
                                             scale=modcol[:, l, s, 8 * SC2 + k:8 * SC2 + k + 1],
                                             bias=modcol[:, l, s, 8 * SH2 + k:8 * SH2 + k + 1]) \
                            .then_inc(bank_drained[b], 1)
                for t in tiles(l):
                    b = filled(act, ("OT", l, t))
                    nc.scalar.copy(ohT[:, 4 * (t // 2):4 * (t // 2) + 4, (t % 2) * P:(t % 2 + 1) * P],
                                   psum[:, b, :].rearrange("p (g q) -> p g q", g=4)).then_inc(bank_drained[b], 1)
                Wd = D * M // P
                for e in range(EXPERTS):
                    b = filled(act, ("HG", l, e))
                    if e >= 2:
                        act.wait_ge(hid_ready, EXPERTS * l + e - 1)
                    nc.scalar.activation(sil[:, e % 2, 0:Wd], psum[:, b, 0:Wd], ACT.Silu).then_inc(bank_drained[b], 1)
                    b = filled(act, ("HT", l, e))
                    if e >= 2:
                        filled(act, ("YE", l, e - 2))
                    nc.scalar.copy(hidT[:, e % 2, 0:Wd], psum[:, b, 0:Wd]).then_inc(bank_drained[b], 1)
                norm_roots(l, 1)

        @block.vector
        def _(dve):
            steps = [0]
            V_ = nc.vector

            def run(ins):
                steps[0] += 1
                ins.then_inc(dve_step, 1)
                dve.wait_ge(dve_step, steps[0])

            def mark(sem):
                V_.engine_nop().then_inc(sem, 1)

            def ada_bias(l, third):
                n = 3 * l + third
                dve.wait_ge(mod_loaded, 64 * (n + 1))
                V_.tensor_tensor(modsb[:, :], modsb[:, :], modb[:, :], ALU.add).then_inc(mod_biased, 1)

            def ada_columns(l, third):
                b = filled(dve, ("adaT", l, third))
                src = psum[:, b, 0:32].rearrange("p (s c) -> p s c", s=2)
                dst = modcol[:, l, :, 16 * third:16 * third + 16]
                for at in (0, 8):
                    one = (third, at) in ((0, 8), (2, 0))
                    ins = V_.tensor_scalar(dst[:, :, at:at + 8], src[:, :, at:at + 8], 1.0 if one else 0.0, None,
                                           ALU.add)
                    if at:
                        ins.then_inc(mod_cols, 1)
                mark(bank_drained[b])

            def rope(t, xin, outs, h, half):
                at = C_ROPE + 192 * (t - 2) + (0 if half == 16 else 128)
                w = 4 * half
                cos = cst[:, at:at + w]
                sin = cst[:, at + w:at + 2 * w]
                x3 = xin.rearrange("p (h d) -> p h d", d=w)
                V_.tensor_tensor(m1[:, 0:h * w].rearrange("p (h d) -> p h d", d=w), x3,
                                 cos.unsqueeze(1).to_broadcast([P, h, w]), ALU.mult)
                x5 = xin.rearrange("p (h a z d) -> p h a z d", a=2, z=2, d=half)
                o5 = m2[:, 0:h * w].rearrange("p (h a z d) -> p h a z d", a=2, z=2, d=half)
                s4 = sin.rearrange("p (a z d) -> p a z d", a=2, z=2)
                for z in (0, 1):
                    ins = V_.tensor_tensor(o5[:, :, :, z, :], x5[:, :, :, 1 - z, :],
                                           s4[:, :, z, :].unsqueeze(1).to_broadcast([P, h, 2, half]), ALU.mult)
                    if z == 0:
                        continue
                    run(ins)
                for o, view in outs[:-1]:
                    V_.tensor_tensor(o, view(m1), view(m2), ALU.add)
                o, view = outs[-1]
                run(V_.tensor_tensor(o, view(m1), view(m2), ALU.add))

            def pad_view(i, g):
                return qpad[:, i, 384 * g:384 * g + 384].rearrange("p (r d) -> p r d", r=3)[:, :, HD * g:HD * g + HD]

            def third(v, g):
                return v[:, 192 * g:192 * g + 192].rearrange("p (r d) -> p r d", r=3)

            def heads_out(i, cut):
                outs = [] if cut else [(pad_view(i, 0), lambda v: third(v, 0)), (pad_view(i, 1), lambda v: third(v, 1))]
                return outs + [(knat[:, i, :], lambda v: v[:, 384:512])]

            def qkv(l):
                for step in QKV_STEPS:
                    kind, t = step[0], step[-1]
                    cut = l == DEPTH - 1 and t < 2
                    i = t % 2
                    if kind == "P" and step[1] == 1:
                        b = filled(dve, ("P", l, 1, t))
                        if t == 0:
                            dve.wait_ge(proj_par_in, 96 * (l + 1))
                        dve.wait_ge(root_ready, 8 * l + t + 1)
                        if l or t:
                            dve.wait_ge(cqn_ready, 4 * l + t)
                        run(V_.reciprocal(small[:, 20:22], small[:, 2:4]))
                        if t >= 2:
                            filled(dve, ("N", l, t - 2))
                        V_.scalar_tensor_tensor(cqn[:, i, 0:256], psum[:, b, 128:384], small[:, 20:21],
                                                gain_cq[:, 0:256], ALU.mult, ALU.mult).then_inc(rms_taken, 1)
                        V_.scalar_tensor_tensor(cqn[:, i, 256:384], psum[:, b, 384:512], small[:, 21:22],
                                                gain_cq[:, 256:384], ALU.mult, ALU.mult).then_inc(cqn_ready, 1)
                        mark(bank_drained[b])
                    if kind == "P" and step[1] == 3:
                        b = second(dve, ("P", l, 3, t))
                        if t < 2:
                            V_.tensor_copy(krr[:, t, :], psum[:, b, 0:ROPE_B]).then_inc(bank_drained[b], 1)
                        else:
                            rope(t, psum[:, b, 0:ROPE_B], [(krr[:, t, :], lambda v: v[:, 0:ROPE_B])], 1, 8)
                            mark(bank_drained[b])
                    if kind == "U":
                        qb = qbn[:, i, :].rearrange("p (h d) -> p h d", h=4)
                        kb = kbn[:, i, :].rearrange("p (h d) -> p h d", h=4)
                        if t >= 2:
                            filled(dve, ("TBk", l, t - 2))
                        if not cut:
                            b = filled(dve, ("UQ", l, t))
                            src = psum[:, b, 0:384].rearrange("p (h d) -> p h d", h=4)
                            if t < 2:
                                V_.tensor_copy(qb, src).then_inc(bank_drained[b], 1)
                            else:
                                V_.tensor_copy(qb[:, :, 0:HD], src[:, :, 0:HD])
                                run(V_.tensor_copy(xg[:, 0:128].rearrange("p (h d) -> p h d", h=4), src[:, :, HD:]))
                                rope(t, xg[:, 0:128], [(qb[:, :, HD:], lambda v: v[:, 0:128].rearrange(
                                    "p (h d) -> p h d", h=4))], 4, 8)
                                mark(bank_drained[b])
                        b = second(dve, ("UKV", l, t))
                        V_.tensor_copy(kb[:, :, 0:HD],
                                       psum[:, b, :].rearrange("p (h d) -> p h d", h=4)[:, :, 0:HD]) \
                            .then_inc(bank_drained[b], 1)
                        drained(dve, ("P", l, 3, t))
                        V_.tensor_copy(kb[:, :, HD:], krr[:, t, :].unsqueeze(1).to_broadcast([P, 4, ROPE_B])) \
                            .then_inc(qkb_ready, 1)
                    if kind == "P" and step[1] == 0:
                        b = filled(dve, ("P", l, 0, t))
                        if t == 0:
                            dve.wait_ge(pads_zero, l + 1)
                        if t >= 2:
                            filled(dve, ("TAr", l, t - 2))
                        if t < 2:
                            for o, view in heads_out(i, cut):
                                V_.tensor_copy(o, view(psum[:, b, :]))
                        else:
                            rope(t, psum[:, b, :], heads_out(i, cut), 8, 16)
                        mark(bank_drained[b])
                        mark(qk_ready)
                    if kind == "P" and step[1] == 2:
                        b = filled(dve, ("P", l, 2, t))
                        h0 = 6 if cut else 0
                        second(dve, ("P", l, 2, t))
                        V_.tensor_reduce(small[:, 4 + h0:12],
                                         sq[:, 64 * h0:512].rearrange("p (h d) -> p h d", d=HD), AX, ALU.add) \
                            .then_inc(sumsq_ready, 1)
                        dve.wait_ge(root_ready, 8 * l + 4 + t + 1)
                        run(V_.reciprocal(small[:, 32 + h0:40], small[:, 12 + h0:20]))
                        nh = 8 - h0
                        run(V_.tensor_tensor(xg[:, 64 * h0:512].rearrange("p (h d) -> p h d", d=HD),
                                             psum[:, b, 64 * h0:512].rearrange("p (h d) -> p h d", d=HD),
                                             small[:, 32 + h0:40].unsqueeze(2).to_broadcast([P, nh, HD]), ALU.mult))
                        mark(bank_drained[b])
                        mark(rms_taken)
                        filled(dve, ("TAr", l, t + 2) if t < 2 else ("TCr", l, t - 2))
                        g6 = gain_q.unsqueeze(1).to_broadcast([P, 6, HD])
                        g2 = gain_k.unsqueeze(1).to_broadcast([P, 2, HD])
                        k2 = xg[:, 384:512].rearrange("p (h d) -> p h d", d=HD)
                        if t < 2:
                            if not cut:
                                for g in (0, 1):
                                    V_.tensor_tensor(pad_view(i, g), third(xg, g),
                                                     gain_q.unsqueeze(1).to_broadcast([P, 3, HD]), ALU.mult)
                            V_.tensor_tensor(knat[:, i, :].rearrange("p (h d) -> p h d", d=HD), k2, g2, ALU.mult) \
                                .then_inc(qk_ready, 1)
                        else:
                            q6 = xg[:, 0:384].rearrange("p (h d) -> p h d", d=HD)
                            V_.tensor_tensor(q6, q6, g6, ALU.mult)
                            run(V_.tensor_tensor(k2, k2, g2, ALU.mult))
                            rope(t, xg, heads_out(i, cut), 8, 16)
                            mark(qk_ready)

            def attention(l, s, step):
                nk = 2 if s == 0 else 4
                us = units(l, s)
                for i in range(len(us) + 4):
                    if i < len(us):
                        u, j, h, q = us[i]
                        br, head = PAIRS[j][0], PAIRS[j][1] + h
                        b = filled(dve, ("S", l, s, u))
                        c4 = 24 + 4 * (u % 2)
                        if br == "A" and s == 1:
                            run(V_.tensor_tensor(psum[:, b, 256:512], psum[:, b, 256:512],
                                                 cst[:, C_MASK + 256 * q:C_MASK + 256 * q + 256], ALU.add))
                        run(V_.tensor_reduce(small[:, c4 + 3:c4 + 4], psum[:, b, 0:nk * P], AX, ALU.max, negate=True))
                        if br == "A":
                            V_.tensor_scalar(small[:, c4:c4 + 1], small[:, c4 + 3:c4 + 4], SCALE_AC,
                                             nsink[:, head:head + 1], ALU.mult, ALU.min).then_inc(max_ready, 1)
                        else:
                            V_.tensor_scalar(small[:, c4:c4 + 1], small[:, c4 + 3:c4 + 4],
                                             SCALE_B if br == "B" else SCALE_AC, None, ALU.mult) \
                                .then_inc(max_ready, 1)
                    if l == 0:
                        due = ada_events(step)
                        if "bias" in due:
                            ada_bias(*due["bias"])
                        if "columns" in due:
                            ada_columns(*due["columns"])
                    step += 1
                    if 1 <= i < len(us) + 1:
                        u, j, h, q = us[i - 1]
                        c4 = 24 + 4 * (u % 2)
                        drained(dve, ("S", l, s, u))
                        if PAIRS[j][0] == "A":
                            run(V_.tensor_tensor(small[:, c4 + 2:c4 + 3], small[:, c4 + 2:c4 + 3],
                                                 small[:, c4 + 1:c4 + 2], ALU.add))
                        run(V_.reciprocal(small[:, c4 + 2:c4 + 3], small[:, c4 + 2:c4 + 3]))
                        V_.tensor_scalar(prob[:, u % 2, 0:nk * P], prob[:, u % 2, 0:nk * P],
                                         small[:, c4 + 2:c4 + 3], None, ALU.mult).then_inc(prob_ready, 1)
                return step

            def layer_norm(l, t, n, xt):
                V_.bn_stats(stats[:, 0, :], xt[:, 0:512])
                run(V_.bn_stats(stats[:, 1, :], xt[:, 512:1024]))
                if n:
                    dve.wait_ge(std_ready, n)
                V_.bn_aggr(small[:, 41:43], stats[:, :, :].rearrange("p a b -> p (a b)")).then_inc(var_ready, 1)
                dve.wait_ge(std_ready, n + 1)
                run(V_.reciprocal(small[:, 46:47], small[:, 43:44]))
                run(V_.tensor_scalar(xt, xt, small[:, 41:42], small[:, 46:47], ALU.subtract, ALU.mult))
                run(V_.tensor_tensor(xt, xt, norm_g, ALU.mult))
                run(V_.tensor_tensor(X[:, t, :], xt, norm_b, ALU.add))
                mark(x_ready)

            def project(l):
                for i, t in enumerate(tiles(l)):
                    if i == 0:
                        dve.wait_ge(norm_par_in, 64 * (2 * l + 1))
                    lt = ln_t[:, i % 2, :]
                    for n in (0, 1):
                        b = filled(dve, ("Y", l, t, n))
                        ins = V_.tensor_tensor(lt[:, 512 * n:512 * n + 512], psum[:, b, :],
                                               gate_of[t // 2][:, 512 * n:512 * n + 512], ALU.mult)
                        ins.then_inc(bank_drained[b], 1)
                    drained(dve, ("Y", l, t, 1))
                    run(V_.scalar_tensor_tensor(lt, X[:, t, :], ALPHA, lt, ALU.mult, ALU.add))
                    layer_norm(l, t, 2 * first_tile(l) + i, lt)

            def route(l):
                S0 = streams(l)[0]
                R = EXPERTS * len(streams(l))
                for i, t in enumerate(tiles(l)):
                    b = filled(dve, ("R", l, t))
                    col = 16 * (t // 2 - S0)
                    V_.tensor_reduce(small[:, 44:45], psum[:, b, 0:EXPERTS], AX, ALU.max, negate=True) \
                        .then_inc(aff_max, 1)
                    drained(dve, ("R", l, t))
                    run(V_.reciprocal(small[:, 45:46], small[:, 45:46]))
                    a = affn[:, t % 2, col:col + 16]
                    run(V_.tensor_scalar(a, a, small[:, 45:46], None, ALU.mult))
                mark(aff_ready)
                run(V_.memset(ones[0:R, :], 1.0))
                b = filled(dve, ("AT", l))
                run(V_.tensor_copy(topT[0:R, 0, :], psum[0:R, b, 0:256]))
                mark(bank_drained[b])
                for r in range(CAP // 8):
                    run(V_.max(max8[0:R, :], topT[0:R, r % 2, :]))
                    run(V_.match_replace(topT[0:R, (r + 1) % 2, :], max8[0:R, :], topT[0:R, r % 2, :], -1.0))
                run(V_.tensor_scalar(topT[0:R, 2, :], topT[0:R, 0, :], 0.0, None, ALU.is_lt))
                run(V_.tensor_tensor_scan(topT[0:R, 3, :], ones[0:R, :], topT[0:R, 2, :], 0.0, ALU.mult, ALU.add))
                V_.tensor_tensor(topT[0:R, 3, :], topT[0:R, 3, :], topT[0:R, 2, :], ALU.mult).then_inc(pos_ready, 1)
                b = filled(dve, ("PT", l))
                run(V_.tensor_copy(posn[:, :, 0:R], psum[:, b, 0:2 * R].rearrange("p (i r) -> p i r", i=2)))
                mark(bank_drained[b])
                for t in tiles(l):
                    col = 16 * (t // 2 - S0)
                    oh = onehot[:, t, :].rearrange("p (e m) -> p e m", m=CAP)
                    V_.tensor_tensor(oh, iota1.unsqueeze(1).to_broadcast([P, EXPERTS, CAP]),
                                     posn[:, t % 2, col:col + 16].unsqueeze(2).to_broadcast([P, EXPERTS, CAP]),
                                     ALU.is_equal).then_inc(onehot_ready, 1)
                    dve.wait_ge(onehot_ready, 2 * first_tile(l) + 2 * tiles(l).index(t) + 1)
                    V_.tensor_tensor(ohw[:, t, :].rearrange("p (e m) -> p e m", m=CAP), oh,
                                     affn[:, t % 2, col:col + 16].unsqueeze(2).to_broadcast([P, EXPERTS, CAP]),
                                     ALU.mult).then_inc(onehot_ready, 1)
                for s in streams(l):
                    filled(dve, ("XS", l, KT - 1, s))
                for t in tiles(l):
                    run(V_.tensor_scalar(X[:, t, :], X[:, t, :], ALPHA, None, ALU.mult))

            def experts(l):
                M = CAP * len(streams(l))
                Wd = D * M // P
                dve.wait_ge(norm_par_in, 64 * (2 * l + 2))

                def scatter(g):
                    for i, t in enumerate(tiles(l)):
                        for n in (0, 1):
                            b = filled(dve, ("SC", l, g, t, n))
                            cols = slice(512 * n, 512 * n + 512)
                            V_.tensor_tensor(yg_t, psum[:, b, :], gate_of[t // 2][:, cols], ALU.mult) \
                                .then_inc(bank_drained[b], 1)
                            drained(dve, ("SC", l, g, t, n))
                            run(V_.tensor_tensor(X[:, t, cols], X[:, t, cols], yg_t, ALU.add))
                        if g == 3:
                            layer_norm(l, t, 2 * first_tile(l) + len(tiles(l)) + i, X[:, t, :])

                for e in range(EXPERTS + 1):
                    if e < EXPERTS:
                        b = filled(dve, ("HU", l, e))
                        drained(dve, ("HG", l, e))
                        if e >= 2:
                            filled(dve, ("HT", l, e - 2))
                        V_.tensor_tensor(hid[:, e % 2, 0:Wd], sil[:, e % 2, 0:Wd], psum[:, b, 0:Wd], ALU.mult) \
                            .then_inc(hid_ready, 1)
                        mark(bank_drained[b])
                    if e >= 5 and e % 4 == 1:
                        scatter(e // 4 - 1)
                    if e >= 1:
                        b = filled(dve, ("YE", l, e - 1))
                        if e >= 3:
                            dve.wait_ge(y_moved[(e - 1) % 2], 64 * (EXPERTS * l // 2 + (e - 1) // 2))
                        V_.tensor_copy(ysb[:, (e - 1) % 2, 0:Wd], psum[:, b, 0:Wd]).then_inc(y_ready, 1)
                        mark(bank_drained[b])
                scatter(3)

            dve.wait_ge(consts_in, 16)
            ada_bias(0, 0)
            ada_columns(0, 0)
            step = 0
            for l in range(DEPTH):
                dve.wait_ge(sink_in, 16 * (l + 1))
                run(V_.tensor_scalar(nsink[:, :], sink[:, :], -1.0, None, ALU.mult))
                qkv(l)
                for s in streams(l):
                    step = attention(l, s, step)
                n_gates = 6 * first_tile(l)
                for n in (0, 1):
                    for br in range(3):
                        for t in tiles(l):
                            b = filled(dve, ("BR", l, n, br, t))
                            drained(dve, ("G", l, n, br, t))
                            i = n_gates
                            n_gates += 1
                            dst = merged[:, t, 512 * n:512 * n + 512]
                            V_.tensor_tensor(dst if br == 0 else gtmp, sg[:, i % 2, :], psum[:, b, :], ALU.mult) \
                                .then_inc(gate_used, 1)
                            mark(bank_drained[b])
                            if br:
                                dve.wait_ge(gate_used, i + 1)
                                ins = V_.tensor_tensor(dst, dst, gtmp, ALU.add)
                                run(ins)
                                if br == 2 and n == 1:
                                    mark(merged_ready)
                project(l)
                route(l)
                experts(l)


_INS = ["x", "c", "ctx", "c_ctx", "w_ada", "b_ada", "w_in", "a_sink", "b_q_norm", "b_kv_norm", "b_w_uq", "b_w_ukv",
        "c_q_norm", "c_k_norm", "w_branch", "w_out", "ln1_g", "ln1_b", "w_router", "w_gate", "w_up", "w_down",
        "ln2_g", "ln2_b"]


def tables():
    import numpy as np
    grid_w, window = 64, 128
    t = np.zeros((P, C_ALL), np.float32)
    t[:, C_ID:C_ID + P] = np.eye(P)
    for q in (0, 1):
        pos = q * P + np.arange(P)
        far = np.abs(pos[:, None] - np.arange(256)[None, :]) > window
        t[:, C_MASK + 256 * q:C_MASK + 256 * q + 256] = np.where(far, -1e30, 0.0)
        at = C_ROPE + 192 * q
        for half in (16, 8):
            freqs = (np.float32(10000.0) ** (-np.arange(half, dtype=np.float32) / half)).astype(np.float32)
            for axis, p in enumerate((pos // grid_w, pos % grid_w)):
                ang = p.astype(np.float32)[:, None] * freqs
                a = at + 2 * half * axis
                t[:, a:a + 2 * half] = np.concatenate([np.cos(ang), np.cos(ang)], 1)
                t[:, a + 4 * half:a + 6 * half] = np.concatenate([-np.sin(ang), np.sin(ang)], 1)
            at += 8 * half
    t[:, C_IOTA:C_IOTA + CAP] = 1 + np.arange(CAP)
    return t


def kernel(**inputs):
    import numpy as np
    import concourse.bacc as bacc
    from concourse.bass_utils import run_bass_kernel_spmd

    nc = bacc.Bacc("TRN2", target_bir_lowering=False, num_devices=1)
    arrays, args = {}, []
    for name in _INS:
        a = np.ascontiguousarray(inputs[name])
        arrays[f"in_{name}"] = a
        args.append(nc.dram_tensor(f"in_{name}", a.shape, F32, kind="ExternalInput").ap())
    arrays["in_tables"] = tables()
    args.append(nc.dram_tensor("in_tables", (P, C_ALL), F32, kind="ExternalInput").ap())
    out = nc.dram_tensor("out", (1, 256, D), F32, kind="ExternalOutput").ap()
    trunk(nc, *args, out)
    r = run_bass_kernel_spmd(nc, [arrays], core_ids=[0])
    return r.results[0]["out"]
```

```python
import concourse.bass as bass
from concourse import mybir
from contextlib import ExitStack

F32 = mybir.dt.float32
F32R = mybir.dt.float32r
ALU = mybir.AluOpType
ACT = mybir.ActivationFunctionType
AX = mybir.AxisListType.X

P = 128
D = 1024
KT = D // P
DEPTH = 2
HD = 64
HEADS_A, HEADS_B = 6, 4
QK_B, ROPE_B = 96, 32
EXPERTS, CAP = 16, 32
ALPHA = (2 * DEPTH) ** 0.25
SCALE_AC, SCALE_B = HD ** -0.5, QK_B ** -0.5
LN_EPS, RMS_EPS = 1e-5, 1e-6
RING, SLOT = 8, 2048
ADA_BANK, TURN_BANK = 7, 6
GATE_COL = 1696
CHUNKS = {0: [(0, 512)], 1: [(512, 512)], 2: [(1056, 512)], 3: [(1024, 32), (1568, 128)]}
BRANCH_TILES = [(0, 3), (3, 5), (5, 8)]
SH1, SC1, G1, SH2, SC2, G2 = range(6)
C_ID, C_MASK, C_ROPE, C_IOTA, C_ALL = 0, 128, 640, 1024, 1056

QKV_STEPS = [("P", 1, 0), ("P", 1, 1), ("N", 0), ("P", 1, 2), ("N", 1), ("P", 1, 3), ("N", 2), ("P", 3, 0), ("N", 3),
             ("P", 3, 1), ("U", 0), ("P", 3, 2), ("U", 1), ("TB", 0), ("P", 3, 3), ("U", 2), ("TB", 1), ("P", 0, 0),
             ("U", 3), ("TB", 2), ("P", 0, 1), ("TB", 3), ("TA", 0), ("P", 0, 2), ("TA", 1), ("P", 0, 3), ("TA", 2),
             ("P", 2, 0), ("TA", 3), ("P", 2, 1), ("TC", 0), ("P", 2, 2), ("TC", 1), ("P", 2, 3), ("TC", 2),
             ("TC", 3)]
PAIRS = [("A", 0), ("A", 2), ("A", 4), ("B", 0), ("B", 2), ("C", 0), ("C", 2), ("C", 4)]


def trunk(nc, x, c, ctx_in, c_ctx, w_ada, b_ada, w_in, a_sink, b_q_norm, b_kv_norm, b_w_uq, b_w_ukv, c_q_norm,
          c_k_norm, w_branch, w_out, ln1_g, ln1_b, w_router, w_gate, w_up, w_down, ln2_g, ln2_b, consts, out):
    es = ExitStack()
    with es:
        def sb(name, shape):
            return es.enter_context(nc.sbuf_tensor(name, shape, F32))

        def sem(name):
            return es.enter_context(nc.semaphore(name))

        arena = nc.sbuf_base + (-nc.sbuf_base) % 64
        sizes = {"ring": RING * SLOT, "X": 4 * D, "hT": KT * 512, "A": 13312, "B": 4096, "PR": 4096, "W": 4096}
        sb("arena", [P, sum(sizes.values()) + 16])
        place, at = {}, arena
        for name, n in sizes.items():
            place[name] = at
            at += 4 * n

        def fixed(name, shape, dtype=F32, where=None, skip=0):
            return nc.alloc_sbuf_tensor_at(name, shape, dtype, offset=place[where or name] + 4 * skip)

        ring = fixed("ring", [P, RING, SLOT])
        X = fixed("X", [P, 4, D])
        hT = fixed("hT", [P, KT, 512])
        A = fixed("A", [P, 13312])
        B = fixed("B", [P, 4096])
        PR = fixed("PR", [P, 4096])
        W = fixed("W", [P, 4096])
        ring_r = fixed("ring_r", [P, RING, SLOT], F32R, "ring")
        h_hi = fixed("h_hi", [P, KT, 512], F32R, "A", 4096)
        h_lo = fixed("h_lo", [P, KT, 512], F32R, "hT")
        o_hi = fixed("o_hi", [P, KT, 512], F32R, "A", 8192)
        o_lo = fixed("o_lo", [P, KT, 512], F32R, "B")
        cst = sb("cst", [P, C_ALL])
        cs = sb("cs", [P, KT, 32])
        modrow = sb("modrow", [P, 512])
        bias_cols = sb("bias_cols", [P, 48 * DEPTH])
        modcol = sb("modcol", [P, DEPTH, 2, 48])
        mod_rows = sb("mod_rows", [96, P])
        wr = sb("wr", [P, KT, EXPERTS])
        sink = sb("sink", [P, HEADS_A])
        nsink = sb("nsink", [P, HEADS_A])
        eps = sb("eps", [P, 2])
        krr = sb("krr", [P, 4, ROPE_B])
        small = sb("small", [P, 96])
        stats = sb("stats", [P, 2, 6])
        affn = sb("affn", [P, 2, 32])
        posn = sb("posn", [P, 2, 32])
        max8 = sb("max8", [32, 8])
        psum = es.enter_context(nc.psum_tensor("psum", [P, 8, 512], F32))
        mod_all = nc.dram_tensor("mod_all", (DEPTH, 2, 48, P), F32).ap()

        def part(t, at, *shape):
            n = 1
            for s in shape:
                n *= s
            v = t[:, at:at + n]
            if len(shape) == 2:
                v = v.rearrange("p (a b) -> p a b", b=shape[1])
            if len(shape) == 3:
                v = v.rearrange("p (a b c) -> p a b c", b=shape[1], c=shape[2])
            return v

        ident = cst[:, C_ID:C_ID + P]
        iota1 = cst[:, C_IOTA:C_IOTA + CAP]
        qT = {"A": part(A, 0, 6, 512), "C": part(A, 3072, 6, 512), "B": part(A, 6144, 4, 512)}
        kT = {"A": part(A, 8192, 512), "C": part(A, 8704, 512), "B": part(A, 9216, 4, 512)}
        V = {"A": part(A, 11264, 4, P), "C": part(A, 11776, 4, P), "B": part(A, 12288, 4, 256)}
        merged = part(A, 0, 4, D)
        mT = part(A, 4096, KT, 512)
        xsT = part(A, 0, KT, 1024)
        sil = part(A, 8192, 2, 512)
        hid = part(A, 9216, 2, 512)
        hidT = part(A, 10240, 2, 512)
        ysb = part(A, 11264, 2, 512)
        qpad = part(B, 0, 2, 768)
        knat = part(B, 1536, 2, P)
        cqn = part(B, 1792, 2, 384)
        qbn = part(B, 2560, 2, 384)
        kbn = part(B, 3328, 2, 384)
        oT = part(B, 0, KT, 512)
        YG = part(B, 0, 4, D)
        uq = part(PR, 0, 2, 384)
        ukv = part(PR, 768, 512)
        gain_cq = part(PR, 1280, 384)
        gain_q = part(PR, 1664, HD)
        gain_k = part(PR, 1728, HD)
        bias_rows, cin = part(PR, 3584, P)[0:48 * DEPTH, :], part(PR, 3712, P)[0:2 * KT, :]
        norm_g, norm_b = part(PR, 0, D), part(PR, D, D)
        gate_of = {0: part(PR, 2048, D), 1: part(PR, 3072, D)}
        gate_y = part(PR, 2048, 512)
        m1, m2, sq, xg = (part(W, 512 * i, 512) for i in range(4))
        cqT = part(W, 2048, 3, 512)
        prob = part(PR, 0, 4, 512)
        pT = part(W, 0, 3, 1024)
        sg = part(W, 0, 4, 512)
        gtmp = part(W, 2048, 512)
        ln_t = part(W, 0, 2, D)
        onehot = part(W, 0, 4, 512)
        ones = part(W, 2560, 256)
        topT = part(W, 3072, 4, 256)
        ohw = part(hT[:, :, :].rearrange("p a b -> p (a b)"), 0, 4, 512)
        ohT = part(hT[:, :, :].rearrange("p a b -> p (a b)"), 2048, 8, 256)

        bank_filled = [sem(f"bank_filled{b}") for b in range(8)]
        bank_drained = [sem(f"bank_drained{b}") for b in range(8)]
        slot_filled = [sem(f"slot_filled{s}") for s in range(RING)]
        slot_free = [sem(f"slot_free{s}") for s in range(RING)]
        consts_in = sem("consts_in")
        c_in = sem("c_in")
        zeros_set = sem("zeros_set")
        x_in = sem("x_in")
        proj_par_in = sem("proj_par_in")
        norm_par_in = sem("norm_par_in")
        router_in = sem("router_in")
        sink_in = sem("sink_in")
        bias_in = sem("bias_in")
        mod_stored = sem("mod_stored")
        mod_cols = sem("mod_cols")
        part_in = sem("part_in")
        parts = [0]
        early_in = [sem(f"early_in{i}") for i in range(4)]
        split_high = sem("split_high")
        split_low = sem("split_low")
        root_ready = sem("root_ready")
        sumsq_ready = sem("sumsq_ready")
        rms_taken = sem("rms_taken")
        cqn_ready = sem("cqn_ready")
        qkb_ready = sem("qkb_ready")
        qk_ready = sem("qk_ready")
        pads_zero = sem("pads_zero")
        max_ready = sem("max_ready")
        prob_ready = sem("prob_ready")
        gate_used = sem("gate_used")
        merged_ready = sem("merged_ready")
        var_ready = sem("var_ready")
        std_ready = sem("std_ready")
        x_ready = sem("x_ready")
        aff_max = sem("aff_max")
        aff_exp = sem("aff_exp")
        aff_ready = sem("aff_ready")
        pos_ready = sem("pos_ready")
        onehot_ready = sem("onehot_ready")
        weighted_ready = sem("weighted_ready")
        hid_ready = sem("hid_ready")
        y_ready = sem("y_ready")
        y_moved = [sem(f"y_moved{i}") for i in (0, 1)]
        y_used = sem("y_used")
        out_stored = sem("out_stored")
        dve_step = sem("dve_step")
        act_step = sem("act_step")
        pool_step = sem("pool_step")
        block = es.enter_context(nc.Block())

        groups = {}
        fills, drains = [0] * 8, [0] * 8
        turn = [0]
        pieces, freed = [], []
        stream, gates_done = [], {}
        early = [(A, 8192), (A, 10240), (B, 0), (B, 2048)]
        frees, loads = [0] * RING, [0] * RING
        splits = [[] for _ in range(DEPTH)]

        def filled(eng, key):
            b, n, _ = groups[key]
            eng.wait_ge(bank_filled[b], n)
            return b

        def drained(eng, key):
            b, _, n = groups[key]
            eng.wait_ge(bank_drained[b], n)

        def second(eng, key):
            b, _, n = groups[key]
            eng.wait_ge(bank_drained[b], n - 1)
            return b

        def streams(l):
            return [0, 1] if l < DEPTH - 1 else [1]

        def tiles(l):
            return [t for s in streams(l) for t in (2 * s, 2 * s + 1)]

        def first_tile(l):
            return sum(len(tiles(i)) for i in range(l))

        def first_splits(l):
            return 2 * len(tiles(l)) + 3

        def split_base(l):
            return sum(first_splits(i) + 15 for i in range(l))

        def split_order(l):
            f = first_splits(l)
            out = []
            for s in range(6):
                before = list(range(f)) if s == 0 else []
                after = []
                if s < 5:
                    before += [f + 3 * s, f + 3 * s + 1]
                    after = [f + 3 * s + 2]
                out.append((before, after))
            return out

        def units(l, s):
            return [(4 * j + 2 * h + q, j, h, q) for j in range(8) for h in (0, 1) for q in (0, 1)]

        def unit_base(l, s):
            return 32 * (2 * l + s) if l == 0 else 64

        ADA_LATER = [(0, 1), (0, 2), (1, 0), (1, 1), (1, 2)]
        QKV_TURNS = 16
        ada_due = {}
        for n in range(8 * len(ADA_LATER)):
            at = n if n < QKV_TURNS else QKV_TURNS + (n - QKV_TURNS) * 11 // 4
            which = ADA_LATER[n // 8]
            ada_due.setdefault(at, {})["products"] = which + (n % 8,)
            if n % 8 == 7:
                ada_due.setdefault(at, {})["move"] = which
                ada_due.setdefault(at + 2, {})["turn"] = which
                if which[1] == 2:
                    ada_due.setdefault(at + 4, {})["rows"] = which[0]

        @block.tensor
        def _(pe):
            def begin(key, takers=1, bank=None):
                b = turn[0] % 6 if bank is None else bank
                if bank is None:
                    turn[0] += 1
                if drains[b]:
                    pe.wait_ge(bank_drained[b], drains[b])
                fills[b] += 1
                drains[b] += takers
                groups[key] = (b, fills[b], drains[b])
                return b

            def end(ins, b):
                ins.then_inc(bank_filled[b], 1)
                return (bank_filled[b], fills[b])

            def piece(src, *shape):
                n = load(src, *shape)
                pe.wait_ge(slot_filled[n % RING], 16 * loads[n % RING])
                return n, pieces[n][0]

            def load(src, *shape):
                n = len(pieces)
                pieces.append((part(ring[:, n % RING, :], 0, *shape), src))
                stream.append((*pieces[n], n, None))
                freed.append(None)
                loads[n % RING] += 1
                return n

            def early_piece(l, i, src, *shape):
                dst = part(*early[i], *shape)
                stream.append((dst, src, i, gates_done[l]))
                pe.wait_ge(early_in[i], 16 * (l + 1))
                return dst

            def split_piece(l, src, *shape):
                n = load(src, *shape)
                pieces.append(None)
                freed.append(None)
                hi, lo = (part(ring_r[:, m % RING, :], 0, *shape) for m in (n + 1, n))
                splits[l].append((pieces[n][0], hi, lo, hi.bitcast(F32),
                                  (n, 16 * loads[n % RING])))
                return len(splits[l]), n, hi, lo

            def split_rows(l, src, hi, lo, t):
                cols = slice(t * P, (t + 1) * P)
                splits[l].append((src[:, :, cols], hi[:, :, cols], lo[:, :, cols], hi[:, :, cols].bitcast(F32), None))
                return len(splits[l])

            def free(n, ins=None, event=None):
                if event is None:
                    frees[n % RING] += 1
                    ins.then_inc(slot_free[n % RING], 1)
                    event = (slot_free[n % RING], frees[n % RING])
                freed[n] = event

            def mm(o, a, b, start=True, stop=True):
                return nc.tensor.matmul(o, a, b, start=start, stop=stop, skip_group_check=True)

            def ada_products(l, third, k):
                if k == 0:
                    begin(("ada", l, third), bank=ADA_BANK)
                n, w = piece(w_ada[l, k * P:(k + 1) * P, third * 2048:(third + 1) * 2048], 2048)
                for g in range(4):
                    ins = mm(psum[32 * g:32 * g + 32, ADA_BANK, :], cs[:, k, :], w[:, 512 * g:512 * g + 512],
                             k == 0, k == KT - 1)
                if k == KT - 1:
                    free(n, event=end(ins, ADA_BANK))
                else:
                    free(n, ins)

            def ada_turn(l, third):
                drained(pe, ("ada", l, third))
                b = begin(("adaT", l, third), bank=TURN_BANK)
                for j in range(4):
                    ins = nc.tensor.transpose(psum[:, b, P * j:P * j + P], modrow[:, P * j:P * j + P], ident)
                end(ins, b)

            def ada_rows(l):
                pe.wait_ge(mod_cols, 3 * l + 3)
                b = begin(("adaR", l), bank=TURN_BANK)
                end(nc.tensor.transpose(psum[0:96, b, 0:P], modcol[:, l, :, :].rearrange("p s c -> p (s c)"), ident), b)

            def ada_hook(step):
                due = ada_due.get(step, {})
                if "turn" in due:
                    ada_turn(*due["turn"])
                if "rows" in due:
                    ada_rows(due["rows"])
                if "products" in due:
                    ada_products(*due["products"])

            def transposes(key, sources, rows=P, takers=1):
                b = begin(key, takers)
                for i, s in enumerate(sources):
                    ins = nc.tensor.transpose(psum[0:rows, b, i * P:(i + 1) * P], s, ident)
                end(ins, b)

            def x_transposes(name, l, t):
                for j in (0, 1):
                    transposes((name, l, t, j), [X[:, t, k * P:(k + 1) * P] for k in range(4 * j, 4 * j + 4)])

            def qkv(l):
                held, turns = None, 0
                for step in QKV_STEPS:
                    kind, t = step[0], step[-1]
                    cut = l == DEPTH - 1 and t < 2
                    if kind == "P":
                        ch = step[1]
                        width = sum(w for _, w in CHUNKS[ch])
                        if t == 0:
                            held = [piece([w_in[l, 512 * h:512 * h + 512, a:a + w] for a, w in CHUNKS[ch]], 4, width)
                                    for h in (0, 1)]
                        b = begin(("P", l, ch, t), takers=2 if ch != 0 else 1)
                        lo = 384 if cut and ch in (0, 2) else 0
                        if ch == 1:
                            drained(pe, ("hT", l, t, 0))
                            drained(pe, ("hT", l, t, 1))
                        for k in range(KT):
                            ins = mm(psum[:, b, lo:width], hT[:, k, t * P:(t + 1) * P], held[k // 4][1][:, k % 4, lo:],
                                     k == 0, k == KT - 1)
                        event = end(ins, b)
                        if t == 3:
                            for n, _ in held:
                                free(n, event=event)
                        if l == 0:
                            ada_hook(turns)
                            turns += 1
                    if kind == "N":
                        pe.wait_ge(cqn_ready, 4 * l + t + 1)
                        transposes(("N", l, t), [cqn[:, t % 2, j * P:(j + 1) * P] for j in range(3)])
                    if kind == "U":
                        drained(pe, ("N", l, t))
                        if t == 0:
                            pe.wait_ge(proj_par_in, 96 * (l + 1))
                        if not cut:
                            b = begin(("UQ", l, t))
                            for j in (0, 1):
                                ins = mm(psum[:, b, 0:384], cqT[:, j, t * P:(t + 1) * P], uq[:, j, :], j == 0, j == 1)
                            end(ins, b)
                        b = begin(("UKV", l, t), takers=2)
                        end(mm(psum[:, b, :], cqT[:, 2, t * P:(t + 1) * P], ukv), b)
                    if kind == "TB":
                        pe.wait_ge(qkb_ready, 4 * l + t + 1)
                        kb = kbn[:, t % 2, :].rearrange("p (h d) -> p h d", h=4)
                        qb = qbn[:, t % 2, :].rearrange("p (h d) -> p h d", h=4)
                        if not cut:
                            transposes(("TBq", l, t), [qb[:, h, :] for h in range(4)], rows=QK_B)
                        transposes(("TBk", l, t), [kb[:, h, :] for h in range(4)], rows=QK_B)
                    if kind in ("TA", "TC"):
                        pe.wait_ge(qk_ready, 8 * l + t + 1 + 4 * (kind == "TC"))
                        q = qpad[:, t % 2, :].rearrange("p (h d) -> p h d", h=6)
                        if not cut:
                            transposes((kind + "q", l, t), [q[:, h, :] for h in range(4)])
                            transposes((kind + "r", l, t), [q[:, h, :] for h in (4, 5)] + [knat[:, t % 2, :]])
                        else:
                            transposes((kind + "r", l, t), [knat[:, t % 2, :]])

            def attention(l, s, step):
                nk = 2 if s == 0 else 4
                us = units(l, s)
                for i in range(len(us) + 5):
                    if i < len(us):
                        u, j, h, q = us[i]
                        br, head = PAIRS[j][0], PAIRS[j][1] + h
                        t = 2 * s + q
                        b = begin(("S", l, s, u))
                        if br == "B":
                            mm_in = qT["B"][0:QK_B, head, t * P:(t + 1) * P], kT["B"][0:QK_B, head, 0:nk * P]
                        else:
                            mm_in = qT[br][:, head, t * P:(t + 1) * P], kT[br][:, 0:nk * P]
                        if i == 0:
                            for tt in range(4):
                                drained(pe, ("TBk", l, tt))
                                drained(pe, ("TAr", l, tt))
                                drained(pe, ("TCr", l, tt))
                                if not (l == DEPTH - 1 and tt < 2):
                                    for name in ("TBq", "TAq", "TCq"):
                                        drained(pe, (name, l, tt))
                        end(mm(psum[:, b, 0:nk * P], *mm_in), b)
                    if l == 0:
                        ada_hook(step)
                    step += 1
                    if 3 <= i < len(us) + 3:
                        u = us[i - 3][0]
                        pe.wait_ge(prob_ready, unit_base(l, s) + u + 1)
                        transposes(("T", l, s, u), [prob[:, u % 4, k * P:(k + 1) * P] for k in range(nk)])
                    if i >= 5 and us[i - 5][0] % 4 == 3:
                        u, j, _, _ = us[i - 5]
                        for v in range(u - 3, u + 1):
                            drained(pe, ("T", l, s, v))
                        b = begin(("O", l, s, j))
                        br, h0 = PAIRS[j]
                        for k in range(nk):
                            for h in (0, 1):
                                col = HD * (h0 + h if br == "B" else (h0 + h) // 3)
                                p = pT[:, (2 * j + h) % 3, :].rearrange("p (k q) -> p k q", q=256)
                                ins = mm(psum[HD * h:HD * h + HD, b, 0:256], V[br][:, k, col:col + HD], p[:, k, :],
                                         k == 0, k == nk - 1)
                        end(ins, b)
                return step

            def mm3(o, a_hi, a_lo, b_hi, b_lo, first, last):
                mm(o, a_hi, b_hi, first, False)
                mm(o, a_hi, b_lo, False, False)
                return mm(o, a_lo, b_hi, False, last)

            def gates(l):
                ts = tiles(l)
                base = split_base(l)
                h_split, o_split = {}, {}
                ready = [0]

                def need(number):
                    if number > ready[0]:
                        ready[0] = number
                        pe.wait_ge(split_low, base + number)

                sets = [(n, br) for n in (0, 1) for br in range(3)]

                def gate_pieces(n, br):
                    at = GATE_COL + br * D + n * 512
                    return [split_piece(l, [w_in[l, 512 * h:512 * h + 512, at:at + 512]], 4, 512) for h in (0, 1)]

                for n, br in sets:
                    lo_k, hi_k = BRANCH_TILES[br]
                    if (n, br) == (0, 0):
                        h_split[ts[0]] = split_rows(l, hT, h_hi, h_lo, ts[0])
                        at = GATE_COL
                        wg = [split_piece(l, [w_in[l, 0:512, at:at + 512]], 4, 512)]
                        for t in ts[1:]:
                            h_split[t] = split_rows(l, hT, h_hi, h_lo, t)
                        wg.append(split_piece(l, [w_in[l, 512:1024, at:at + 512]], 4, 512))
                    else:
                        wg = gate_pieces(n, br)
                    wb = split_piece(l, [w_branch[l, lo_k * P:hi_k * P, n * 512:n * 512 + 512]], hi_k - lo_k, 512)
                    if (n, br) == (0, 0):
                        for t in ts:
                            o_split[t] = split_rows(l, oT, o_hi, o_lo, t)
                    banks = {}
                    for h in (0, 1):
                        number, m, w_hi, w_lo = wg[h]
                        for t in ts:
                            cols = slice(t * P, (t + 1) * P)
                            if h == 0:
                                banks[t] = (begin(("G", l, n, br, t)), )
                            need(number)
                            need(h_split[t])
                            b = banks[t][0]
                            for k in range(4 * h, 4 * h + 4):
                                ins = mm3(psum[:, b, :], h_hi[:, k, cols], h_lo[:, k, cols], w_hi[:, k % 4, :],
                                          w_lo[:, k % 4, :], k == 0, k == KT - 1)
                            if h == 1:
                                event = end(ins, b)
                        if h == 0:
                            free(m, ins)
                            freed[m + 1] = freed[m]
                        else:
                            freed[m] = freed[m + 1] = event
                    number, m, w_hi, w_lo = wb
                    for t in ts:
                        cols = slice(t * P, (t + 1) * P)
                        b = begin(("BR", l, n, br, t))
                        need(number)
                        need(o_split[t])
                        for k in range(lo_k, hi_k):
                            ins = mm3(psum[:, b, :], o_hi[:, k, cols], o_lo[:, k, cols], w_hi[:, k - lo_k, :],
                                      w_lo[:, k - lo_k, :], k == lo_k, k == hi_k - 1)
                        event = end(ins, b)
                    freed[m] = freed[m + 1] = event
                gates_done[l] = event

            def project_and_route(l):
                ts = tiles(l)
                wo = None
                for i in range(len(ts) + 3):
                    if i < len(ts):
                        t = ts[i]
                        pe.wait_ge(merged_ready, first_tile(l) + i + 1)
                        for j in (0, 1):
                            transposes(("M", l, t, j),
                                       [merged[:, t, k * P:(k + 1) * P] for k in range(4 * j, 4 * j + 4)])
                    if 1 <= i <= len(ts):
                        t = ts[i - 1]
                        if wo is None:
                            wo = [piece([w_out[l, 512 * h:512 * h + 512, 512 * n:512 * n + 512]], 4, 512)
                                  for n in (0, 1) for h in (0, 1)]
                        drained(pe, ("M", l, t, 0))
                        drained(pe, ("M", l, t, 1))
                        for n in (0, 1):
                            b = begin(("Y", l, t, n))
                            for k in range(KT):
                                ins = mm(psum[:, b, :], mT[:, k, t * P:(t + 1) * P], wo[2 * n + k // 4][1][:, k % 4, :],
                                         k == 0, k == KT - 1)
                            event = end(ins, b)
                        if i == len(ts):
                            for m, _ in wo:
                                free(m, event=event)
                    if 2 <= i <= len(ts) + 1:
                        pe.wait_ge(x_ready, 2 * first_tile(l) + i - 1)
                        x_transposes("h2T", l, ts[i - 2])
                    if i >= 3:
                        t = ts[i - 3]
                        drained(pe, ("h2T", l, t, 0))
                        drained(pe, ("h2T", l, t, 1))
                        if i == 3:
                            pe.wait_ge(router_in, 16 * (l + 1))
                        b = begin(("R", l, t))
                        for k in range(KT):
                            ins = mm(psum[:, b, 0:EXPERTS], hT[:, k, t * P:(t + 1) * P], wr[:, k, :], k == 0,
                                     k == KT - 1)
                        end(ins, b)

            def gather(l, quarter):
                for k in range(KT):
                    for s in streams(l):
                        b = begin(("XS", l, k, s, quarter))
                        for i in (0, 1):
                            ins = mm(psum[:, b, 0:P], X[:, 2 * s + i, k * P:(k + 1) * P],
                                     onehot[:, 2 * s + i, P * quarter:P * quarter + P], i == 0, i == 1)
                        end(ins, b)

            def choose(l):
                R = EXPERTS * len(streams(l))
                pe.wait_ge(aff_ready, l + 1)
                transposes(("AT", l), [affn[:, i, 0:R] for i in (0, 1)], rows=R)
                b = begin(("PT", l))
                pe.wait_ge(pos_ready, l + 1)
                for i in (0, 1):
                    ins = nc.tensor.transpose(psum[:, b, R * i:R * i + R], topT[0:R, 3, i * P:(i + 1) * P],
                                              ident[0:R, 0:R])
                end(ins, b)
                pe.wait_ge(onehot_ready, first_tile(l) + len(tiles(l)))
                gather(l, 0)

            def experts(l):
                M = CAP * len(streams(l))
                G = P // M
                Wd = D // G

                def into(e):
                    bg = begin(("HG", l, e))
                    bu = begin(("HU", l, e))
                    if e % 4 == 0:
                        for k in range(KT):
                            for s in streams(l):
                                drained(pe, ("XS", l, k, s, e // 4))
                    for kp in range(4):
                        for at, (b, w) in enumerate(((bg, w_gate), (bu, w_up))):
                            src = [w[l, e, kp * 256:kp * 256 + 256, :]]
                            if e == 0 and kp < 2:
                                n, v = None, early_piece(l, 2 * kp + at, src, 2, D)
                            else:
                                n, v = piece(src, 2, D)
                            for k in (2 * kp, 2 * kp + 1):
                                for g in range(G):
                                    ins = mm(psum[g * M:(g + 1) * M, b, 0:Wd], xsT[:, k, e * M:(e + 1) * M],
                                             v[:, k % 2, g * Wd:(g + 1) * Wd], k == 0, k == KT - 1)
                            if kp == 3:
                                free(n, event=end(ins, b))
                            elif n is not None:
                                free(n, ins)

                def turn_hidden(e):
                    pe.wait_ge(hid_ready, EXPERTS * l + e + 1)
                    transposes(("HT", l, e), [hid[:, e % 2, j * P:(j + 1) * P] for j in range(Wd // P)])

                def down(e):
                    drained(pe, ("HT", l, e))
                    b = begin(("YE", l, e))
                    for kp in range(4):
                        n, v = piece([w_down[l, e, kp * 256:kp * 256 + 256, :]], 2, D)
                        for k in (2 * kp, 2 * kp + 1):
                            q, j = k // (Wd // P), k % (Wd // P)
                            for g in range(G):
                                ins = mm(psum[g * M:(g + 1) * M, b, 0:Wd],
                                         hidT[:, e % 2, j * P + q * M:j * P + (q + 1) * M],
                                         v[:, k % 2, g * Wd:(g + 1) * Wd], k == 0, k == KT - 1)
                        if kp == 3:
                            free(n, event=end(ins, b))
                        else:
                            free(n, ins)

                def scatter(g):
                    if g == 0:
                        for t in tiles(l):
                            drained(pe, ("OT", l, t))
                    for half in y_moved:
                        pe.wait_ge(half, 64 * 2 * (4 * l + g + 1))
                    for t in tiles(l):
                        s, i = t // 2, t % 2
                        for n in (0, 1):
                            b = begin(("SC", l, g, t, n))
                            end(mm(psum[:, b, :], ohT[:, 4 * s + g, i * P:(i + 1) * P],
                                   YG[:, 2 * (g % 2) + s, 512 * n:512 * n + 512]), b)

                for e in range(EXPERTS + 1):
                    if e < EXPERTS:
                        into(e)
                    if e == 0:
                        pe.wait_ge(weighted_ready, first_tile(l) + len(tiles(l)))
                        for t in tiles(l):
                            transposes(("OT", l, t), [ohw[:, t, g * P:(g + 1) * P] for g in range(4)])
                    if 1 <= e <= 3:
                        gather(l, e)
                    if e >= 5 and e % 4 == 1:
                        scatter(e // 4 - 1)
                    if e >= 1:
                        down(e - 1)
                    if e < EXPERTS:
                        turn_hidden(e)
                scatter(3)

            pe.wait_ge(consts_in, 16)
            pe.wait_ge(c_in, 32)
            b = begin("c", bank=ADA_BANK)
            end(nc.tensor.transpose(psum[:, b, 0:2 * KT], cin[:, :], ident[0:2 * KT, 0:2 * KT]), b)
            pe.wait_ge(bias_in, 32)
            b = begin("bias", bank=TURN_BANK)
            end(nc.tensor.transpose(psum[:, b, 0:48 * DEPTH], bias_rows[:, :], ident[0:48 * DEPTH, 0:48 * DEPTH]), b)
            for k in range(KT):
                ada_products(0, 0, k)
            ada_turn(0, 0)
            step = QKV_TURNS
            for l in range(DEPTH):
                for t in range(4):
                    if l == 0:
                        if t == 0:
                            pe.wait_ge(x_in, 32)
                    else:
                        pe.wait_ge(x_ready, 2 * first_tile(l - 1) + len(tiles(l - 1)) + t + 1)
                    x_transposes("hT", l, t)
                qkv(l)
                for s in streams(l):
                    step = attention(l, s, step)
                gates(l)
                project_and_route(l)
                choose(l)
                experts(l)

        @block.sync
        def _(sp):
            for dst, src, n, after in stream:
                if after:
                    sp.wait_ge(*after)
                    sp.dma_start(dst, src[0].rearrange("(k p) n -> p k n", p=P)).then_inc(early_in[n], 16)
                    continue
                if n >= RING:
                    sp.wait_ge(*freed[n - RING])
                if not isinstance(src, list):
                    sp.dma_start(dst, src).then_inc(slot_filled[n % RING], 16)
                    continue
                if len(src) == 1:
                    sp.dma_start(dst, src[0].rearrange("(k p) n -> p k n", p=P)).then_inc(slot_filled[n % RING], 16)
                    continue
                at = 0
                for i, s in enumerate(src):
                    w = s.shape[1]
                    ins = sp.dma_start(dst[:, :, at:at + w], s.rearrange("(k p) n -> p k n", p=P))
                    if i == 0:
                        ins.then_inc(part_in, 16)
                        parts[0] += 16
                        sp.wait_ge(part_in, parts[0])
                    else:
                        ins.then_inc(slot_filled[n % RING], 16)
                    at += w
            sp.wait_ge(x_ready, 2 * first_tile(DEPTH))
            sp.dma_start(out.rearrange("b (t p) d -> p (b t) d", p=P), X[:, 2:4, :]).then_inc(out_stored, 16)
            sp.wait_ge(out_stored, 16)

        @block.gpsimd
        def _(pool):
            nc.gpsimd.memset(cs[:, :, :], 0.0).then_inc(zeros_set, 1)
            nc.gpsimd.memset(eps[:, 0:1], LN_EPS).then_inc(zeros_set, 1)
            nc.gpsimd.memset(eps[:, 1:2], RMS_EPS).then_inc(zeros_set, 1)
            pool.dma_start(X[:, 0:2, :], ctx_in.rearrange("b (t p) d -> p (b t) d", p=P)).then_inc(x_in, 16)
            pool.dma_start(X[:, 2:4, :], x.rearrange("b (t p) d -> p (b t) d", p=P)).then_inc(x_in, 16)

            def store_rows(l):
                drained(pool, ("adaR", l))
                pool.dma_start(mod_all[l].rearrange("s c p -> (s c) p"), mod_rows[:, :]).then_inc(mod_stored, 16)

            def row(ap):
                return ap.rearrange("(a n) -> a n", a=1).partition_broadcast(P)

            def norm_par(l, second):
                g, b = ((ln2_g, ln2_b) if second else (ln1_g, ln1_b))
                pool.dma_start(norm_g, row(g[l, :])).then_inc(norm_par_in, 16)
                pool.dma_start(norm_b, row(b[l, :])).then_inc(norm_par_in, 16)
                if not second:
                    for s in (0, 1):
                        pool.dma_start(gate_of[s], row(mod_all[l, s, 8 * G1:8 * G1 + 8, :].rearrange("c p -> (c p)"))) \
                            .then_inc(norm_par_in, 16)
                    return
                w = D * CAP * len(streams(l)) // P
                at = 0
                for n in range(D // w):
                    for s in streams(l):
                        cut = mod_all[l, s, 8 * G2:8 * G2 + 8, :].rearrange("c p -> (c p)")[n * w:(n + 1) * w]
                        pool.dma_start(gate_y[at:at + CAP, 0:w],
                                       cut.rearrange("(a n) -> a n", a=1).partition_broadcast(CAP)) \
                            .then_inc(norm_par_in, 16)
                        at += CAP

            for l in range(DEPTH):
                if l:
                    pool.wait_ge(x_ready, 2 * first_tile(l))
                    for t in tiles(l - 1):
                        for n in (0, 1):
                            filled(pool, ("SC", l - 1, 3, t, n))
                pool.dma_start(uq, b_w_uq[l].rearrange("(j p) n -> p j n", p=P)).then_inc(proj_par_in, 16)
                pool.dma_start(ukv, b_w_ukv[l]).then_inc(proj_par_in, 16)
                pool.dma_start(gain_cq[:, 0:256], row(b_q_norm[l, :])).then_inc(proj_par_in, 16)
                pool.dma_start(gain_cq[:, 256:384], row(b_kv_norm[l, :])).then_inc(proj_par_in, 16)
                pool.dma_start(part(PR, 1664, HD), row(c_q_norm[l, :])).then_inc(proj_par_in, 16)
                pool.dma_start(part(PR, 1728, HD), row(c_k_norm[l, :])).then_inc(proj_par_in, 16)
                pool.dma_start(sink[:, :], row(a_sink[l, :])).then_inc(sink_in, 16)
                pool.dma_start(wr[:, :, :], w_router[l].rearrange("(k p) e -> p k e", p=P)).then_inc(router_in, 16)
                nc.gpsimd.memset(qpad[:, :, :], 0.0).then_inc(pads_zero, 1)
                if l == 0:
                    store_rows(0)
                    store_rows(1)
                filled(pool, ("T", l, 1, 31))
                pool.wait_ge(mod_stored, 16 * DEPTH)
                norm_par(l, False)
                pool.wait_ge(x_ready, 2 * first_tile(l) + len(tiles(l)))
                norm_par(l, True)
                M = CAP * len(streams(l))
                Wd = D * M // P
                for e in range(EXPERTS):
                    g = e // 4
                    if e % 4 == 0 and g >= 2:
                        for t in tiles(l):
                            for n in (0, 1):
                                filled(pool, ("SC", l, g - 2, t, n))
                    pool.wait_ge(y_ready, EXPERTS * l + e + 1)
                    for n in range(P // M):
                        for i, s in enumerate(streams(l)):
                            at = n * M + i * CAP
                            pool.dma_start(YG[CAP * (e % 4):CAP * (e % 4) + CAP, 2 * (g % 2) + s,
                                              n * Wd:(n + 1) * Wd], ysb[at:at + CAP, e % 2, 0:Wd]) \
                                .then_inc(y_moved[e % 2], 16)

        @block.scalar
        def _(act):
            act.dma_start(cin[0:KT, :], c_ctx.rearrange("(k p) -> k p", p=P)).then_inc(c_in, 16)
            act.dma_start(cin[KT:2 * KT, :], c[0, :].rearrange("(k p) -> k p", p=P)).then_inc(c_in, 16)
            act.dma_start(cst[:, :], consts).then_inc(consts_in, 16)
            for l in range(DEPTH):
                act.dma_start(bias_rows[48 * l:48 * l + 48, :], b_ada[l, :].rearrange("(c p) -> c p", p=P)) \
                    .then_inc(bias_in, 16)
            steps = [0]

            def run(ins):
                steps[0] += 1
                ins.then_inc(act_step, 1)

            def settle():
                act.wait_ge(act_step, steps[0])

            act.wait_ge(zeros_set, 3)
            b = filled(act, "c")
            nc.scalar.activation(cs[:, :, 0:2], psum[:, b, 0:2 * KT].rearrange("p (s k) -> p k s", s=2), ACT.Silu) \
                .then_inc(bank_drained[b], 1)

            def ada_move(l, third):
                b = filled(act, ("ada", l, third))
                if (l, third) != (0, 0):
                    filled(act, ("adaT", *divmod(3 * l + third - 1, 3)))
                nc.scalar.copy(modrow[:, :], psum[:, b, :]).then_inc(bank_drained[b], 1)

            def ada_hook(step):
                due = ada_due.get(step, {})
                if "move" in due:
                    ada_move(*due["move"])
                if "rows" in due:
                    b = filled(act, ("adaR", due["rows"]))
                    if due["rows"]:
                        act.wait_ge(mod_stored, 16 * due["rows"])
                    nc.scalar.copy(mod_rows[:, :], psum[0:96, b, 0:P]).then_inc(bank_drained[b], 1)

            def modulated(name, l, t, scale, shift, halves=(0,)):
                s = t // 2
                for j in halves:
                    b = filled(act, (name, l, t, j))
                    for i in range(4):
                        k = 4 * j + i
                        ins = nc.scalar.activation(hT[:, k, t * P:(t + 1) * P], psum[:, b, i * P:(i + 1) * P],
                                                   ACT.Identity, scale=modcol[:, l, s, 8 * scale + k:8 * scale + k + 1],
                                                   bias=modcol[:, l, s, 8 * shift + k:8 * shift + k + 1])
                    ins.then_inc(bank_drained[b], 1)

            def qkv(l):
                turns = 0
                for step in QKV_STEPS:
                    kind, t = step[0], step[-1]
                    cut = l == DEPTH - 1 and t < 2
                    cols = slice(t * P, (t + 1) * P)
                    n = 8 * l + t
                    if kind == "P":
                        if l == 0 and turns:
                            ada_hook(turns - 1)
                        turns += 1
                    if kind == "P" and step[1] == 1:
                        b = filled(act, ("P", l, 1, t))
                        nc.scalar.copy(V["A"][:, t, :], psum[:, b, 0:P])
                        if n:
                            act.wait_ge(rms_taken, n if t else 8 * l)
                        run(nc.scalar.activation(sq[:, 0:256], psum[:, b, 128:384], ACT.Square,
                                                 accum_out=small[:, 0:1]))
                        settle()
                        nc.scalar.activation(sq[:, 0:128], psum[:, b, 384:512], ACT.Square,
                                             accum_out=small[:, 1:2]).then_inc(bank_drained[b], 1)
                        run(nc.scalar.activation(small[:, 2:3], small[:, 0:1], ACT.Sqrt, bias=eps[:, 1:2],
                                                 scale=1.0 / 256))
                        settle()
                        nc.scalar.activation(small[:, 3:4], small[:, 1:2], ACT.Sqrt, bias=eps[:, 1:2],
                                             scale=1.0 / 128).then_inc(root_ready, 1)
                    if kind == "P" and step[1] == 3:
                        b = filled(act, ("P", l, 3, t))
                        nc.scalar.copy(V["C"][:, t, :], psum[:, b, 32:160]).then_inc(bank_drained[b], 1)
                    if kind == "P" and step[1] == 2:
                        b = filled(act, ("P", l, 2, t))
                        lo = 384 if cut else 0
                        act.wait_ge(rms_taken, 8 * l + 4 + t)
                        nc.scalar.activation(sq[:, lo:512], psum[:, b, lo:512], ACT.Square) \
                            .then_inc(bank_drained[b], 1)
                        act.wait_ge(sumsq_ready, 4 * l + t + 1)
                        nc.scalar.activation(small[:, 12 + lo // 64:20], small[:, 4 + lo // 64:12], ACT.Sqrt,
                                             bias=eps[:, 1:2], scale=1.0 / HD).then_inc(root_ready, 1)
                    if kind == "N":
                        b = filled(act, ("N", l, t))
                        nc.scalar.copy(cqT[:, :, cols], psum[:, b, 0:384].rearrange("p (j q) -> p j q", j=3)) \
                            .then_inc(bank_drained[b], 1)
                    if kind == "U":
                        b = filled(act, ("UKV", l, t))
                        nc.scalar.copy(V["B"][:, t, :].rearrange("p (h d) -> p h d", h=4),
                                       psum[:, b, :].rearrange("p (h d) -> p h d", h=4)[:, :, HD:]) \
                            .then_inc(bank_drained[b], 1)
                    if kind == "TB":
                        for name, dst in ((("TBq", qT["B"]),) if not cut else ()) + (("TBk", kT["B"]),):
                            b = filled(act, (name, l, t))
                            nc.scalar.copy(dst[0:QK_B, :, cols], psum[0:QK_B, b, :].rearrange("p (h q) -> p h q", h=4)) \
                                .then_inc(bank_drained[b], 1)
                    if kind in ("TA", "TC"):
                        if not cut:
                            b = filled(act, (kind + "q", l, t))
                            nc.scalar.copy(qT[kind[1]][:, 0:4, cols], psum[:, b, :].rearrange("p (h q) -> p h q", h=4)) \
                                .then_inc(bank_drained[b], 1)
                            b = filled(act, (kind + "r", l, t))
                            nc.scalar.copy(qT[kind[1]][:, 4:6, cols],
                                           psum[:, b, 0:256].rearrange("p (h q) -> p h q", h=2))
                            nc.scalar.copy(kT[kind[1]][:, cols], psum[:, b, 256:384]).then_inc(bank_drained[b], 1)
                        else:
                            b = filled(act, (kind + "r", l, t))
                            nc.scalar.copy(kT[kind[1]][:, cols], psum[:, b, 0:P]).then_inc(bank_drained[b], 1)

            def attention(l, s, step):
                nk = 2 if s == 0 else 4
                us = units(l, s)
                for i in range(len(us) + 5):
                    if i < len(us):
                        u, j, h, q = us[i]
                        br, head = PAIRS[j][0], PAIRS[j][1] + h
                        b = filled(act, ("S", l, s, u))
                        act.wait_ge(max_ready, unit_base(l, s) + u + 1)
                        if u >= 4:
                            filled(act, ("T", l, s, u - 4))
                        c4 = 64 + 4 * (u % 4)
                        if br == "A":
                            nc.scalar.activation(small[:, c4 + 1:c4 + 2], sink[:, head:head + 1], ACT.Exp,
                                                 bias=small[:, c4:c4 + 1])
                        nc.scalar.activation(prob[:, u % 4, 0:nk * P], psum[:, b, 0:nk * P], ACT.Exp,
                                             bias=small[:, c4:c4 + 1], scale=SCALE_B if br == "B" else SCALE_AC,
                                             accum_out=small[:, c4 + 2:c4 + 3]).then_inc(bank_drained[b], 1)
                    if l == 0:
                        ada_hook(step)
                    step += 1
                    if 3 <= i < len(us) + 3:
                        u, j, h, q = us[i - 3]
                        b = filled(act, ("T", l, s, u))
                        hd = 2 * j + h
                        if hd >= 3:
                            filled(act, ("O", l, s, (hd - 3) // 2))
                        p = pT[:, hd % 3, :].rearrange("p (k q) -> p k q", q=256)
                        nc.scalar.copy(p[:, 0:nk, q * P:(q + 1) * P],
                                       psum[:, b, 0:nk * P].rearrange("p (k q) -> p k q", k=nk)) \
                            .then_inc(bank_drained[b], 1)
                    if i >= 5 and us[i - 5][0] % 4 == 3:
                        j = us[i - 5][1]
                        b = filled(act, ("O", l, s, j))
                        nc.scalar.copy(oT[:, j, 256 * s:256 * s + 256], psum[:, b, 0:256]) \
                            .then_inc(bank_drained[b], 1)
                return step

            def norm_root(n):
                act.wait_ge(var_ready, n)
                nc.scalar.activation(small[:, 43:44], small[:, 42:43], ACT.Sqrt, bias=eps[:, 0:1]) \
                    .then_inc(std_ready, 1)

            step = QKV_TURNS
            ada_move(0, 0)
            for l in range(DEPTH):
                n_gates = 6 * first_tile(l)
                for t in range(4):
                    if t == 0:
                        act.wait_ge(mod_cols, 1 if l == 0 else 6)
                    modulated("hT", l, t, SC1, SH1)
                qkv(l)
                if l == 0:
                    ada_hook(QKV_TURNS - 1)
                for s in streams(l):
                    step = attention(l, s, step)
                drained(act, ("O", l, 1, 7))

                def high(i):
                    src, hi, _, _, where = splits[l][i]
                    if where:
                        m, count = where
                        act.wait_ge(slot_filled[m % RING], count)
                        if m + 1 >= RING:
                            act.wait_ge(*freed[m + 1 - RING])
                    nc.scalar.copy(hi, src).then_inc(split_high, 1)

                for (before, after), (n, br) in zip(split_order(l), [(n, br) for n in (0, 1) for br in range(3)]):
                    for i in before:
                        high(i)
                    for t in tiles(l):
                        b = filled(act, ("G", l, n, br, t))
                        i = n_gates
                        n_gates += 1
                        if i >= 4:
                            act.wait_ge(gate_used, i - 3)
                        nc.scalar.activation(sg[:, i % 4, :], psum[:, b, :], ACT.Sigmoid) \
                            .then_inc(bank_drained[b], 1)
                    for i in after:
                        high(i)
                ts = tiles(l)
                for i in range(len(ts) + 3):
                    if i < len(ts):
                        for j in (0, 1):
                            b = filled(act, ("M", l, ts[i], j))
                            nc.scalar.copy(mT[:, 4 * j:4 * j + 4, ts[i] * P:(ts[i] + 1) * P],
                                           psum[:, b, :].rearrange("p (k q) -> p k q", k=4)) \
                                .then_inc(bank_drained[b], 1)
                    if 2 <= i <= len(ts) + 1:
                        if i == 2:
                            act.wait_ge(mod_cols, 3 * (l + 1))
                        modulated("h2T", l, ts[i - 2], SC2, SH2, (0, 1) if i <= len(ts) else (0,))
                    if 1 <= i <= len(ts):
                        norm_root(2 * first_tile(l) + i)
                    if i >= 3:
                        t = ts[i - 3]
                        col = 16 * (t // 2 - streams(l)[0])
                        b = filled(act, ("R", l, t))
                        act.wait_ge(aff_max, first_tile(l) + i - 2)
                        nc.scalar.activation(affn[:, t % 2, col:col + 16], psum[:, b, 0:EXPERTS], ACT.Exp,
                                             bias=small[:, 44:45], accum_out=small[:, 45:46]) \
                            .then_inc(bank_drained[b], 1)
                M = CAP * len(streams(l))

                def gathered(quarter):
                    for k in range(KT):
                        for i, s in enumerate(streams(l)):
                            b = filled(act, ("XS", l, k, s, quarter))
                            dst = xsT[:, k, 4 * quarter * M:4 * quarter * M + 4 * M] \
                                .rearrange("p (e m) -> p e m", m=M)[:, :, CAP * i:CAP * i + CAP]
                            nc.scalar.activation(dst, psum[:, b, 0:P].rearrange("p (e m) -> p e m", m=CAP),
                                                 ACT.Identity, scale=modcol[:, l, s, 8 * SC2 + k:8 * SC2 + k + 1],
                                                 bias=modcol[:, l, s, 8 * SH2 + k:8 * SH2 + k + 1]) \
                                .then_inc(bank_drained[b], 1)

                gathered(0)
                Wd = D * M // P
                for e in range(EXPERTS):
                    b = filled(act, ("HG", l, e))
                    if e >= 2:
                        act.wait_ge(hid_ready, EXPERTS * l + e - 1)
                    nc.scalar.activation(sil[:, e % 2, 0:Wd], psum[:, b, 0:Wd], ACT.Silu).then_inc(bank_drained[b], 1)
                    if e == 0:
                        for t in tiles(l):
                            b = filled(act, ("OT", l, t))
                            nc.scalar.copy(ohT[:, 4 * (t // 2):4 * (t // 2) + 4, (t % 2) * P:(t % 2 + 1) * P],
                                           psum[:, b, :].rearrange("p (g q) -> p g q", g=4)).then_inc(bank_drained[b], 1)
                    if 1 <= e <= 3:
                        gathered(e)
                    b = filled(act, ("HT", l, e))
                    if e >= 2:
                        filled(act, ("YE", l, e - 2))
                    nc.scalar.copy(hidT[:, e % 2, 0:Wd], psum[:, b, 0:Wd]).then_inc(bank_drained[b], 1)
                for i in range(len(ts)):
                    norm_root(2 * first_tile(l) + len(ts) + i + 1)

        @block.vector
        def _(dve):
            steps = [0]
            V_ = nc.vector

            def run(ins):
                steps[0] += 1
                ins.then_inc(dve_step, 1)
                dve.wait_ge(dve_step, steps[0])

            def mark(sem):
                V_.engine_nop().then_inc(sem, 1)

            def ada_columns(l, third):
                b = filled(dve, ("adaT", l, third))
                src = psum[:, b, :].rearrange("p (j g r) -> p g j r", j=4, g=4)
                bias = bias_cols[:, 48 * l + 16 * third:48 * l + 16 * third + 16].rearrange("p (g j) -> p g j", g=4)
                dst = modcol[:, l, :, 16 * third:16 * third + 16]
                for s in (0, 1):
                    ins = V_.tensor_tensor(dst[:, s, :].rearrange("p (g j) -> p g j", g=4), src[:, :, :, s], bias,
                                           ALU.add)
                run(ins)
                mark(bank_drained[b])
                if third != 1:
                    at = 8 if third == 0 else 0
                    run(V_.tensor_scalar(dst[:, :, at:at + 8], dst[:, :, at:at + 8], 1.0, None, ALU.add))
                mark(mod_cols)

            def ada_hook(step):
                due = ada_due.get(step, {})
                if "turn" in due:
                    ada_columns(*due["turn"])

            def modulated(name, l, t, scale, shift):
                s = t // 2
                b = filled(dve, (name, l, t, 1))
                for i in range(4):
                    k = 4 + i
                    ins = V_.tensor_scalar(hT[:, k, t * P:(t + 1) * P], psum[:, b, i * P:(i + 1) * P],
                                           modcol[:, l, s, 8 * scale + k:8 * scale + k + 1],
                                           modcol[:, l, s, 8 * shift + k:8 * shift + k + 1], ALU.mult, ALU.add)
                ins.then_inc(bank_drained[b], 1)

            def rope(t, xin, outs, h, half):
                at = C_ROPE + 192 * (t - 2) + (0 if half == 16 else 128)
                w = 4 * half
                cos = cst[:, at:at + w]
                sin = cst[:, at + w:at + 2 * w]
                x3 = xin.rearrange("p (h d) -> p h d", d=w)
                V_.tensor_tensor(m1[:, 0:h * w].rearrange("p (h d) -> p h d", d=w), x3,
                                 cos.unsqueeze(1).to_broadcast([P, h, w]), ALU.mult)
                x5 = xin.rearrange("p (h a z d) -> p h a z d", a=2, z=2, d=half)
                o5 = m2[:, 0:h * w].rearrange("p (h a z d) -> p h a z d", a=2, z=2, d=half)
                s4 = sin.rearrange("p (a z d) -> p a z d", a=2, z=2)
                for z in (0, 1):
                    ins = V_.tensor_tensor(o5[:, :, :, z, :], x5[:, :, :, 1 - z, :],
                                           s4[:, :, z, :].unsqueeze(1).to_broadcast([P, h, 2, half]), ALU.mult)
                    if z == 0:
                        continue
                    run(ins)
                for o, view in outs[:-1]:
                    V_.tensor_tensor(o, view(m1), view(m2), ALU.add)
                o, view = outs[-1]
                run(V_.tensor_tensor(o, view(m1), view(m2), ALU.add))

            def pad_view(i, g):
                return qpad[:, i, 384 * g:384 * g + 384].rearrange("p (r d) -> p r d", r=3)[:, :, HD * g:HD * g + HD]

            def third(v, g):
                return v[:, 192 * g:192 * g + 192].rearrange("p (r d) -> p r d", r=3)

            def heads_out(i, cut):
                outs = [] if cut else [(pad_view(i, 0), lambda v: third(v, 0)), (pad_view(i, 1), lambda v: third(v, 1))]
                return outs + [(knat[:, i, :], lambda v: v[:, 384:512])]

            def qkv(l):
                turns = 0
                for step in QKV_STEPS:
                    kind, t = step[0], step[-1]
                    cut = l == DEPTH - 1 and t < 2
                    i = t % 2
                    if kind == "P":
                        if l == 0 and turns:
                            ada_hook(turns - 1)
                        turns += 1
                    if kind == "P" and step[1] == 1:
                        b = filled(dve, ("P", l, 1, t))
                        if t == 0:
                            dve.wait_ge(proj_par_in, 96 * (l + 1))
                        dve.wait_ge(root_ready, 8 * l + t + 1)
                        if l or t:
                            dve.wait_ge(cqn_ready, 4 * l + t)
                        run(V_.reciprocal(small[:, 20:22], small[:, 2:4]))
                        if t >= 2:
                            filled(dve, ("N", l, t - 2))
                        V_.scalar_tensor_tensor(cqn[:, i, 0:256], psum[:, b, 128:384], small[:, 20:21],
                                                gain_cq[:, 0:256], ALU.mult, ALU.mult).then_inc(rms_taken, 1)
                        V_.scalar_tensor_tensor(cqn[:, i, 256:384], psum[:, b, 384:512], small[:, 21:22],
                                                gain_cq[:, 256:384], ALU.mult, ALU.mult).then_inc(cqn_ready, 1)
                        mark(bank_drained[b])
                    if kind == "P" and step[1] == 3:
                        b = second(dve, ("P", l, 3, t))
                        if t < 2:
                            V_.tensor_copy(krr[:, t, :], psum[:, b, 0:ROPE_B]).then_inc(bank_drained[b], 1)
                        else:
                            rope(t, psum[:, b, 0:ROPE_B], [(krr[:, t, :], lambda v: v[:, 0:ROPE_B])], 1, 8)
                            mark(bank_drained[b])
                    if kind == "U":
                        qb = qbn[:, i, :].rearrange("p (h d) -> p h d", h=4)
                        kb = kbn[:, i, :].rearrange("p (h d) -> p h d", h=4)
                        if t >= 2:
                            filled(dve, ("TBk", l, t - 2))
                        if not cut:
                            b = filled(dve, ("UQ", l, t))
                            src = psum[:, b, 0:384].rearrange("p (h d) -> p h d", h=4)
                            if t < 2:
                                V_.tensor_copy(qb, src).then_inc(bank_drained[b], 1)
                            else:
                                V_.tensor_copy(qb[:, :, 0:HD], src[:, :, 0:HD])
                                run(V_.tensor_copy(xg[:, 0:128].rearrange("p (h d) -> p h d", h=4), src[:, :, HD:]))
                                rope(t, xg[:, 0:128], [(qb[:, :, HD:], lambda v: v[:, 0:128].rearrange(
                                    "p (h d) -> p h d", h=4))], 4, 8)
                                mark(bank_drained[b])
                        b = second(dve, ("UKV", l, t))
                        V_.tensor_copy(kb[:, :, 0:HD],
                                       psum[:, b, :].rearrange("p (h d) -> p h d", h=4)[:, :, 0:HD]) \
                            .then_inc(bank_drained[b], 1)
                        drained(dve, ("P", l, 3, t))
                        V_.tensor_copy(kb[:, :, HD:], krr[:, t, :].unsqueeze(1).to_broadcast([P, 4, ROPE_B])) \
                            .then_inc(qkb_ready, 1)
                    if kind == "P" and step[1] == 0:
                        b = filled(dve, ("P", l, 0, t))
                        if t == 0:
                            dve.wait_ge(pads_zero, l + 1)
                        if t >= 2:
                            filled(dve, ("TAr", l, t - 2))
                        if t < 2:
                            for o, view in heads_out(i, cut):
                                V_.tensor_copy(o, view(psum[:, b, :]))
                        else:
                            rope(t, psum[:, b, :], heads_out(i, cut), 8, 16)
                        mark(bank_drained[b])
                        mark(qk_ready)
                    if kind == "P" and step[1] == 2:
                        b = filled(dve, ("P", l, 2, t))
                        h0 = 6 if cut else 0
                        second(dve, ("P", l, 2, t))
                        V_.tensor_reduce(small[:, 4 + h0:12],
                                         sq[:, 64 * h0:512].rearrange("p (h d) -> p h d", d=HD), AX, ALU.add) \
                            .then_inc(sumsq_ready, 1)
                        dve.wait_ge(root_ready, 8 * l + 4 + t + 1)
                        run(V_.reciprocal(small[:, 32 + h0:40], small[:, 12 + h0:20]))
                        nh = 8 - h0
                        run(V_.tensor_tensor(xg[:, 64 * h0:512].rearrange("p (h d) -> p h d", d=HD),
                                             psum[:, b, 64 * h0:512].rearrange("p (h d) -> p h d", d=HD),
                                             small[:, 32 + h0:40].unsqueeze(2).to_broadcast([P, nh, HD]), ALU.mult))
                        mark(bank_drained[b])
                        mark(rms_taken)
                        filled(dve, ("TAr", l, t + 2) if t < 2 else ("TCr", l, t - 2))
                        g6 = gain_q.unsqueeze(1).to_broadcast([P, 6, HD])
                        g2 = gain_k.unsqueeze(1).to_broadcast([P, 2, HD])
                        k2 = xg[:, 384:512].rearrange("p (h d) -> p h d", d=HD)
                        if t < 2:
                            if not cut:
                                for g in (0, 1):
                                    V_.tensor_tensor(pad_view(i, g), third(xg, g),
                                                     gain_q.unsqueeze(1).to_broadcast([P, 3, HD]), ALU.mult)
                            V_.tensor_tensor(knat[:, i, :].rearrange("p (h d) -> p h d", d=HD), k2, g2, ALU.mult) \
                                .then_inc(qk_ready, 1)
                        else:
                            q6 = xg[:, 0:384].rearrange("p (h d) -> p h d", d=HD)
                            V_.tensor_tensor(q6, q6, g6, ALU.mult)
                            run(V_.tensor_tensor(k2, k2, g2, ALU.mult))
                            rope(t, xg, heads_out(i, cut), 8, 16)
                            mark(qk_ready)

            def attention(l, s, step):
                nk = 2 if s == 0 else 4
                us = units(l, s)
                for i in range(len(us) + 5):
                    if i < len(us):
                        u, j, h, q = us[i]
                        br, head = PAIRS[j][0], PAIRS[j][1] + h
                        b = filled(dve, ("S", l, s, u))
                        c4 = 64 + 4 * (u % 4)
                        if br == "A" and s == 1:
                            run(V_.tensor_tensor(psum[:, b, 256:512], psum[:, b, 256:512],
                                                 cst[:, C_MASK + 256 * q:C_MASK + 256 * q + 256], ALU.add))
                        run(V_.tensor_reduce(small[:, c4 + 3:c4 + 4], psum[:, b, 0:nk * P], AX, ALU.max, negate=True))
                        if br == "A":
                            V_.tensor_scalar(small[:, c4:c4 + 1], small[:, c4 + 3:c4 + 4], SCALE_AC,
                                             nsink[:, head:head + 1], ALU.mult, ALU.min).then_inc(max_ready, 1)
                        else:
                            V_.tensor_scalar(small[:, c4:c4 + 1], small[:, c4 + 3:c4 + 4],
                                             SCALE_B if br == "B" else SCALE_AC, None, ALU.mult) \
                                .then_inc(max_ready, 1)
                    if l == 0:
                        ada_hook(step)
                    step += 1
                    if 1 <= i < len(us) + 1:
                        u, j, h, q = us[i - 1]
                        c4 = 64 + 4 * (u % 4)
                        drained(dve, ("S", l, s, u))
                        if PAIRS[j][0] == "A":
                            run(V_.tensor_tensor(small[:, c4 + 2:c4 + 3], small[:, c4 + 2:c4 + 3],
                                                 small[:, c4 + 1:c4 + 2], ALU.add))
                        run(V_.reciprocal(small[:, c4 + 2:c4 + 3], small[:, c4 + 2:c4 + 3]))
                        V_.tensor_scalar(prob[:, u % 4, 0:nk * P], prob[:, u % 4, 0:nk * P],
                                         small[:, c4 + 2:c4 + 3], None, ALU.mult).then_inc(prob_ready, 1)
                return step

            def layer_norm(l, t, n, xt):
                V_.bn_stats(stats[:, 0, :], xt[:, 0:512])
                run(V_.bn_stats(stats[:, 1, :], xt[:, 512:1024]))
                if n:
                    dve.wait_ge(std_ready, n)
                V_.bn_aggr(small[:, 41:43], stats[:, :, :].rearrange("p a b -> p (a b)")).then_inc(var_ready, 1)
                dve.wait_ge(std_ready, n + 1)
                run(V_.reciprocal(small[:, 46:47], small[:, 43:44]))
                run(V_.scalar_tensor_tensor(xt, xt, small[:, 41:42], norm_g, ALU.subtract, ALU.mult))
                run(V_.scalar_tensor_tensor(X[:, t, :], xt, small[:, 46:47], norm_b, ALU.mult, ALU.add))
                mark(x_ready)

            def project(l, i):
                    t = tiles(l)[i]
                    if i == 0:
                        dve.wait_ge(norm_par_in, 160 * l + 64)
                    lt = ln_t[:, i % 2, :]
                    for n in (0, 1):
                        b = filled(dve, ("Y", l, t, n))
                        ins = V_.tensor_tensor(lt[:, 512 * n:512 * n + 512], psum[:, b, :],
                                               gate_of[t // 2][:, 512 * n:512 * n + 512], ALU.mult)
                        ins.then_inc(bank_drained[b], 1)
                    drained(dve, ("Y", l, t, 1))
                    run(V_.scalar_tensor_tensor(lt, X[:, t, :], ALPHA, lt, ALU.mult, ALU.add))
                    layer_norm(l, t, 2 * first_tile(l) + i, lt)

            def affinity(l, i):
                t = tiles(l)[i]
                b = filled(dve, ("R", l, t))
                V_.tensor_reduce(small[:, 44:45], psum[:, b, 0:EXPERTS], AX, ALU.max, negate=True) \
                    .then_inc(aff_max, 1)
                drained(dve, ("R", l, t))
                run(V_.reciprocal(small[:, 45:46], small[:, 45:46]))
                a = affn[:, t % 2, 16 * (t // 2 - streams(l)[0]):16 * (t // 2 - streams(l)[0]) + 16]
                run(V_.tensor_scalar(a, a, small[:, 45:46], None, ALU.mult))

            def route(l):
                S0 = streams(l)[0]
                R = EXPERTS * len(streams(l))
                for i in range(len(tiles(l)) + 3):
                    if 1 <= i <= len(tiles(l)):
                        project(l, i - 1)
                    if i == len(tiles(l)) + 1:
                        modulated("h2T", l, tiles(l)[-1], SC2, SH2)
                    if i >= 3:
                        affinity(l, i - 3)
                mark(aff_ready)
                run(V_.memset(ones[0:R, :], 1.0))
                b = filled(dve, ("AT", l))
                run(V_.tensor_copy(topT[0:R, 0, :], psum[0:R, b, 0:256]))
                mark(bank_drained[b])
                for r in range(CAP // 8):
                    run(V_.max(max8[0:R, :], topT[0:R, r % 2, :]))
                    run(V_.match_replace(topT[0:R, (r + 1) % 2, :], max8[0:R, :], topT[0:R, r % 2, :], -1.0))
                run(V_.tensor_scalar(topT[0:R, 2, :], topT[0:R, 0, :], 0.0, None, ALU.is_lt))
                run(V_.tensor_tensor_scan(topT[0:R, 3, :], ones[0:R, :], topT[0:R, 2, :], 0.0, ALU.mult, ALU.add))
                V_.tensor_tensor(topT[0:R, 3, :], topT[0:R, 3, :], topT[0:R, 2, :], ALU.mult).then_inc(pos_ready, 1)
                b = filled(dve, ("PT", l))
                run(V_.tensor_copy(posn[:, :, 0:R], psum[:, b, 0:2 * R].rearrange("p (i r) -> p i r", i=2)))
                mark(bank_drained[b])
                for t in tiles(l):
                    col = 16 * (t // 2 - S0)
                    V_.tensor_tensor(onehot[:, t, :].rearrange("p (e m) -> p e m", m=CAP),
                                     iota1.unsqueeze(1).to_broadcast([P, EXPERTS, CAP]),
                                     posn[:, t % 2, col:col + 16].unsqueeze(2).to_broadcast([P, EXPERTS, CAP]),
                                     ALU.is_equal).then_inc(onehot_ready, 1)
                dve.wait_ge(onehot_ready, first_tile(l) + len(tiles(l)))
                for t in tiles(l):
                    col = 16 * (t // 2 - S0)
                    V_.tensor_tensor(ohw[:, t, :].rearrange("p (e m) -> p e m", m=CAP),
                                     onehot[:, t, :].rearrange("p (e m) -> p e m", m=CAP),
                                     affn[:, t % 2, col:col + 16].unsqueeze(2).to_broadcast([P, EXPERTS, CAP]),
                                     ALU.mult).then_inc(weighted_ready, 1)

            def experts(l):
                M = CAP * len(streams(l))
                Wd = D * M // P
                dve.wait_ge(norm_par_in, 160 * l + 160)

                def scatter(g):
                    for i, t in enumerate(tiles(l)):
                        for n in (0, 1):
                            b = filled(dve, ("SC", l, g, t, n))
                            cols = slice(512 * n, 512 * n + 512)
                            V_.tensor_tensor(X[:, t, cols], X[:, t, cols], psum[:, b, :], ALU.add) \
                                .then_inc(bank_drained[b], 1)
                        drained(dve, ("SC", l, g, t, 1))
                        if g == 3:
                            layer_norm(l, t, 2 * first_tile(l) + len(tiles(l)) + i, X[:, t, :])

                for e in range(EXPERTS + 1):
                    if e < EXPERTS:
                        b = filled(dve, ("HU", l, e))
                        drained(dve, ("HG", l, e))
                        if e >= 2:
                            filled(dve, ("HT", l, e - 2))
                        V_.tensor_tensor(hid[:, e % 2, 0:Wd], sil[:, e % 2, 0:Wd], psum[:, b, 0:Wd], ALU.mult) \
                            .then_inc(hid_ready, 1)
                        mark(bank_drained[b])
                    if e == 4:
                        for s in streams(l):
                            filled(dve, ("XS", l, KT - 1, s, 3))
                        for t in tiles(l):
                            run(V_.tensor_scalar(X[:, t, :], X[:, t, :], ALPHA, None, ALU.mult))
                    if e >= 5 and e % 4 == 1:
                        scatter(e // 4 - 1)
                    if e >= 1:
                        b = filled(dve, ("YE", l, e - 1))
                        if e >= 3:
                            dve.wait_ge(y_moved[(e - 1) % 2], 64 * (EXPERTS * l // 2 + (e - 1) // 2))
                        V_.tensor_tensor(ysb[:, (e - 1) % 2, 0:Wd], psum[:, b, 0:Wd], gate_y[:, 0:Wd], ALU.mult) \
                            .then_inc(y_ready, 1)
                        mark(bank_drained[b])
                scatter(3)

            dve.wait_ge(consts_in, 16)
            b = filled(dve, "bias")
            V_.tensor_copy(bias_cols[:, :], psum[:, b, 0:48 * DEPTH]).then_inc(bank_drained[b], 1)
            drained(dve, "bias")
            ada_columns(0, 0)
            step = QKV_TURNS
            for l in range(DEPTH):
                dve.wait_ge(sink_in, 16 * (l + 1))
                run(V_.tensor_scalar(nsink[:, :], sink[:, :], -1.0, None, ALU.mult))
                for t in range(4):
                    modulated("hT", l, t, SC1, SH1)
                qkv(l)
                if l == 0:
                    ada_hook(QKV_TURNS - 1)
                for s in streams(l):
                    step = attention(l, s, step)
                n_gates = 6 * first_tile(l)

                def low(i):
                    src, _, lo, hi_read, _ = splits[l][i]
                    dve.wait_ge(split_high, split_base(l) + i + 1)
                    V_.tensor_tensor(lo, src, hi_read, ALU.subtract).then_inc(split_low, 1)

                for (before, after), (n, br) in zip(split_order(l), [(n, br) for n in (0, 1) for br in range(3)]):
                    for i in before:
                        low(i)
                    for t in tiles(l):
                        b = filled(dve, ("BR", l, n, br, t))
                        drained(dve, ("G", l, n, br, t))
                        i = n_gates
                        n_gates += 1
                        dst = merged[:, t, 512 * n:512 * n + 512]
                        V_.tensor_tensor(dst if br == 0 else gtmp, sg[:, i % 4, :], psum[:, b, :], ALU.mult) \
                            .then_inc(gate_used, 1)
                        mark(bank_drained[b])
                        if br:
                            dve.wait_ge(gate_used, i + 1)
                            run(V_.tensor_tensor(dst, dst, gtmp, ALU.add))
                            if br == 2 and n == 1:
                                mark(merged_ready)
                    for i in after:
                        low(i)
                route(l)
                experts(l)


_INS = ["x", "c", "ctx", "c_ctx", "w_ada", "b_ada", "w_in", "a_sink", "b_q_norm", "b_kv_norm", "b_w_uq", "b_w_ukv",
        "c_q_norm", "c_k_norm", "w_branch", "w_out", "ln1_g", "ln1_b", "w_router", "w_gate", "w_up", "w_down",
        "ln2_g", "ln2_b"]


def tables():
    import numpy as np
    grid_w, window = 64, 128
    t = np.zeros((P, C_ALL), np.float32)
    t[:, C_ID:C_ID + P] = np.eye(P)
    for q in (0, 1):
        pos = q * P + np.arange(P)
        far = np.abs(pos[:, None] - np.arange(256)[None, :]) > window
        t[:, C_MASK + 256 * q:C_MASK + 256 * q + 256] = np.where(far, -1e30, 0.0)
        at = C_ROPE + 192 * q
        for half in (16, 8):
            freqs = (np.float32(10000.0) ** (-np.arange(half, dtype=np.float32) / half)).astype(np.float32)
            for axis, p in enumerate((pos // grid_w, pos % grid_w)):
                ang = p.astype(np.float32)[:, None] * freqs
                a = at + 2 * half * axis
                t[:, a:a + 2 * half] = np.concatenate([np.cos(ang), np.cos(ang)], 1)
                t[:, a + 4 * half:a + 6 * half] = np.concatenate([-np.sin(ang), np.sin(ang)], 1)
            at += 8 * half
    t[:, C_IOTA:C_IOTA + CAP] = 1 + np.arange(CAP)
    return t


def kernel(**inputs):
    import numpy as np
    import concourse.bacc as bacc
    from concourse.bass_utils import run_bass_kernel_spmd

    nc = bacc.Bacc("TRN2", target_bir_lowering=False, num_devices=1)
    arrays, args = {}, []
    for name in _INS:
        a = np.ascontiguousarray(inputs[name])
        arrays[f"in_{name}"] = a
        args.append(nc.dram_tensor(f"in_{name}", a.shape, F32, kind="ExternalInput").ap())
    arrays["in_tables"] = tables()
    args.append(nc.dram_tensor("in_tables", (P, C_ALL), F32, kind="ExternalInput").ap())
    out = nc.dram_tensor("out", (1, 256, D), F32, kind="ExternalOutput").ap()
    trunk(nc, *args, out)
    r = run_bass_kernel_spmd(nc, [arrays], core_ids=[0])
    return r.results[0]["out"]
```

```python
import concourse.bass as bass
from concourse import mybir
from contextlib import ExitStack

F32 = mybir.dt.float32
F32R = mybir.dt.float32r
ALU = mybir.AluOpType
ACT = mybir.ActivationFunctionType
AX = mybir.AxisListType.X

P = 128
D = 1024
KT = D // P
DEPTH = 2
HD = 64
HEADS_A, HEADS_B = 6, 4
QK_B, ROPE_B = 96, 32
EXPERTS, CAP = 16, 32
ALPHA = (2 * DEPTH) ** 0.25
SCALE_AC, SCALE_B = HD ** -0.5, QK_B ** -0.5
LN_EPS, RMS_EPS = 1e-5, 1e-6
RING, SLOT = 8, 2048
ADA_BANK, TURN_BANK = 7, 6
GATE_COL = 1696
CHUNKS = {0: [(0, 512)], 1: [(512, 512)], 2: [(1056, 512)], 3: [(1024, 32), (1568, 128)]}
BRANCH_TILES = [(0, 3), (3, 5), (5, 8)]
SH1, SC1, G1, SH2, SC2, G2 = range(6)
C_ID, C_MASK, C_ROPE, C_IOTA, C_ALL = 0, 128, 640, 1024, 1056

QKV_STEPS = [("P", 1, 0), ("P", 1, 1), ("N", 0), ("P", 1, 2), ("N", 1), ("P", 1, 3), ("N", 2), ("P", 3, 0), ("N", 3),
             ("P", 3, 1), ("U", 0), ("P", 3, 2), ("U", 1), ("TB", 0), ("P", 3, 3), ("U", 2), ("TB", 1), ("P", 0, 0),
             ("U", 3), ("TB", 2), ("P", 0, 1), ("TB", 3), ("TA", 0), ("P", 0, 2), ("TA", 1), ("P", 0, 3), ("TA", 2),
             ("P", 2, 0), ("TA", 3), ("P", 2, 1), ("TC", 0), ("P", 2, 2), ("TC", 1), ("P", 2, 3), ("TC", 2)]
LAST_TURN, LAST_TURN_AT = [("TC", 3)], 2
PE_FIRST = [("H", 0), ("P", 1, 0), ("H", 1), ("P", 1, 1), ("H", 2), ("H", 3)]
ACT_FIRST = [("R", 0), ("H", 0), ("R", 1), ("R", 2), ("H", 1), ("R", 3), ("P", 1, 0), ("H", 2), ("H", 3), ("P", 1, 1)]
DVE_FIRST = [("H", 2), ("H", 3), ("P", 1, 0), ("P", 1, 1)]
QKV_NEXT = [("P", 1, 2), ("N", 0), ("P", 1, 3), ("N", 1)] + QKV_STEPS[6:]
EARLY_SPLITS = 2
EARLY_SPLITS_AT = (24, 28)
GATHERS = [(0, 4), (4, 8), (8, 12), (12, 16)]
H_EARLY = [("H", 0), ("H", 1)]
FIRST_STEPS = [("P", 1, 0), ("H", 2), ("P", 1, 1), ("H", 3)] + QKV_STEPS[2:]
PAIRS = [("A", 0), ("A", 2), ("A", 4), ("B", 0), ("B", 2), ("C", 0), ("C", 2), ("C", 4)]


def trunk(nc, x, c, ctx_in, c_ctx, w_ada, b_ada, w_in, a_sink, b_q_norm, b_kv_norm, b_w_uq, b_w_ukv, c_q_norm,
          c_k_norm, w_branch, w_out, ln1_g, ln1_b, w_router, w_gate, w_up, w_down, ln2_g, ln2_b, consts, out):
    es = ExitStack()
    with es:
        def sb(name, shape):
            return es.enter_context(nc.sbuf_tensor(name, shape, F32))

        def sem(name):
            return es.enter_context(nc.semaphore(name))

        arena = nc.sbuf_base + (-nc.sbuf_base) % 64
        sizes = {"ring": RING * SLOT, "X": 4 * D, "hT": KT * 512, "A": 13312, "B": 4096, "PR": 4096, "W": 4096}
        sb("arena", [P, sum(sizes.values()) + 16])
        place, at = {}, arena
        for name, n in sizes.items():
            place[name] = at
            at += 4 * n

        def fixed(name, shape, dtype=F32, where=None, skip=0):
            return nc.alloc_sbuf_tensor_at(name, shape, dtype, offset=place[where or name] + 4 * skip)

        ring = fixed("ring", [P, RING, SLOT])
        X = fixed("X", [P, 4, D])
        hT = fixed("hT", [P, KT, 512])
        A = fixed("A", [P, 13312])
        B = fixed("B", [P, 4096])
        PR = fixed("PR", [P, 4096])
        W = fixed("W", [P, 4096])
        ring_r = fixed("ring_r", [P, RING, SLOT], F32R, "ring")
        h_hi = fixed("h_hi", [P, KT, 512], F32R, "A", 4096)
        h_lo = fixed("h_lo", [P, KT, 512], F32R, "hT")
        o_hi = fixed("o_hi", [P, KT, 512], F32R, "A", 8192)
        o_lo = fixed("o_lo", [P, KT, 512], F32R, "B")
        cst = sb("cst", [P, C_ALL])
        cs = sb("cs", [P, KT, 32])
        modrow = sb("modrow", [P, 512])
        bias_cols = sb("bias_cols", [P, 48 * DEPTH])
        modcol = sb("modcol", [P, DEPTH, 2, 48])
        mod_rows = sb("mod_rows", [96, P])
        wr = sb("wr", [P, KT, EXPERTS])
        sink = sb("sink", [P, HEADS_A])
        nsink = sb("nsink", [P, HEADS_A])
        eps = sb("eps", [P, 2])
        krr = sb("krr", [P, 4, ROPE_B])
        small = sb("small", [P, 96])
        stats = sb("stats", [P, 2, 6])
        affn = sb("affn", [P, 2, 32])
        posn = sb("posn", [P, 2, 32])
        max8 = sb("max8", [32, 8])
        psum = es.enter_context(nc.psum_tensor("psum", [P, 8, 512], F32))
        mod_all = nc.dram_tensor("mod_all", (DEPTH, 2, 48, P), F32).ap()

        def part(t, at, *shape):
            n = 1
            for s in shape:
                n *= s
            v = t[:, at:at + n]
            if len(shape) == 2:
                v = v.rearrange("p (a b) -> p a b", b=shape[1])
            if len(shape) == 3:
                v = v.rearrange("p (a b c) -> p a b c", b=shape[1], c=shape[2])
            return v

        ident = cst[:, C_ID:C_ID + P]
        iota1 = cst[:, C_IOTA:C_IOTA + CAP]
        qT = {"A": part(A, 0, 6, 512), "C": part(A, 3072, 6, 512), "B": part(A, 6144, 4, 512)}
        kT = {"A": part(A, 8192, 512), "C": part(A, 8704, 512), "B": part(A, 9216, 4, 512)}
        V = {"A": part(A, 11264, 4, P), "C": part(A, 11776, 4, P), "B": part(A, 12288, 4, 256)}
        merged = part(A, 0, 4, D)
        mT = part(A, 4096, KT, 512)
        xsT = part(A, 0, KT, 1024)
        sil = part(A, 8192, 2, 512)
        hid = part(A, 9216, 2, 512)
        hidT = part(A, 10240, 2, 512)
        ysb = part(A, 11264, 2, 512)
        qpad = part(B, 0, 2, 768)
        knat = part(B, 1536, 2, P)
        cqn = part(B, 1792, 2, 384)
        qbn = part(B, 2560, 2, 384)
        kbn = part(B, 3328, 2, 384)
        oT = part(B, 0, KT, 512)
        YG = part(B, 0, 4, D)
        uq = part(PR, 0, 2, 384)
        ukv = part(PR, 768, 512)
        gain_cq = part(PR, 1280, 384)
        gain_q = part(PR, 1664, HD)
        gain_k = part(PR, 1728, HD)
        bias_rows, cin = part(PR, 3584, P)[0:48 * DEPTH, :], part(PR, 3712, P)[0:2 * KT, :]
        norm_g, norm_b = part(PR, 0, D), part(PR, D, D)
        gate_of = {0: part(PR, 2048, D), 1: part(PR, 3072, D)}
        gate_y = part(PR, 2048, 512)
        m1, m2, sq, xg = (part(W, 512 * i, 512) for i in range(4))
        cqT = part(W, 2048, 3, 512)
        prob = part(PR, 0, 4, 512)
        pT = part(W, 0, 3, 1024)
        sg = part(W, 0, 4, 512)
        gtmp = part(W, 2048, 512)
        ln_t = part(W, 0, 2, D)
        onehot = part(W, 0, 4, 512)
        ones = part(W, 2560, 256)
        topT = part(W, 3072, 4, 256)
        ohw = part(hT[:, :, :].rearrange("p a b -> p (a b)"), 0, 4, 512)
        ohT = part(hT[:, :, :].rearrange("p a b -> p (a b)"), 2048, 8, 256)

        bank_filled = [sem(f"bank_filled{b}") for b in range(8)]
        bank_drained = [sem(f"bank_drained{b}") for b in range(8)]
        slot_filled = [sem(f"slot_filled{s}") for s in range(RING)]
        slot_free = [sem(f"slot_free{s}") for s in range(RING)]
        consts_in = sem("consts_in")
        c_in = sem("c_in")
        zeros_set = sem("zeros_set")
        context_in = sem("context_in")
        x_in = sem("x_in")
        proj_par_in = sem("proj_par_in")
        norm_par_in = sem("norm_par_in")
        router_in = sem("router_in")
        sink_in = sem("sink_in")
        bias_in = sem("bias_in")
        mod_stored = sem("mod_stored")
        mod_cols = sem("mod_cols")
        part_in = sem("part_in")
        parts = [0]
        early_in = [sem(f"early_in{i}") for i in range(4)]
        split_high = sem("split_high")
        split_low = sem("split_low")
        root_ready = sem("root_ready")
        sumsq_ready = sem("sumsq_ready")
        rms_taken = sem("rms_taken")
        cqn_ready = sem("cqn_ready")
        qkb_ready = sem("qkb_ready")
        qk_ready = sem("qk_ready")
        pads_zero = sem("pads_zero")
        max_ready = sem("max_ready")
        prob_ready = sem("prob_ready")
        gate_used = sem("gate_used")
        merged_ready = sem("merged_ready")
        var_ready = sem("var_ready")
        std_ready = sem("std_ready")
        x_ready = sem("x_ready")
        aff_shifted = sem("aff_shifted")
        aff_exp = sem("aff_exp")
        aff_ready = sem("aff_ready")
        pos_ready = sem("pos_ready")
        onehot_ready = sem("onehot_ready")
        weighted_ready = sem("weighted_ready")
        hid_ready = sem("hid_ready")
        y_ready = sem("y_ready")
        y_moved = [sem(f"y_moved{i}") for i in (0, 1)]
        last_y_moved = sem("last_y_moved")
        y_used = sem("y_used")
        out_stored = sem("out_stored")
        dve_step = sem("dve_step")
        act_step = sem("act_step")
        pool_step = sem("pool_step")
        block = es.enter_context(nc.Block())

        groups = {}
        fills, drains = [0] * 8, [0] * 8
        turn = [0]
        pieces, freed = [], []
        stream, gates_done = [], {}
        early = [(A, 8192), (A, 10240), (B, 0), (B, 2048)]
        frees, loads = [0] * RING, [0] * RING
        splits = [[] for _ in range(DEPTH)]

        def filled(eng, key):
            b, n, _ = groups[key]
            eng.wait_ge(bank_filled[b], n)
            return b

        def drained(eng, key):
            b, _, n = groups[key]
            eng.wait_ge(bank_drained[b], n)

        def second(eng, key):
            b, _, n = groups[key]
            eng.wait_ge(bank_drained[b], n - 1)
            return b

        def streams(l):
            return [0, 1] if l < DEPTH - 1 else [1]

        def tiles(l):
            return [t for s in streams(l) for t in (2 * s, 2 * s + 1)]

        def first_tile(l):
            return sum(len(tiles(i)) for i in range(l))

        def gather_cut(l, part):
            lo, hi = GATHERS[part]
            w = CAP * (hi - lo)
            return CAP * lo, w, 512 // (w * len(streams(l)))

        def first_splits(l):
            return 2 * len(tiles(l)) + 3

        def split_base(l):
            return sum(first_splits(i) + 15 for i in range(l))

        def split_order(l):
            f = first_splits(l)
            out = []
            for s in range(6):
                before = list(range(EARLY_SPLITS, f)) if s == 0 else []
                after = []
                if s < 5:
                    before += [f + 3 * s, f + 3 * s + 1]
                    after = [f + 3 * s + 2]
                out.append((before, after))
            return out

        def units(l, s):
            return [(4 * j + 2 * h + q, j, h, q) for j in range(8) for h in (0, 1) for q in (0, 1)]

        def unit_base(l, s):
            return 32 * (2 * l + s) if l == 0 else 64

        ADA_LATER = [(0, 1), (0, 2), (1, 0), (1, 1), (1, 2)]
        ROUTE_WAITS = {"norm": (4, 5, 6), "turned": (7,), "softmax": (), "largest": ()}
        QKV_TURNS = 16
        ada_due = {}
        for n in range(8 * len(ADA_LATER) - sum(len(ks) for ks in ROUTE_WAITS.values())):
            at = n if n < QKV_TURNS else QKV_TURNS + (n - QKV_TURNS) * 11 // 4
            which = ADA_LATER[n // 8]
            ada_due.setdefault(at, {})["products"] = which + (n % 8,)
            if n % 8 == 7:
                ada_due.setdefault(at, {})["move"] = which
                ada_due.setdefault(at + 2, {})["turn"] = which
                if which[1] == 2:
                    ada_due.setdefault(at + 4, {})["rows"] = which[0]
        for where, ks in ROUTE_WAITS.items():
            for k in ks:
                ada_due[(where, k)] = {"products": (1, 2, k)}
        ada_due["routed"] = {"move": (1, 2)}
        ada_due[("expert", 2)] = {"turn": (1, 2)}
        ada_due[("expert", 3)] = {"rows": 1}

        def moved(l, half, n):
            return y_moved[half], 64 * ((EXPERTS // 2 - half) * l + n)

        def move_rows(eng, l, e, signal):
            M = CAP * len(streams(l))
            Wd = D * M // P
            g = e // 4
            if g >= 2 and (e % 4 == 0 or e == EXPERTS - 1):
                for t in tiles(l):
                    for n in (0, 1):
                        filled(eng, ("SC", l, g - 2, t, n))
            eng.wait_ge(y_ready, EXPERTS * l + e + 1)
            for n in range(P // M):
                for i, s in enumerate(streams(l)):
                    at = n * M + i * CAP
                    eng.dma_start(YG[CAP * (e % 4):CAP * (e % 4) + CAP, 2 * (g % 2) + s, n * Wd:(n + 1) * Wd],
                                  ysb[at:at + CAP, e % 2, 0:Wd]).then_inc(signal, 16)

        @block.tensor
        def _(pe):
            def begin(key, takers=1, bank=None):
                b = turn[0] % 6 if bank is None else bank
                if bank is None:
                    turn[0] += 1
                if drains[b]:
                    pe.wait_ge(bank_drained[b], drains[b])
                fills[b] += 1
                drains[b] += takers
                groups[key] = (b, fills[b], drains[b])
                return b

            def end(ins, b):
                ins.then_inc(bank_filled[b], 1)
                return (bank_filled[b], fills[b])

            def piece(src, *shape):
                n = load(src, *shape)
                pe.wait_ge(slot_filled[n % RING], 16 * loads[n % RING])
                return n, pieces[n][0]

            def load(src, *shape):
                n = len(pieces)
                pieces.append((part(ring[:, n % RING, :], 0, *shape), src))
                stream.append((*pieces[n], n, None))
                freed.append(None)
                loads[n % RING] += 1
                return n

            def early_piece(l, i, src, *shape):
                dst = part(*early[i], *shape)
                stream.append((dst, src, i, gates_done[l]))
                pe.wait_ge(early_in[i], 16 * (l + 1))
                return dst

            def split_piece(l, src, *shape):
                n = load(src, *shape)
                pieces.append(None)
                freed.append(None)
                hi, lo = (part(ring_r[:, m % RING, :], 0, *shape) for m in (n + 1, n))
                splits[l].append((pieces[n][0], hi, lo, hi.bitcast(F32),
                                  (n, 16 * loads[n % RING])))
                return len(splits[l]), n, hi, lo

            def split_rows(l, src, hi, lo, t):
                cols = slice(t * P, (t + 1) * P)
                splits[l].append((src[:, :, cols], hi[:, :, cols], lo[:, :, cols], hi[:, :, cols].bitcast(F32), None))
                return len(splits[l])

            def free(n, ins=None, event=None):
                if event is None:
                    frees[n % RING] += 1
                    ins.then_inc(slot_free[n % RING], 1)
                    event = (slot_free[n % RING], frees[n % RING])
                freed[n] = event

            def mm(o, a, b, start=True, stop=True):
                return nc.tensor.matmul(o, a, b, start=start, stop=stop, skip_group_check=True)

            def ada_products(l, third, k):
                if k == 0:
                    begin(("ada", l, third), bank=ADA_BANK)
                n, w = piece(w_ada[l, k * P:(k + 1) * P, third * 2048:(third + 1) * 2048], 2048)
                for g in range(4):
                    ins = mm(psum[32 * g:32 * g + 32, ADA_BANK, :], cs[:, k, :], w[:, 512 * g:512 * g + 512],
                             k == 0, k == KT - 1)
                if k == KT - 1:
                    free(n, event=end(ins, ADA_BANK))
                else:
                    free(n, ins)

            def ada_turn(l, third):
                drained(pe, ("ada", l, third))
                b = begin(("adaT", l, third), bank=TURN_BANK)
                for j in range(4):
                    ins = nc.tensor.transpose(psum[:, b, P * j:P * j + P], modrow[:, P * j:P * j + P], ident)
                end(ins, b)

            def ada_rows(l):
                pe.wait_ge(mod_cols, 3 * l + 3)
                b = begin(("adaR", l), bank=TURN_BANK)
                end(nc.tensor.transpose(psum[0:96, b, 0:P], modcol[:, l, :, :].rearrange("p s c -> p (s c)"), ident), b)

            def ada_hook(step):
                due = ada_due.get(step, {})
                if "turn" in due:
                    ada_turn(*due["turn"])
                if "rows" in due:
                    ada_rows(due["rows"])
                if "products" in due:
                    ada_products(*due["products"])

            def ada_fill(l, where):
                for k in ROUTE_WAITS[where] if l == 0 else ():
                    ada_hook((where, k))

            def transposes(key, sources, rows=P, takers=1):
                b = begin(key, takers)
                for i, s in enumerate(sources):
                    ins = nc.tensor.transpose(psum[0:rows, b, i * P:(i + 1) * P], s, ident)
                end(ins, b)

            def x_transposes(name, l, t):
                for j in (0, 1):
                    transposes((name, l, t, j), [X[:, t, k * P:(k + 1) * P] for k in range(4 * j, 4 * j + 4)])

            def qkv(l, steps):
                held, turns = None, 0
                for step in steps:
                    kind, t = step[0], step[-1]
                    cut = l == DEPTH - 1 and t < 2
                    if kind == "H":
                        if l == 0:
                            pe.wait_ge(x_in, 16)
                        else:
                            pe.wait_ge(x_ready, 2 * first_tile(l - 1) + len(tiles(l - 1)) + t + 1)
                        x_transposes("hT", l, t)
                    if kind == "P":
                        ch = step[1]
                        width = sum(w for _, w in CHUNKS[ch])
                        if t == 0:
                            held = []
                        b = begin(("P", l, ch, t), takers=2 if ch != 0 else 1,
                                  bank=ADA_BANK if l and (ch, t) == (1, 0) else None)
                        lo = 384 if cut and ch in (0, 2) else 0
                        if ch == 1:
                            drained(pe, ("hT", l, t, 0))
                            drained(pe, ("hT", l, t, 1))
                        for k in range(KT):
                            if t == 0 and k % 4 == 0:
                                held.append(piece([w_in[l, P * k:P * k + 512, a:a + w] for a, w in CHUNKS[ch]], 4,
                                                  width))
                            ins = mm(psum[:, b, lo:width], hT[:, k, t * P:(t + 1) * P], held[k // 4][1][:, k % 4, lo:],
                                     k == 0, k == KT - 1)
                        event = end(ins, b)
                        if t == 3:
                            for n, _ in held:
                                free(n, event=event)
                        if l == 0:
                            ada_hook(turns)
                            turns += 1
                    if kind == "N":
                        pe.wait_ge(cqn_ready, 4 * l + t + 1)
                        transposes(("N", l, t), [cqn[:, t % 2, j * P:(j + 1) * P] for j in range(3)])
                    if kind == "U":
                        drained(pe, ("N", l, t))
                        if t == 0:
                            pe.wait_ge(proj_par_in, 96 * (l + 1))
                        if not cut:
                            b = begin(("UQ", l, t))
                            for j in (0, 1):
                                ins = mm(psum[:, b, 0:384], cqT[:, j, t * P:(t + 1) * P], uq[:, j, :], j == 0, j == 1)
                            end(ins, b)
                        b = begin(("UKV", l, t), takers=2)
                        end(mm(psum[:, b, :], cqT[:, 2, t * P:(t + 1) * P], ukv), b)
                    if kind == "TB":
                        pe.wait_ge(qkb_ready, 4 * l + t + 1)
                        kb = kbn[:, t % 2, :].rearrange("p (h d) -> p h d", h=4)
                        qb = qbn[:, t % 2, :].rearrange("p (h d) -> p h d", h=4)
                        if not cut:
                            transposes(("TBq", l, t), [qb[:, h, :] for h in range(4)], rows=QK_B)
                        transposes(("TBk", l, t), [kb[:, h, :] for h in range(4)], rows=QK_B)
                    if kind in ("TA", "TC"):
                        pe.wait_ge(qk_ready, 8 * l + t + 1 + 4 * (kind == "TC"))
                        q = qpad[:, t % 2, :].rearrange("p (h d) -> p h d", h=6)
                        if not cut:
                            transposes((kind + "q", l, t), [q[:, h, :] for h in range(4)])
                            transposes((kind + "r", l, t), [q[:, h, :] for h in (4, 5)] + [knat[:, t % 2, :]])
                        else:
                            transposes((kind + "r", l, t), [knat[:, t % 2, :]])

            def attention(l, s, step):
                nk = 2 if s == 0 else 4
                us = units(l, s)
                for i in range(len(us) + 5):
                    if s == streams(l)[0] and i == LAST_TURN_AT:
                        qkv(l, LAST_TURN)
                    if i < len(us):
                        u, j, h, q = us[i]
                        br, head = PAIRS[j][0], PAIRS[j][1] + h
                        t = 2 * s + q
                        b = begin(("S", l, s, u))
                        if br == "B":
                            mm_in = qT["B"][0:QK_B, head, t * P:(t + 1) * P], kT["B"][0:QK_B, head, 0:nk * P]
                        else:
                            mm_in = qT[br][:, head, t * P:(t + 1) * P], kT[br][:, 0:nk * P]
                        if u % 4 == 0 and (j == 0 or PAIRS[j - 1][0] != br):
                            for tt in range(4):
                                drained(pe, (f"T{br}k" if br == "B" else f"T{br}r", l, tt))
                                if not (l == DEPTH - 1 and tt < 2):
                                    drained(pe, (f"T{br}q", l, tt))
                        end(mm(psum[:, b, 0:nk * P], *mm_in), b)
                    if l == 0:
                        ada_hook(step)
                    step += 1
                    if 3 <= i < len(us) + 3:
                        u = us[i - 3][0]
                        pe.wait_ge(prob_ready, unit_base(l, s) + u + 1)
                        transposes(("T", l, s, u), [prob[:, u % 4, k * P:(k + 1) * P] for k in range(nk)])
                    if i >= 5 and us[i - 5][0] % 4 == 3:
                        u, j, _, _ = us[i - 5]
                        for v in range(u - 3, u + 1):
                            drained(pe, ("T", l, s, v))
                        b = begin(("O", l, s, j))
                        br, h0 = PAIRS[j]
                        for k in range(nk):
                            for h in (0, 1):
                                col = HD * (h0 + h if br == "B" else (h0 + h) // 3)
                                p = pT[:, (2 * j + h) % 3, :].rearrange("p (k q) -> p k q", q=256)
                                ins = mm(psum[HD * h:HD * h + HD, b, 0:256], V[br][:, k, col:col + HD], p[:, k, :],
                                         k == 0, k == nk - 1)
                        end(ins, b)
                return step

            def mm3(o, a_hi, a_lo, b_hi, b_lo, first, last):
                mm(o, a_hi, b_hi, first, False)
                mm(o, a_hi, b_lo, False, False)
                return mm(o, a_lo, b_hi, False, last)

            def gates(l):
                ts = tiles(l)
                base = split_base(l)
                h_split, o_split = {}, {}
                ready = [0]

                def need(number):
                    if number > ready[0]:
                        ready[0] = number
                        pe.wait_ge(split_low, base + number)

                sets = [(n, br) for n in (0, 1) for br in range(3)]

                def gate_pieces(n, br):
                    at = GATE_COL + br * D + n * 512
                    return [split_piece(l, [w_in[l, 512 * h:512 * h + 512, at:at + 512]], 4, 512) for h in (0, 1)]

                for n, br in sets:
                    lo_k, hi_k = BRANCH_TILES[br]
                    if (n, br) == (0, 0):
                        wg = gate_pieces(n, br)
                        for t in ts:
                            h_split[t] = split_rows(l, hT, h_hi, h_lo, t)
                    else:
                        wg = gate_pieces(n, br)
                    wb = split_piece(l, [w_branch[l, lo_k * P:hi_k * P, n * 512:n * 512 + 512]], hi_k - lo_k, 512)
                    if (n, br) == (0, 0):
                        for t in ts:
                            o_split[t] = split_rows(l, oT, o_hi, o_lo, t)
                    banks = {}
                    for h in (0, 1):
                        number, m, w_hi, w_lo = wg[h]
                        for t in ts:
                            cols = slice(t * P, (t + 1) * P)
                            if h == 0:
                                banks[t] = (begin(("G", l, n, br, t)), )
                            need(number)
                            need(h_split[t])
                            b = banks[t][0]
                            for k in range(4 * h, 4 * h + 4):
                                ins = mm3(psum[:, b, :], h_hi[:, k, cols], h_lo[:, k, cols], w_hi[:, k % 4, :],
                                          w_lo[:, k % 4, :], k == 0, k == KT - 1)
                            if h == 1:
                                event = end(ins, b)
                        if h == 0:
                            free(m, ins)
                            freed[m + 1] = freed[m]
                        else:
                            freed[m] = freed[m + 1] = event
                    number, m, w_hi, w_lo = wb
                    for t in ts:
                        cols = slice(t * P, (t + 1) * P)
                        b = begin(("BR", l, n, br, t))
                        need(number)
                        need(o_split[t])
                        for k in range(lo_k, hi_k):
                            ins = mm3(psum[:, b, :], o_hi[:, k, cols], o_lo[:, k, cols], w_hi[:, k - lo_k, :],
                                      w_lo[:, k - lo_k, :], k == lo_k, k == hi_k - 1)
                        event = end(ins, b)
                    freed[m] = freed[m + 1] = event
                gates_done[l] = event

            def project_and_route(l):
                ts = tiles(l)
                R = EXPERTS * len(streams(l))
                wo = None
                scores = begin(("R", l), bank=TURN_BANK)
                for i in range(len(ts) + 2):
                    if i < len(ts):
                        t = ts[i]
                        pe.wait_ge(merged_ready, first_tile(l) + i + 1)
                        for j in (0, 1):
                            transposes(("M", l, t, j),
                                       [merged[:, t, k * P:(k + 1) * P] for k in range(4 * j, 4 * j + 4)])
                    if 1 <= i <= len(ts):
                        t = ts[i - 1]
                        if wo is None:
                            wo = [piece([w_out[l, 512 * h:512 * h + 512, 512 * n:512 * n + 512]], 4, 512)
                                  for n in (0, 1) for h in (0, 1)]
                        drained(pe, ("M", l, t, 0))
                        drained(pe, ("M", l, t, 1))
                    if i == len(ts) + 1:
                        ada_fill(l, "norm")
                    for n in (0, 1):
                        if n == 1 and i >= 2:
                            pe.wait_ge(x_ready, 2 * first_tile(l) + i - 1)
                            x_transposes("h2T", l, ts[i - 2])
                        if 1 <= i <= len(ts):
                            t = ts[i - 1]
                            b = begin(("Y", l, t, n))
                            for k in range(KT):
                                ins = mm(psum[:, b, :], mT[:, k, t * P:(t + 1) * P], wo[2 * n + k // 4][1][:, k % 4, :],
                                         k == 0, k == KT - 1)
                            event = end(ins, b)
                    if i == len(ts):
                        for m, _ in wo:
                            free(m, event=event)
                    if i == len(ts) + 1:
                        ada_fill(l, "turned")
                    if i >= 2:
                        t = ts[i - 2]
                        if i == 2:
                            pe.wait_ge(router_in, 16 * (l + 1))
                        col = R * (t % 2) + EXPERTS * (t // 2 - streams(l)[0])
                        for k in range(KT):
                            if k % 4 == 0:
                                drained(pe, ("h2T", l, t, k // 4))
                            ins = mm(psum[:, scores, col:col + EXPERTS], hT[:, k, t * P:(t + 1) * P], wr[:, k, :],
                                     k == 0, k == KT - 1)
                end(ins, scores)

            def gather(l, part):
                lo, w, per = gather_cut(l, part)
                for k0 in range(0, KT, per):
                    b = begin(("XS", l, part, k0))
                    at = 0
                    for k in range(k0, k0 + per):
                        for s in streams(l):
                            for i in (0, 1):
                                ins = mm(psum[:, b, at:at + w], X[:, 2 * s + i, k * P:(k + 1) * P],
                                         onehot[:, 2 * s + i, lo:lo + w], i == 0, i == 1)
                            at += w
                    end(ins, b)

            def choose(l):
                R = EXPERTS * len(streams(l))
                ada_fill(l, "softmax")
                pe.wait_ge(aff_ready, l + 1)
                transposes(("AT", l), [affn[:, i, 0:R] for i in (0, 1)], rows=R)
                ada_fill(l, "largest")
                b = begin(("PT", l))
                pe.wait_ge(pos_ready, l + 1)
                for i in (0, 1):
                    ins = nc.tensor.transpose(psum[:, b, R * i:R * i + R], topT[0:R, 3, i * P:(i + 1) * P],
                                              ident[0:R, 0:R])
                end(ins, b)
                pe.wait_ge(onehot_ready, 2 * first_tile(l) + len(tiles(l)))
                gather(l, 0)

            def experts(l):
                M = CAP * len(streams(l))
                G = P // M
                Wd = D // G

                def into(e):
                    bg = begin(("HG", l, e))
                    bu = begin(("HU", l, e))
                    for part, (lo, _) in enumerate(GATHERS):
                        if e == lo:
                            for k0 in range(0, KT, gather_cut(l, part)[2]):
                                drained(pe, ("XS", l, part, k0))
                    for kp in range(4):
                        for at, (b, w) in enumerate(((bg, w_gate), (bu, w_up))):
                            src = [w[l, e, kp * 256:kp * 256 + 256, :]]
                            if e == 0 and kp < 2:
                                n, v = None, early_piece(l, 2 * kp + at, src, 2, D)
                            else:
                                n, v = piece(src, 2, D)
                            for k in (2 * kp, 2 * kp + 1):
                                for g in range(G):
                                    ins = mm(psum[g * M:(g + 1) * M, b, 0:Wd], xsT[:, k, e * M:(e + 1) * M],
                                             v[:, k % 2, g * Wd:(g + 1) * Wd], k == 0, k == KT - 1)
                            if kp == 3:
                                free(n, event=end(ins, b))
                            elif n is not None:
                                free(n, ins)

                def turn_hidden(e):
                    pe.wait_ge(hid_ready, EXPERTS * l + e + 1)
                    transposes(("HT", l, e), [hid[:, e % 2, j * P:(j + 1) * P] for j in range(Wd // P)])

                def down(e):
                    drained(pe, ("HT", l, e))
                    b = begin(("YE", l, e))
                    for kp in range(4):
                        n, v = piece([w_down[l, e, kp * 256:kp * 256 + 256, :]], 2, D)
                        for k in (2 * kp, 2 * kp + 1):
                            q, j = k // (Wd // P), k % (Wd // P)
                            for g in range(G):
                                ins = mm(psum[g * M:(g + 1) * M, b, 0:Wd],
                                         hidT[:, e % 2, j * P + q * M:j * P + (q + 1) * M],
                                         v[:, k % 2, g * Wd:(g + 1) * Wd], k == 0, k == KT - 1)
                        if kp == 3:
                            free(n, event=end(ins, b))
                        else:
                            free(n, ins)

                def scatter(g):
                    if g == 0:
                        for t in tiles(l):
                            drained(pe, ("OT", l, t))
                    pe.wait_ge(*moved(l, 0, 2 * g + 2))
                    pe.wait_ge(*moved(l, 1, min(2 * g + 2, EXPERTS // 2 - 1)))
                    if g == 3:
                        pe.wait_ge(last_y_moved, 64 * (l + 1))
                    for t in tiles(l):
                        s, i = t // 2, t % 2
                        for n in (0, 1):
                            b = begin(("SC", l, g, t, n))
                            end(mm(psum[:, b, :], ohT[:, 4 * s + g, i * P:(i + 1) * P],
                                   YG[:, 2 * (g % 2) + s, 512 * n:512 * n + 512]), b)

                for e in range(EXPERTS + 1):
                    if l == 0:
                        ada_hook(("expert", e))
                    if e < EXPERTS:
                        into(e)
                    if e == 0:
                        pe.wait_ge(weighted_ready, first_tile(l) + len(tiles(l)))
                        for t in tiles(l):
                            transposes(("OT", l, t), [ohw[:, t, g * P:(g + 1) * P] for g in range(4)])
                        pe.wait_ge(onehot_ready, 2 * (first_tile(l) + len(tiles(l))))
                    if 1 <= e <= 3:
                        gather(l, e)
                    if e >= 5 and e % 4 == 1:
                        scatter(e // 4 - 1)
                    if e >= 1:
                        down(e - 1)
                    if e < EXPERTS:
                        turn_hidden(e)
                scatter(3)

            pe.wait_ge(consts_in, 16)
            pe.wait_ge(c_in, 32)
            b = begin("c", bank=ADA_BANK)
            end(nc.tensor.transpose(psum[:, b, 0:2 * KT], cin[:, :], ident[0:2 * KT, 0:2 * KT]), b)
            for k in range(KT):
                if k == 4:
                    pe.wait_ge(context_in, 16)
                    for _, t in H_EARLY:
                        x_transposes("hT", 0, t)
                ada_products(0, 0, k)
            pe.wait_ge(bias_in, 32)
            b = begin("bias", bank=TURN_BANK)
            end(nc.tensor.transpose(psum[:, b, 0:48 * DEPTH], bias_rows[:, :], ident[0:48 * DEPTH, 0:48 * DEPTH]), b)
            ada_turn(0, 0)
            step = QKV_TURNS
            for l in range(DEPTH):
                qkv(l, PE_FIRST + QKV_NEXT if l else FIRST_STEPS)
                for s in streams(l):
                    step = attention(l, s, step)
                gates(l)
                project_and_route(l)
                choose(l)
                experts(l)

        @block.sync
        def _(sp):
            sp.dma_start(cst[:, :], consts).then_inc(consts_in, 16)
            for dst, src, n, after in stream:
                if after:
                    sp.wait_ge(*after)
                    sp.dma_start(dst, src[0].rearrange("(k p) n -> p k n", p=P)).then_inc(early_in[n], 16)
                    continue
                if n >= RING:
                    sp.wait_ge(*freed[n - RING])
                if not isinstance(src, list):
                    sp.dma_start(dst, src).then_inc(slot_filled[n % RING], 16)
                    continue
                if len(src) == 1:
                    sp.dma_start(dst, src[0].rearrange("(k p) n -> p k n", p=P)).then_inc(slot_filled[n % RING], 16)
                    continue
                at = 0
                for i, s in enumerate(src):
                    w = s.shape[1]
                    ins = sp.dma_start(dst[:, :, at:at + w], s.rearrange("(k p) n -> p k n", p=P))
                    if i == 0:
                        ins.then_inc(part_in, 16)
                        parts[0] += 16
                        sp.wait_ge(part_in, parts[0])
                    else:
                        ins.then_inc(slot_filled[n % RING], 16)
                    at += w
            for i, t in enumerate(tiles(DEPTH - 1)):
                sp.wait_ge(x_ready, 2 * first_tile(DEPTH) - len(tiles(DEPTH - 1)) + i + 1)
                sp.dma_start(out[0, i * P:(i + 1) * P, :], X[:, t, :]).then_inc(out_stored, 16)
            sp.wait_ge(out_stored, 16 * len(tiles(DEPTH - 1)))

        @block.gpsimd
        def _(pool):
            nc.gpsimd.memset(cs[:, :, :], 0.0).then_inc(zeros_set, 1)
            nc.gpsimd.memset(eps[:, 0:1], LN_EPS).then_inc(zeros_set, 1)
            nc.gpsimd.memset(eps[:, 1:2], RMS_EPS).then_inc(zeros_set, 1)
            pool.dma_start(X[:, 0:2, :], ctx_in.rearrange("b (t p) d -> p (b t) d", p=P)).then_inc(context_in, 16)
            pool.wait_ge(slot_filled[3], 16)
            pool.dma_start(X[:, 2:4, :], x.rearrange("b (t p) d -> p (b t) d", p=P)).then_inc(x_in, 16)

            def store_rows(l):
                drained(pool, ("adaR", l))
                pool.dma_start(mod_all[l].rearrange("s c p -> (s c) p"), mod_rows[:, :]).then_inc(mod_stored, 16)

            def row(ap):
                return ap.rearrange("(a n) -> a n", a=1).partition_broadcast(P)

            def norm_par(l, second):
                g, b = ((ln2_g, ln2_b) if second else (ln1_g, ln1_b))
                pool.dma_start(norm_g, row(g[l, :])).then_inc(norm_par_in, 16)
                pool.dma_start(norm_b, row(b[l, :])).then_inc(norm_par_in, 16)
                if not second:
                    for s in (0, 1):
                        pool.dma_start(gate_of[s], row(mod_all[l, s, 8 * G1:8 * G1 + 8, :].rearrange("c p -> (c p)"))) \
                            .then_inc(norm_par_in, 16)
                    return
                w = D * CAP * len(streams(l)) // P
                at = 0
                for n in range(D // w):
                    for s in streams(l):
                        cut = mod_all[l, s, 8 * G2:8 * G2 + 8, :].rearrange("c p -> (c p)")[n * w:(n + 1) * w]
                        pool.dma_start(gate_y[at:at + CAP, 0:w],
                                       cut.rearrange("(a n) -> a n", a=1).partition_broadcast(CAP)) \
                            .then_inc(norm_par_in, 16)
                        at += CAP

            for l in range(DEPTH):
                if l:
                    pool.wait_ge(x_ready, 2 * first_tile(l))
                    for t in tiles(l - 1):
                        for n in (0, 1):
                            filled(pool, ("SC", l - 1, 3, t, n))
                pool.dma_start(uq, b_w_uq[l].rearrange("(j p) n -> p j n", p=P)).then_inc(proj_par_in, 16)
                pool.dma_start(ukv, b_w_ukv[l]).then_inc(proj_par_in, 16)
                pool.dma_start(gain_cq[:, 0:256], row(b_q_norm[l, :])).then_inc(proj_par_in, 16)
                pool.dma_start(gain_cq[:, 256:384], row(b_kv_norm[l, :])).then_inc(proj_par_in, 16)
                pool.dma_start(part(PR, 1664, HD), row(c_q_norm[l, :])).then_inc(proj_par_in, 16)
                pool.dma_start(part(PR, 1728, HD), row(c_k_norm[l, :])).then_inc(proj_par_in, 16)
                pool.dma_start(sink[:, :], row(a_sink[l, :])).then_inc(sink_in, 16)
                pool.dma_start(wr[:, :, :], w_router[l].rearrange("(k p) e -> p k e", p=P)).then_inc(router_in, 16)
                nc.gpsimd.memset(qpad[:, :, :], 0.0).then_inc(pads_zero, 1)
                if l == 0:
                    store_rows(0)
                filled(pool, ("T", l, 1, 31))
                pool.wait_ge(mod_stored, 16 * (l + 1))
                norm_par(l, False)
                pool.wait_ge(x_ready, 2 * first_tile(l) + len(tiles(l)))
                norm_par(l, True)
                for e in range(EXPERTS - 1):
                    move_rows(pool, l, e, y_moved[e % 2])
                    if l == 0 and e == 3:
                        store_rows(1)

        @block.scalar
        def _(act):
            act.dma_start(cin[0:KT, :], c_ctx.rearrange("(k p) -> k p", p=P)).then_inc(c_in, 16)
            act.dma_start(cin[KT:2 * KT, :], c[0, :].rearrange("(k p) -> k p", p=P)).then_inc(c_in, 16)
            for l in range(DEPTH):
                act.dma_start(bias_rows[48 * l:48 * l + 48, :], b_ada[l, :].rearrange("(c p) -> c p", p=P)) \
                    .then_inc(bias_in, 16)
            steps = [0]

            def run(ins):
                steps[0] += 1
                ins.then_inc(act_step, 1)

            def settle():
                act.wait_ge(act_step, steps[0])

            act.wait_ge(zeros_set, 3)
            b = filled(act, "c")
            nc.scalar.activation(cs[:, :, 0:2], psum[:, b, 0:2 * KT].rearrange("p (s k) -> p k s", s=2), ACT.Silu) \
                .then_inc(bank_drained[b], 1)

            def ada_move(l, third):
                b = filled(act, ("ada", l, third))
                if (l, third) != (0, 0):
                    filled(act, ("adaT", *divmod(3 * l + third - 1, 3)))
                nc.scalar.copy(modrow[:, :], psum[:, b, :]).then_inc(bank_drained[b], 1)

            def ada_hook(step):
                due = ada_due.get(step, {})
                if "move" in due:
                    ada_move(*due["move"])
                if "rows" in due:
                    b = filled(act, ("adaR", due["rows"]))
                    if due["rows"]:
                        act.wait_ge(mod_stored, 16 * due["rows"])
                    nc.scalar.copy(mod_rows[:, :], psum[0:96, b, 0:P]).then_inc(bank_drained[b], 1)

            def modulated(name, l, t, scale, shift, halves=(0,)):
                s = t // 2
                for j in halves:
                    b = filled(act, (name, l, t, j))
                    for i in range(4):
                        k = 4 * j + i
                        ins = nc.scalar.activation(hT[:, k, t * P:(t + 1) * P], psum[:, b, i * P:(i + 1) * P],
                                                   ACT.Identity, scale=modcol[:, l, s, 8 * scale + k:8 * scale + k + 1],
                                                   bias=modcol[:, l, s, 8 * shift + k:8 * shift + k + 1])
                    ins.then_inc(bank_drained[b], 1)

            def qkv(l, steps):
                turns = 0
                for step in steps:
                    kind, t = step[0], step[-1]
                    cut = l == DEPTH - 1 and t < 2
                    cols = slice(t * P, (t + 1) * P)
                    n = 8 * l + t
                    if kind == "R":
                        norm_root(2 * first_tile(l - 1) + len(tiles(l - 1)) + t + 1)
                    if kind == "H":
                        if t == 0:
                            act.wait_ge(mod_cols, 1 if l == 0 else 6)
                        modulated("hT", l, t, SC1, SH1, (0, 1) if l and t < 2 else (0,))
                    if kind == "P":
                        if l == 0 and turns:
                            ada_hook(turns - 1)
                        turns += 1
                    if kind == "P" and step[1] == 1:
                        b = filled(act, ("P", l, 1, t))
                        nc.scalar.copy(V["A"][:, t, :], psum[:, b, 0:P])
                        if n:
                            act.wait_ge(rms_taken, n if t else 8 * l)
                        run(nc.scalar.activation(sq[:, 0:256], psum[:, b, 128:384], ACT.Square,
                                                 accum_out=small[:, 0:1]))
                        settle()
                        nc.scalar.activation(sq[:, 0:128], psum[:, b, 384:512], ACT.Square,
                                             accum_out=small[:, 1:2]).then_inc(bank_drained[b], 1)
                        run(nc.scalar.activation(small[:, 2:3], small[:, 0:1], ACT.Sqrt, bias=eps[:, 1:2],
                                                 scale=1.0 / 256))
                        settle()
                        nc.scalar.activation(small[:, 3:4], small[:, 1:2], ACT.Sqrt, bias=eps[:, 1:2],
                                             scale=1.0 / 128).then_inc(root_ready, 1)
                    if kind == "P" and step[1] == 3:
                        b = filled(act, ("P", l, 3, t))
                        nc.scalar.copy(V["C"][:, t, :], psum[:, b, 32:160]).then_inc(bank_drained[b], 1)
                    if kind == "P" and step[1] == 2:
                        b = filled(act, ("P", l, 2, t))
                        lo = 384 if cut else 0
                        act.wait_ge(rms_taken, 8 * l + 4 + t)
                        nc.scalar.activation(sq[:, lo:512], psum[:, b, lo:512], ACT.Square) \
                            .then_inc(bank_drained[b], 1)
                        act.wait_ge(sumsq_ready, 4 * l + t + 1)
                        nc.scalar.activation(small[:, 12 + lo // 64:20], small[:, 4 + lo // 64:12], ACT.Sqrt,
                                             bias=eps[:, 1:2], scale=1.0 / HD).then_inc(root_ready, 1)
                    if kind == "N":
                        b = filled(act, ("N", l, t))
                        nc.scalar.copy(cqT[:, :, cols], psum[:, b, 0:384].rearrange("p (j q) -> p j q", j=3)) \
                            .then_inc(bank_drained[b], 1)
                    if kind == "U":
                        b = filled(act, ("UKV", l, t))
                        nc.scalar.copy(V["B"][:, t, :].rearrange("p (h d) -> p h d", h=4),
                                       psum[:, b, :].rearrange("p (h d) -> p h d", h=4)[:, :, HD:]) \
                            .then_inc(bank_drained[b], 1)
                    if kind == "TB":
                        for name, dst in ((("TBq", qT["B"]),) if not cut else ()) + (("TBk", kT["B"]),):
                            b = filled(act, (name, l, t))
                            nc.scalar.copy(dst[0:QK_B, :, cols], psum[0:QK_B, b, :].rearrange("p (h q) -> p h q", h=4)) \
                                .then_inc(bank_drained[b], 1)
                    if kind in ("TA", "TC"):
                        if not cut:
                            b = filled(act, (kind + "q", l, t))
                            nc.scalar.copy(qT[kind[1]][:, 0:4, cols], psum[:, b, :].rearrange("p (h q) -> p h q", h=4)) \
                                .then_inc(bank_drained[b], 1)
                            b = filled(act, (kind + "r", l, t))
                            nc.scalar.copy(qT[kind[1]][:, 4:6, cols],
                                           psum[:, b, 0:256].rearrange("p (h q) -> p h q", h=2))
                            nc.scalar.copy(kT[kind[1]][:, cols], psum[:, b, 256:384]).then_inc(bank_drained[b], 1)
                        else:
                            b = filled(act, (kind + "r", l, t))
                            nc.scalar.copy(kT[kind[1]][:, cols], psum[:, b, 0:P]).then_inc(bank_drained[b], 1)

            def attention(l, s, step):
                nk = 2 if s == 0 else 4
                us = units(l, s)
                for i in range(len(us) + 5):
                    if s == streams(l)[0] and i == LAST_TURN_AT:
                        qkv(l, LAST_TURN)
                    if i < len(us):
                        u, j, h, q = us[i]
                        br, head = PAIRS[j][0], PAIRS[j][1] + h
                        b = filled(act, ("S", l, s, u))
                        act.wait_ge(max_ready, unit_base(l, s) + u + 1)
                        if u >= 4:
                            filled(act, ("T", l, s, u - 4))
                        c4 = 64 + 4 * (u % 4)
                        if br == "A":
                            nc.scalar.activation(small[:, c4 + 1:c4 + 2], sink[:, head:head + 1], ACT.Exp,
                                                 bias=small[:, c4:c4 + 1])
                        nc.scalar.activation(prob[:, u % 4, 0:nk * P], psum[:, b, 0:nk * P], ACT.Exp,
                                             bias=small[:, c4:c4 + 1], scale=SCALE_B if br == "B" else SCALE_AC,
                                             accum_out=small[:, c4 + 2:c4 + 3]).then_inc(bank_drained[b], 1)
                    if l == 0:
                        ada_hook(step)
                    step += 1
                    if 3 <= i < len(us) + 3:
                        u, j, h, q = us[i - 3]
                        b = filled(act, ("T", l, s, u))
                        hd = 2 * j + h
                        if hd >= 3:
                            filled(act, ("O", l, s, (hd - 3) // 2))
                        p = pT[:, hd % 3, :].rearrange("p (k q) -> p k q", q=256)
                        nc.scalar.copy(p[:, 0:nk, q * P:(q + 1) * P],
                                       psum[:, b, 0:nk * P].rearrange("p (k q) -> p k q", k=nk)) \
                            .then_inc(bank_drained[b], 1)
                    if i >= 5 and us[i - 5][0] % 4 == 3:
                        j = us[i - 5][1]
                        b = filled(act, ("O", l, s, j))
                        nc.scalar.copy(oT[:, j, 256 * s:256 * s + 256], psum[:, b, 0:256]) \
                            .then_inc(bank_drained[b], 1)
                    if s == 1 and i in EARLY_SPLITS_AT:
                        high(l, EARLY_SPLITS_AT.index(i))
                return step

            def high(l, i):
                src, hi, _, _, where = splits[l][i]
                if where:
                    m, count = where
                    act.wait_ge(slot_filled[m % RING], count)
                    if m + 1 >= RING:
                        act.wait_ge(*freed[m + 1 - RING])
                nc.scalar.copy(hi, src).then_inc(split_high, 1)

            def norm_root(n):
                act.wait_ge(var_ready, n)
                nc.scalar.activation(small[:, 43:44], small[:, 42:43], ACT.Sqrt, bias=eps[:, 0:1]) \
                    .then_inc(std_ready, 1)

            step = QKV_TURNS
            ada_move(0, 0)
            for l in range(DEPTH):
                n_gates = 6 * first_tile(l)
                qkv(l, ACT_FIRST + QKV_NEXT if l else H_EARLY + FIRST_STEPS)
                if l == 0:
                    ada_hook(QKV_TURNS - 1)
                for s in streams(l):
                    step = attention(l, s, step)
                drained(act, ("O", l, 1, 7))

                for (before, after), (n, br) in zip(split_order(l), [(n, br) for n in (0, 1) for br in range(3)]):
                    for i in before:
                        high(l, i)
                    for t in tiles(l):
                        b = filled(act, ("G", l, n, br, t))
                        i = n_gates
                        n_gates += 1
                        if i >= 4:
                            act.wait_ge(gate_used, i - 3)
                        nc.scalar.activation(sg[:, i % 4, :], psum[:, b, :], ACT.Sigmoid) \
                            .then_inc(bank_drained[b], 1)
                    for i in after:
                        high(l, i)
                ts = tiles(l)
                for i in range(len(ts) + 2):
                    if i < len(ts):
                        for j in (0, 1):
                            b = filled(act, ("M", l, ts[i], j))
                            nc.scalar.copy(mT[:, 4 * j:4 * j + 4, ts[i] * P:(ts[i] + 1) * P],
                                           psum[:, b, :].rearrange("p (k q) -> p k q", k=4)) \
                                .then_inc(bank_drained[b], 1)
                    if i >= 2:
                        if i == 2:
                            act.wait_ge(mod_cols, 3 * (l + 1))
                        modulated("h2T", l, ts[i - 2], SC2, SH2, (0, 1) if i <= len(ts) else (0,))
                    if 1 <= i <= len(ts):
                        norm_root(2 * first_tile(l) + i)
                act.wait_ge(aff_shifted, l + 1)
                scores = affn[:, :, 0:EXPERTS * len(streams(l))]
                nc.scalar.activation(scores, scores, ACT.Exp).then_inc(aff_exp, 1)
                M = CAP * len(streams(l))

                def gathered(part):
                    lo, w, per = gather_cut(l, part)
                    n = len(streams(l))
                    for k0 in range(0, KT, per):
                        b = filled(act, ("XS", l, part, k0))
                        at = 0
                        for k in range(k0, k0 + per):
                            dst = xsT[:, k, n * lo:n * (lo + w)].rearrange("p (e m) -> p e m", m=M)
                            for i, s in enumerate(streams(l)):
                                ins = nc.scalar.activation(dst[:, :, CAP * i:CAP * i + CAP],
                                                           psum[:, b, at:at + w].rearrange("p (e m) -> p e m", m=CAP),
                                                           ACT.Identity,
                                                           scale=modcol[:, l, s, 8 * SC2 + k:8 * SC2 + k + 1],
                                                           bias=modcol[:, l, s, 8 * SH2 + k:8 * SH2 + k + 1])
                                at += w
                        ins.then_inc(bank_drained[b], 1)

                if l == 0:
                    ada_hook("routed")
                gathered(0)
                Wd = D * M // P
                for e in range(EXPERTS):
                    if l == 0:
                        ada_hook(("expert", e))
                    b = filled(act, ("HG", l, e))
                    if e >= 2:
                        act.wait_ge(hid_ready, EXPERTS * l + e - 1)
                    nc.scalar.activation(sil[:, e % 2, 0:Wd], psum[:, b, 0:Wd], ACT.Silu).then_inc(bank_drained[b], 1)
                    if e == 0:
                        for t in tiles(l):
                            b = filled(act, ("OT", l, t))
                            nc.scalar.copy(ohT[:, 4 * (t // 2):4 * (t // 2) + 4, (t % 2) * P:(t % 2 + 1) * P],
                                           psum[:, b, :].rearrange("p (g q) -> p g q", g=4)).then_inc(bank_drained[b], 1)
                    if 1 <= e <= 3:
                        gathered(e)
                    b = filled(act, ("HT", l, e))
                    if e >= 2:
                        filled(act, ("YE", l, e - 2))
                    nc.scalar.copy(hidT[:, e % 2, 0:Wd], psum[:, b, 0:Wd]).then_inc(bank_drained[b], 1)
                move_rows(act, l, EXPERTS - 1, last_y_moved)
                if l == DEPTH - 1:
                    for i in range(len(ts)):
                        norm_root(2 * first_tile(l) + len(ts) + i + 1)

        @block.vector
        def _(dve):
            steps = [0]
            V_ = nc.vector

            def run(ins):
                steps[0] += 1
                ins.then_inc(dve_step, 1)
                dve.wait_ge(dve_step, steps[0])

            def mark(sem):
                V_.engine_nop().then_inc(sem, 1)

            def ada_columns(l, third):
                b = filled(dve, ("adaT", l, third))
                src = psum[:, b, :].rearrange("p (j g r) -> p g j r", j=4, g=4)
                bias = bias_cols[:, 48 * l + 16 * third:48 * l + 16 * third + 16].rearrange("p (g j) -> p g j", g=4)
                dst = modcol[:, l, :, 16 * third:16 * third + 16]
                for s in (0, 1):
                    ins = V_.tensor_tensor(dst[:, s, :].rearrange("p (g j) -> p g j", g=4), src[:, :, :, s], bias,
                                           ALU.add)
                run(ins)
                mark(bank_drained[b])
                if third != 1:
                    at = 8 if third == 0 else 0
                    run(V_.tensor_scalar(dst[:, :, at:at + 8], dst[:, :, at:at + 8], 1.0, None, ALU.add))
                mark(mod_cols)

            def ada_hook(step):
                due = ada_due.get(step, {})
                if "turn" in due:
                    ada_columns(*due["turn"])

            def modulated(name, l, t, scale, shift):
                s = t // 2
                b = filled(dve, (name, l, t, 1))
                for i in range(4):
                    k = 4 + i
                    ins = V_.tensor_scalar(hT[:, k, t * P:(t + 1) * P], psum[:, b, i * P:(i + 1) * P],
                                           modcol[:, l, s, 8 * scale + k:8 * scale + k + 1],
                                           modcol[:, l, s, 8 * shift + k:8 * shift + k + 1], ALU.mult, ALU.add)
                ins.then_inc(bank_drained[b], 1)

            def rope(t, xin, outs, h, half):
                at = C_ROPE + 192 * (t - 2) + (0 if half == 16 else 128)
                w = 4 * half
                cos = cst[:, at:at + w]
                sin = cst[:, at + w:at + 2 * w]
                x3 = xin.rearrange("p (h d) -> p h d", d=w)
                V_.tensor_tensor(m1[:, 0:h * w].rearrange("p (h d) -> p h d", d=w), x3,
                                 cos.unsqueeze(1).to_broadcast([P, h, w]), ALU.mult)
                x5 = xin.rearrange("p (h a z d) -> p h a z d", a=2, z=2, d=half)
                o5 = m2[:, 0:h * w].rearrange("p (h a z d) -> p h a z d", a=2, z=2, d=half)
                s4 = sin.rearrange("p (a z d) -> p a z d", a=2, z=2)
                for z in (0, 1):
                    ins = V_.tensor_tensor(o5[:, :, :, z, :], x5[:, :, :, 1 - z, :],
                                           s4[:, :, z, :].unsqueeze(1).to_broadcast([P, h, 2, half]), ALU.mult)
                    if z == 0:
                        continue
                    run(ins)
                for o, view in outs[:-1]:
                    V_.tensor_tensor(o, view(m1), view(m2), ALU.add)
                o, view = outs[-1]
                run(V_.tensor_tensor(o, view(m1), view(m2), ALU.add))

            def pad_view(i, g):
                return qpad[:, i, 384 * g:384 * g + 384].rearrange("p (r d) -> p r d", r=3)[:, :, HD * g:HD * g + HD]

            def third(v, g):
                return v[:, 192 * g:192 * g + 192].rearrange("p (r d) -> p r d", r=3)

            def heads_out(i, cut):
                outs = [] if cut else [(pad_view(i, 0), lambda v: third(v, 0)), (pad_view(i, 1), lambda v: third(v, 1))]
                return outs + [(knat[:, i, :], lambda v: v[:, 384:512])]

            def qkv(l, steps):
                turns = 0
                for step in steps:
                    kind, t = step[0], step[-1]
                    cut = l == DEPTH - 1 and t < 2
                    i = t % 2
                    if kind == "H":
                        modulated("hT", l, t, SC1, SH1)
                    if kind == "P":
                        if l == 0 and turns:
                            ada_hook(turns - 1)
                        turns += 1
                    if kind == "P" and step[1] == 1:
                        b = filled(dve, ("P", l, 1, t))
                        if t == 0:
                            dve.wait_ge(proj_par_in, 96 * (l + 1))
                        dve.wait_ge(root_ready, 8 * l + t + 1)
                        if l or t:
                            dve.wait_ge(cqn_ready, 4 * l + t)
                        run(V_.reciprocal(small[:, 20:22], small[:, 2:4]))
                        if t >= 2:
                            filled(dve, ("N", l, t - 2))
                        V_.scalar_tensor_tensor(cqn[:, i, 0:256], psum[:, b, 128:384], small[:, 20:21],
                                                gain_cq[:, 0:256], ALU.mult, ALU.mult).then_inc(rms_taken, 1)
                        V_.scalar_tensor_tensor(cqn[:, i, 256:384], psum[:, b, 384:512], small[:, 21:22],
                                                gain_cq[:, 256:384], ALU.mult, ALU.mult).then_inc(cqn_ready, 1)
                        mark(bank_drained[b])
                    if kind == "P" and step[1] == 3:
                        b = second(dve, ("P", l, 3, t))
                        if t < 2:
                            V_.tensor_copy(krr[:, t, :], psum[:, b, 0:ROPE_B]).then_inc(bank_drained[b], 1)
                        else:
                            rope(t, psum[:, b, 0:ROPE_B], [(krr[:, t, :], lambda v: v[:, 0:ROPE_B])], 1, 8)
                            mark(bank_drained[b])
                    if kind == "U":
                        qb = qbn[:, i, :].rearrange("p (h d) -> p h d", h=4)
                        kb = kbn[:, i, :].rearrange("p (h d) -> p h d", h=4)
                        if t >= 2:
                            filled(dve, ("TBk", l, t - 2))
                        if not cut:
                            b = filled(dve, ("UQ", l, t))
                            src = psum[:, b, 0:384].rearrange("p (h d) -> p h d", h=4)
                            if t < 2:
                                V_.tensor_copy(qb, src).then_inc(bank_drained[b], 1)
                            else:
                                V_.tensor_copy(qb[:, :, 0:HD], src[:, :, 0:HD])
                                run(V_.tensor_copy(xg[:, 0:128].rearrange("p (h d) -> p h d", h=4), src[:, :, HD:]))
                                rope(t, xg[:, 0:128], [(qb[:, :, HD:], lambda v: v[:, 0:128].rearrange(
                                    "p (h d) -> p h d", h=4))], 4, 8)
                                mark(bank_drained[b])
                        b = second(dve, ("UKV", l, t))
                        V_.tensor_copy(kb[:, :, 0:HD],
                                       psum[:, b, :].rearrange("p (h d) -> p h d", h=4)[:, :, 0:HD]) \
                            .then_inc(bank_drained[b], 1)
                        drained(dve, ("P", l, 3, t))
                        V_.tensor_copy(kb[:, :, HD:], krr[:, t, :].unsqueeze(1).to_broadcast([P, 4, ROPE_B])) \
                            .then_inc(qkb_ready, 1)
                    if kind == "P" and step[1] == 0:
                        b = filled(dve, ("P", l, 0, t))
                        if t == 0:
                            dve.wait_ge(pads_zero, l + 1)
                        if t >= 2:
                            filled(dve, ("TAr", l, t - 2))
                        if t < 2:
                            for o, view in heads_out(i, cut):
                                V_.tensor_copy(o, view(psum[:, b, :]))
                        else:
                            rope(t, psum[:, b, :], heads_out(i, cut), 8, 16)
                        mark(bank_drained[b])
                        mark(qk_ready)
                    if kind == "P" and step[1] == 2:
                        b = filled(dve, ("P", l, 2, t))
                        h0 = 6 if cut else 0
                        second(dve, ("P", l, 2, t))
                        V_.tensor_reduce(small[:, 4 + h0:12],
                                         sq[:, 64 * h0:512].rearrange("p (h d) -> p h d", d=HD), AX, ALU.add) \
                            .then_inc(sumsq_ready, 1)
                        dve.wait_ge(root_ready, 8 * l + 4 + t + 1)
                        run(V_.reciprocal(small[:, 32 + h0:40], small[:, 12 + h0:20]))
                        nh = 8 - h0
                        run(V_.tensor_tensor(xg[:, 64 * h0:512].rearrange("p (h d) -> p h d", d=HD),
                                             psum[:, b, 64 * h0:512].rearrange("p (h d) -> p h d", d=HD),
                                             small[:, 32 + h0:40].unsqueeze(2).to_broadcast([P, nh, HD]), ALU.mult))
                        mark(bank_drained[b])
                        mark(rms_taken)
                        filled(dve, ("TAr", l, t + 2) if t < 2 else ("TCr", l, t - 2))
                        g6 = gain_q.unsqueeze(1).to_broadcast([P, 6, HD])
                        g2 = gain_k.unsqueeze(1).to_broadcast([P, 2, HD])
                        k2 = xg[:, 384:512].rearrange("p (h d) -> p h d", d=HD)
                        if t < 2:
                            if not cut:
                                for g in (0, 1):
                                    V_.tensor_tensor(pad_view(i, g), third(xg, g),
                                                     gain_q.unsqueeze(1).to_broadcast([P, 3, HD]), ALU.mult)
                            V_.tensor_tensor(knat[:, i, :].rearrange("p (h d) -> p h d", d=HD), k2, g2, ALU.mult) \
                                .then_inc(qk_ready, 1)
                        else:
                            q6 = xg[:, 0:384].rearrange("p (h d) -> p h d", d=HD)
                            V_.tensor_tensor(q6, q6, g6, ALU.mult)
                            run(V_.tensor_tensor(k2, k2, g2, ALU.mult))
                            rope(t, xg, heads_out(i, cut), 8, 16)
                            mark(qk_ready)

            def attention(l, s, step):
                nk = 2 if s == 0 else 4
                us = units(l, s)
                for i in range(len(us) + 5):
                    if i < len(us):
                        u, j, h, q = us[i]
                        br, head = PAIRS[j][0], PAIRS[j][1] + h
                        b = filled(dve, ("S", l, s, u))
                        c4 = 64 + 4 * (u % 4)
                        if br == "A" and s == 1:
                            run(V_.tensor_tensor(psum[:, b, 256:512], psum[:, b, 256:512],
                                                 cst[:, C_MASK + 256 * q:C_MASK + 256 * q + 256], ALU.add))
                        run(V_.tensor_reduce(small[:, c4 + 3:c4 + 4], psum[:, b, 0:nk * P], AX, ALU.max, negate=True))
                        if br == "A":
                            V_.tensor_scalar(small[:, c4:c4 + 1], small[:, c4 + 3:c4 + 4], SCALE_AC,
                                             nsink[:, head:head + 1], ALU.mult, ALU.min).then_inc(max_ready, 1)
                        else:
                            V_.tensor_scalar(small[:, c4:c4 + 1], small[:, c4 + 3:c4 + 4],
                                             SCALE_B if br == "B" else SCALE_AC, None, ALU.mult) \
                                .then_inc(max_ready, 1)
                    if l == 0:
                        ada_hook(step)
                    step += 1
                    if 1 <= i < len(us) + 1:
                        u, j, h, q = us[i - 1]
                        c4 = 64 + 4 * (u % 4)
                        drained(dve, ("S", l, s, u))
                        if PAIRS[j][0] == "A":
                            run(V_.tensor_tensor(small[:, c4 + 2:c4 + 3], small[:, c4 + 2:c4 + 3],
                                                 small[:, c4 + 1:c4 + 2], ALU.add))
                        run(V_.reciprocal(small[:, c4 + 2:c4 + 3], small[:, c4 + 2:c4 + 3]))
                        V_.tensor_scalar(prob[:, u % 4, 0:nk * P], prob[:, u % 4, 0:nk * P],
                                         small[:, c4 + 2:c4 + 3], None, ALU.mult).then_inc(prob_ready, 1)
                return step

            def layer_norm(l, t, n, xt):
                if n:
                    dve.wait_ge(std_ready, n)
                V_.bn_aggr(small[:, 41:43], stats[:, :, :].rearrange("p a b -> p (a b)")).then_inc(var_ready, 1)
                dve.wait_ge(std_ready, n + 1)
                run(V_.reciprocal(small[:, 46:47], small[:, 43:44]))
                run(V_.scalar_tensor_tensor(xt, xt, small[:, 41:42], norm_g, ALU.subtract, ALU.mult))
                run(V_.scalar_tensor_tensor(X[:, t, :], xt, small[:, 46:47], norm_b, ALU.mult, ALU.add))
                mark(x_ready)

            def project(l, i):
                    t = tiles(l)[i]
                    if i == 0:
                        dve.wait_ge(norm_par_in, 160 * l + 64)
                    lt = ln_t[:, i % 2, :]
                    for n in (0, 1):
                        b = filled(dve, ("Y", l, t, n))
                        half = lt[:, 512 * n:512 * n + 512]
                        V_.tensor_tensor(half, psum[:, b, :], gate_of[t // 2][:, 512 * n:512 * n + 512], ALU.mult) \
                            .then_inc(bank_drained[b], 1)
                        drained(dve, ("Y", l, t, n))
                        run(V_.scalar_tensor_tensor(half, X[:, t, 512 * n:512 * n + 512], ALPHA, half, ALU.mult,
                                                    ALU.add))
                        run(V_.bn_stats(stats[:, n, :], half))
                    layer_norm(l, t, 2 * first_tile(l) + i, lt)

            def affinity(l):
                n = len(streams(l))
                b = filled(dve, ("R", l))
                scores = psum[:, b, 0:2 * EXPERTS * n].rearrange("p (i s e) -> p i s e", i=2, s=n)
                a = affn[:, :, 0:EXPERTS * n].rearrange("p i (s e) -> p i s e", s=n)
                peak = small[:, 48:48 + 2 * n].rearrange("p (i s) -> p i s", i=2)
                total = small[:, 52:52 + 2 * n].rearrange("p (i s) -> p i s", i=2)
                run(V_.tensor_reduce(peak, scores, AX, ALU.max))
                V_.tensor_tensor(a, scores, peak.unsqueeze(3).to_broadcast([P, 2, n, EXPERTS]), ALU.subtract) \
                    .then_inc(aff_shifted, 1)
                mark(bank_drained[b])
                dve.wait_ge(aff_exp, l + 1)
                run(V_.tensor_reduce(total, a, AX, ALU.add))
                run(V_.reciprocal(total, total))
                run(V_.tensor_tensor(a, a, total.unsqueeze(3).to_broadcast([P, 2, n, EXPERTS]), ALU.mult))

            def route(l):
                S0 = streams(l)[0]
                R = EXPERTS * len(streams(l))
                for i in range(len(tiles(l))):
                    project(l, i)
                modulated("h2T", l, tiles(l)[-1], SC2, SH2)
                affinity(l)
                mark(aff_ready)
                run(V_.memset(ones[0:R, :], 1.0))
                b = filled(dve, ("AT", l))
                run(V_.tensor_copy(topT[0:R, 0, :], psum[0:R, b, 0:256]))
                mark(bank_drained[b])
                for r in range(CAP // 8):
                    run(V_.max(max8[0:R, :], topT[0:R, r % 2, :]))
                    run(V_.match_replace(topT[0:R, (r + 1) % 2, :], max8[0:R, :], topT[0:R, r % 2, :], -1.0))
                run(V_.tensor_scalar(topT[0:R, 2, :], topT[0:R, 0, :], 0.0, None, ALU.is_lt))
                run(V_.tensor_tensor_scan(topT[0:R, 3, :], ones[0:R, :], topT[0:R, 2, :], 0.0, ALU.mult, ALU.add))
                V_.tensor_tensor(topT[0:R, 3, :], topT[0:R, 3, :], topT[0:R, 2, :], ALU.mult).then_inc(pos_ready, 1)
                b = filled(dve, ("PT", l))
                run(V_.tensor_copy(posn[:, :, 0:R], psum[:, b, 0:2 * R].rearrange("p (i r) -> p i r", i=2)))
                mark(bank_drained[b])
                for lo, hi in (GATHERS[0], (GATHERS[0][1], EXPERTS)):
                    for t in tiles(l):
                        col = EXPERTS * (t // 2 - S0)
                        V_.tensor_tensor(onehot[:, t, CAP * lo:CAP * hi].rearrange("p (e m) -> p e m", m=CAP),
                                         iota1.unsqueeze(1).to_broadcast([P, hi - lo, CAP]),
                                         posn[:, t % 2, col + lo:col + hi].unsqueeze(2)
                                         .to_broadcast([P, hi - lo, CAP]), ALU.is_equal).then_inc(onehot_ready, 1)
                dve.wait_ge(onehot_ready, 2 * (first_tile(l) + len(tiles(l))))
                for t in tiles(l):
                    col = 16 * (t // 2 - S0)
                    V_.tensor_tensor(ohw[:, t, :].rearrange("p (e m) -> p e m", m=CAP),
                                     onehot[:, t, :].rearrange("p (e m) -> p e m", m=CAP),
                                     affn[:, t % 2, col:col + 16].unsqueeze(2).to_broadcast([P, EXPERTS, CAP]),
                                     ALU.mult).then_inc(weighted_ready, 1)

            def experts(l):
                M = CAP * len(streams(l))
                Wd = D * M // P
                dve.wait_ge(norm_par_in, 160 * l + 160)

                def scatter(g):
                    for i, t in enumerate(tiles(l)):
                        for n in (0, 1):
                            b = filled(dve, ("SC", l, g, t, n))
                            cols = slice(512 * n, 512 * n + 512)
                            V_.tensor_tensor(X[:, t, cols], X[:, t, cols], psum[:, b, :], ALU.add) \
                                .then_inc(bank_drained[b], 1)
                            if g == 3:
                                drained(dve, ("SC", l, g, t, n))
                                run(V_.bn_stats(stats[:, n, :], X[:, t, cols]))
                        if g == 3:
                            layer_norm(l, t, 2 * first_tile(l) + len(tiles(l)) + i, X[:, t, :])

                for e in range(EXPERTS + 1):
                    if l == 0:
                        ada_hook(("expert", e))
                    if e < EXPERTS:
                        b = filled(dve, ("HU", l, e))
                        drained(dve, ("HG", l, e))
                        if e >= 2:
                            filled(dve, ("HT", l, e - 2))
                        V_.tensor_tensor(hid[:, e % 2, 0:Wd], sil[:, e % 2, 0:Wd], psum[:, b, 0:Wd], ALU.mult) \
                            .then_inc(hid_ready, 1)
                        mark(bank_drained[b])
                    if e == 4:
                        last = len(GATHERS) - 1
                        filled(dve, ("XS", l, last, KT - gather_cut(l, last)[2]))
                        for t in tiles(l):
                            run(V_.tensor_scalar(X[:, t, :], X[:, t, :], ALPHA, None, ALU.mult))
                    if e >= 5 and e % 4 == 1:
                        scatter(e // 4 - 1)
                    if e >= 1:
                        b = filled(dve, ("YE", l, e - 1))
                        if e >= 3:
                            dve.wait_ge(*moved(l, (e - 1) % 2, (e - 1) // 2))
                        V_.tensor_tensor(ysb[:, (e - 1) % 2, 0:Wd], psum[:, b, 0:Wd], gate_y[:, 0:Wd], ALU.mult) \
                            .then_inc(y_ready, 1)
                        mark(bank_drained[b])
                scatter(3)

            dve.wait_ge(consts_in, 16)
            b = filled(dve, "bias")
            V_.tensor_copy(bias_cols[:, :], psum[:, b, 0:48 * DEPTH]).then_inc(bank_drained[b], 1)
            drained(dve, "bias")
            ada_columns(0, 0)
            step = QKV_TURNS
            for l in range(DEPTH):
                qkv(l, DVE_FIRST + QKV_NEXT if l else H_EARLY + FIRST_STEPS)
                dve.wait_ge(sink_in, 16 * (l + 1))
                run(V_.tensor_scalar(nsink[:, :], sink[:, :], -1.0, None, ALU.mult))
                if l == 0:
                    ada_hook(QKV_TURNS - 1)
                for s in streams(l):
                    step = attention(l, s, step)
                n_gates = 6 * first_tile(l)

                def low(i):
                    src, _, lo, hi_read, _ = splits[l][i]
                    dve.wait_ge(split_high, split_base(l) + i + 1)
                    V_.tensor_tensor(lo, src, hi_read, ALU.subtract).then_inc(split_low, 1)

                for i in range(EARLY_SPLITS):
                    low(i)
                for (before, after), (n, br) in zip(split_order(l), [(n, br) for n in (0, 1) for br in range(3)]):
                    for i in before:
                        low(i)
                    for t in tiles(l):
                        b = filled(dve, ("BR", l, n, br, t))
                        drained(dve, ("G", l, n, br, t))
                        i = n_gates
                        n_gates += 1
                        dst = merged[:, t, 512 * n:512 * n + 512]
                        V_.tensor_tensor(dst if br == 0 else gtmp, sg[:, i % 4, :], psum[:, b, :], ALU.mult) \
                            .then_inc(gate_used, 1)
                        mark(bank_drained[b])
                        if br:
                            dve.wait_ge(gate_used, i + 1)
                            run(V_.tensor_tensor(dst, dst, gtmp, ALU.add))
                            if br == 2 and n == 1:
                                mark(merged_ready)
                    for i in after:
                        low(i)
                route(l)
                experts(l)


_INS = ["x", "c", "ctx", "c_ctx", "w_ada", "b_ada", "w_in", "a_sink", "b_q_norm", "b_kv_norm", "b_w_uq", "b_w_ukv",
        "c_q_norm", "c_k_norm", "w_branch", "w_out", "ln1_g", "ln1_b", "w_router", "w_gate", "w_up", "w_down",
        "ln2_g", "ln2_b"]


def tables():
    import numpy as np
    grid_w, window = 64, 128
    t = np.zeros((P, C_ALL), np.float32)
    t[:, C_ID:C_ID + P] = np.eye(P)
    for q in (0, 1):
        pos = q * P + np.arange(P)
        far = np.abs(pos[:, None] - np.arange(256)[None, :]) > window
        t[:, C_MASK + 256 * q:C_MASK + 256 * q + 256] = np.where(far, -1e30, 0.0)
        at = C_ROPE + 192 * q
        for half in (16, 8):
            freqs = (np.float32(10000.0) ** (-np.arange(half, dtype=np.float32) / half)).astype(np.float32)
            for axis, p in enumerate((pos // grid_w, pos % grid_w)):
                ang = p.astype(np.float32)[:, None] * freqs
                a = at + 2 * half * axis
                t[:, a:a + 2 * half] = np.concatenate([np.cos(ang), np.cos(ang)], 1)
                t[:, a + 4 * half:a + 6 * half] = np.concatenate([-np.sin(ang), np.sin(ang)], 1)
            at += 8 * half
    t[:, C_IOTA:C_IOTA + CAP] = 1 + np.arange(CAP)
    return t


def kernel(**inputs):
    import numpy as np
    import concourse.bacc as bacc
    from concourse.bass_utils import run_bass_kernel_spmd

    nc = bacc.Bacc("TRN2", target_bir_lowering=False, num_devices=1)
    arrays, args = {}, []
    for name in _INS:
        a = np.ascontiguousarray(inputs[name])
        arrays[f"in_{name}"] = a
        args.append(nc.dram_tensor(f"in_{name}", a.shape, F32, kind="ExternalInput").ap())
    arrays["in_tables"] = tables()
    args.append(nc.dram_tensor("in_tables", (P, C_ALL), F32, kind="ExternalInput").ap())
    out = nc.dram_tensor("out", (1, 256, D), F32, kind="ExternalOutput").ap()
    trunk(nc, *args, out)
    r = run_bass_kernel_spmd(nc, [arrays], core_ids=[0])
    return r.results[0]["out"]
```
